# Optimizing a Trainium2 kernel written in Bass

```python
import math
import jax
import jax.numpy as jnp
from jax import lax
import numpy as np

D_MODEL = 1024
BATCH = 1
SEQ = 256
DEPTH = 2

CTX_LEN = 256
GRID_W = 64
N_EVEN = (DEPTH + 1) // 2
N_ODD = DEPTH // 2
EPS = 1e-6
CONV_W = 3

SSD_HEADS = 8
SSD_HEAD_DIM = 64
SSD_INNER = SSD_HEADS * SSD_HEAD_DIM
SSD_GROUPS = 2
SSD_STATE = 64
SSD_CHUNK = 128
SSD_CONV_DIM = SSD_INNER + 2 * SSD_GROUPS * SSD_STATE

ATT_Q_HEADS = 8
ATT_KV_HEADS = 2
ATT_HEAD_DIM = 64
ATT_BLOCK = 128
WINDOW = 128
ROPE_THETA = 10000.0

ML_HEADS = 8
ML_QK_DIM = 64
ML_V_DIM = 128
ML_CHUNK = 128
ML_INNER = ML_HEADS * ML_V_DIM
ML_QKV = 2 * ML_HEADS * ML_QK_DIM + ML_INNER

N_EXPERTS = 16
N_GROUPS = 4
TOPK_GROUP = 1
TOP_K = 2
D_EXPERT = 512

EVEN_SIZES = (SSD_INNER, SSD_CONV_DIM, 2 * SSD_HEADS, ATT_Q_HEADS * ATT_HEAD_DIM, ATT_KV_HEADS * ATT_HEAD_DIM, ATT_KV_HEADS * ATT_HEAD_DIM)
EVEN_IN = sum(EVEN_SIZES)
EVEN_MIX = SSD_INNER + ATT_Q_HEADS * ATT_HEAD_DIM
ODD_SIZES = (ML_QKV, ML_INNER, 2 * ML_HEADS, 2 * ML_HEADS)
ODD_IN = sum(ODD_SIZES)

kernel_name = 'hybrid_ssd_swa_mlstm_moe_prefix_ctx'

def cuts(sizes):
    out, acc = [], 0
    for s in sizes[:-1]:
        acc += s
        out.append(acc)
    return out

def rmsnorm(x, g):
    xf = x.astype(jnp.float32)
    y = xf * lax.rsqrt(jnp.mean(xf * xf, axis=-1, keepdims=True) + EPS)
    return y.astype(x.dtype) * g

def adaln(cvec, w_mod, b_mod):
    m = (jax.nn.silu(cvec) @ w_mod + b_mod)[..., None, :]
    return jnp.split(m, 6, axis=-1)

def rev(t):
    return jnp.flip(t, axis=1)

def ident(t):
    return t

def dwconv_centred(x, w, b):
    L = x.shape[1]
    pad = CONV_W // 2
    xp = jnp.pad(x, ((0, 0), (pad, pad), (0, 0)))
    return sum(xp[:, j:j + L] * w[j] for j in range(CONV_W)) + b

def rope_1d(x, pos):
    n = x.shape[-1] // 2
    inv = ROPE_THETA ** (-jnp.arange(n, dtype=jnp.float32) / n)
    ang = pos.astype(jnp.float32)[:, None] * inv
    cos = jnp.cos(ang)[None, :, None, :]
    sin = jnp.sin(ang)[None, :, None, :]
    x1 = x[..., :n].astype(jnp.float32)
    x2 = x[..., n:].astype(jnp.float32)
    return jnp.concatenate([x1 * cos - x2 * sin, x1 * sin + x2 * cos], axis=-1)

def axial_rope(x, row, col):
    half = x.shape[-1] // 2
    return jnp.concatenate([rope_1d(x[..., :half], row), rope_1d(x[..., half:], col)], axis=-1).astype(x.dtype)

def segsum(a):
    T = a.shape[-1]
    strict = jnp.tril(jnp.ones((T, T), dtype=bool), -1)
    incl = jnp.tril(jnp.ones((T, T), dtype=bool))
    cs = jnp.cumsum(jnp.where(strict, a[..., :, None], 0.0), axis=-2)
    return jnp.where(incl, cs, -jnp.inf)

def ssd_scan(x, dt, A, Bm, Cm, h0):
    Bt, L, H, P = x.shape
    G, N = Bm.shape[2], Bm.shape[3]
    R = H // G
    T = SSD_CHUNK
    nc = L // T
    xc = x.reshape(Bt, nc, T, G, R, P)
    dtc = dt.reshape(Bt, nc, T, G, R)
    Bc = Bm.reshape(Bt, nc, T, G, N)
    Cc = Cm.reshape(Bt, nc, T, G, N)
    a = jnp.moveaxis(dtc * A.reshape(G, R), 2, -1)
    a_cs = jnp.cumsum(a, axis=-1)
    xdt = xc * dtc[..., None]
    Lm = jnp.exp(segsum(a))
    cb = jnp.einsum('bctgn,bcsgn->bcgts', Cc, Bc)
    y_diag = jnp.einsum('bcgts,bcgrts,bcsgrp->bctgrp', cb, Lm, xdt)
    decay_s = jnp.exp(a_cs[..., -1:] - a_cs)
    states = jnp.einsum('bcsgn,bcgrs,bcsgrp->bcgrpn', Bc, decay_s, xdt)
    states = jnp.concatenate([h0.reshape(Bt, 1, G, R, P, N).astype(states.dtype), states], axis=1)
    chunk_tot = jnp.pad(a_cs[..., -1], ((0, 0), (1, 0), (0, 0), (0, 0)))
    decay_chunk = jnp.exp(segsum(jnp.moveaxis(chunk_tot, 1, -1)))
    new_states = jnp.einsum('bgrzc,bcgrpn->bzgrpn', decay_chunk, states)
    states_in, final = new_states[:, :-1], new_states[:, -1]
    y_off = jnp.einsum('bctgn,bcgrpn,bcgrt->bctgrp', Cc, states_in, jnp.exp(a_cs))
    y = (y_diag + y_off).reshape(Bt, L, H, P)
    return y, final.reshape(Bt, H, P, N)

def mlstm_scan(q, k, v, ig, lf, state0):
    Bt, L, H, Dk = q.shape
    Dv = v.shape[-1]
    T = ML_CHUNK
    nc = L // T
    qc = q.reshape(Bt, nc, T, H, Dk)
    kc = k.reshape(Bt, nc, T, H, Dk)
    vc = v.reshape(Bt, nc, T, H, Dv)
    igc = jnp.moveaxis(ig.reshape(Bt, nc, T, H), 2, -1)
    b = jnp.cumsum(jnp.moveaxis(lf.reshape(Bt, nc, T, H), 2, -1), axis=-1)
    b_last = b[..., -1]
    w_end = b_last[..., None] - b + igc
    a_c = jnp.max(w_end, axis=-1)
    e_end = jnp.exp(w_end - a_c[..., None])
    S_c = jnp.einsum('bchs,bcshk,bcshv->bchkv', e_end, kc, vc)
    n_c = jnp.einsum('bchs,bcshk->bchk', e_end, kc)

    def step(carry, inp):
        Cs, ns, m = carry
        bl, a, Sc, nn_c = inp
        m_new = jnp.maximum(bl + m, a)
        sp = jnp.exp(bl + m - m_new)
        sc = jnp.exp(a - m_new)
        Cn = sp[..., None, None] * Cs + sc[..., None, None] * Sc
        nn = sp[..., None] * ns + sc[..., None] * nn_c
        return (Cn, nn, m_new), (Cs, ns, m)

    xs = (jnp.moveaxis(b_last, 1, 0), jnp.moveaxis(a_c, 1, 0), jnp.moveaxis(S_c, 1, 0), jnp.moveaxis(n_c, 1, 0))
    final, (C_in, n_in, m_in) = lax.scan(step, state0, xs)
    C_in = jnp.moveaxis(C_in, 0, 1)
    n_in = jnp.moveaxis(n_in, 0, 1)
    m_in = jnp.moveaxis(m_in, 0, 1)
    causal = jnp.tril(jnp.ones((T, T), dtype=bool))
    Dlog = jnp.where(causal, b[..., :, None] - b[..., None, :] + igc[..., None, :], -jnp.inf)
    g = b + m_in[..., None]
    m_star = jnp.maximum(g, jnp.max(Dlog, axis=-1))
    W = jnp.exp(Dlog - m_star[..., None]) * jnp.einsum('bcthk,bcshk->bchts', qc, kc)
    e_inter = jnp.exp(g - m_star)
    num = jnp.einsum('bchts,bcshv->bcthv', W, vc) + jnp.einsum('bcthk,bchkv,bcht->bcthv', qc, C_in, e_inter)
    den = W.sum(-1) + jnp.einsum('bcthk,bchk->bcht', qc, n_in) * e_inter
    denom = jnp.maximum(jnp.abs(den), jnp.exp(-m_star))
    h = num / jnp.swapaxes(denom, 2, 3)[..., None]
    return h.reshape(Bt, L, H, Dv), final

def window_attention(q, k, v, k_ctx, v_ctx, sink):
    Bt, S = q.shape[:2]
    nb = S // ATT_BLOCK
    G, R, Dh = ATT_KV_HEADS, ATT_Q_HEADS // ATT_KV_HEADS, ATT_HEAD_DIM
    scale = Dh ** -0.5
    qb = q.reshape(Bt, nb, ATT_BLOCK, G, R, Dh)

    def band(t):
        tp = jnp.pad(t, ((0, 0), (ATT_BLOCK, ATT_BLOCK), (0, 0), (0, 0))).reshape(Bt, nb + 2, ATT_BLOCK, G, Dh)
        return jnp.concatenate([tp[:, :-2], tp[:, 1:-1], tp[:, 2:]], axis=2)

    kb, vb = band(k), band(v)
    s_loc = jnp.einsum('bnqgrd,bnkgd->bngrqk', qb, kb, preferred_element_type=jnp.float32) * scale
    qpos = jnp.arange(nb)[:, None] * ATT_BLOCK + jnp.arange(ATT_BLOCK)[None]
    kpos = jnp.arange(nb)[:, None] * ATT_BLOCK - ATT_BLOCK + jnp.arange(3 * ATT_BLOCK)[None]
    valid = (jnp.abs(qpos[:, :, None] - kpos[:, None, :]) <= WINDOW) & (kpos[:, None, :] >= 0) & (kpos[:, None, :] < S)
    s_loc = jnp.where(valid[None, :, None, None], s_loc, -jnp.inf)
    s_ctx = jnp.einsum('bnqgrd,bcgd->bngrqc', qb, k_ctx, preferred_element_type=jnp.float32) * scale
    s_sink = sink.astype(jnp.float32).reshape(1, 1, G, R, 1, 1)
    m = jnp.maximum(jnp.maximum(s_loc.max(-1, keepdims=True), s_ctx.max(-1, keepdims=True)), s_sink)
    p_loc = jnp.exp(s_loc - m)
    p_ctx = jnp.exp(s_ctx - m)
    denom = p_loc.sum(-1, keepdims=True) + p_ctx.sum(-1, keepdims=True) + jnp.exp(s_sink - m)
    o = (jnp.einsum('bngrqk,bnkgd->bnqgrd', p_loc / denom, vb.astype(jnp.float32))
         + jnp.einsum('bngrqc,bcgd->bnqgrd', p_ctx / denom, v_ctx.astype(jnp.float32)))
    return o.reshape(Bt, S, ATT_Q_HEADS * Dh).astype(q.dtype)

def context_attention(q, k, v, sink):
    Bt, C = q.shape[:2]
    G, R = ATT_KV_HEADS, ATT_Q_HEADS // ATT_KV_HEADS
    qg = q.reshape(Bt, C, G, R, ATT_HEAD_DIM)
    s = jnp.einsum('bqgrd,bkgd->bgrqk', qg, k, preferred_element_type=jnp.float32) * ATT_HEAD_DIM ** -0.5
    s_sink = jnp.broadcast_to(sink.astype(jnp.float32).reshape(1, G, R, 1, 1), (Bt, G, R, C, 1))
    p = jax.nn.softmax(jnp.concatenate([s, s_sink], axis=-1), axis=-1)[..., :C]
    o = jnp.einsum('bgrqk,bkgd->bqgrd', p, v.astype(jnp.float32))
    return o.reshape(Bt, C, ATT_Q_HEADS * ATT_HEAD_DIM).astype(q.dtype)

def even_mixer(h_lat, h_ctx, row, col, w_in, conv_w, conv_b, dt_bias, a_log, d_skip, ssd_norm,
               q_norm, k_norm, sink, w_out, with_ctx):
    Bt = h_lat.shape[0]
    A = -jnp.exp(a_log.astype(jnp.float32))

    def project(h):
        L = h.shape[1]
        z, xbc, dt_raw, q, k, v = jnp.split(h @ w_in, cuts(EVEN_SIZES), axis=-1)
        xbc = jax.nn.silu(dwconv_centred(xbc, conv_w, conv_b))
        xs, bm, cm = jnp.split(xbc, [SSD_INNER, SSD_INNER + SSD_GROUPS * SSD_STATE], axis=-1)
        dt = jax.nn.softplus(dt_raw.reshape(Bt, L, 2, SSD_HEADS).astype(jnp.float32) + dt_bias)
        q = rmsnorm(q.reshape(Bt, L, ATT_Q_HEADS, ATT_HEAD_DIM), q_norm)
        k = rmsnorm(k.reshape(Bt, L, ATT_KV_HEADS, ATT_HEAD_DIM), k_norm)
        v = v.reshape(Bt, L, ATT_KV_HEADS, ATT_HEAD_DIM)
        return (z, xs.reshape(Bt, L, SSD_HEADS, SSD_HEAD_DIM), bm.reshape(Bt, L, SSD_GROUPS, SSD_STATE),
                cm.reshape(Bt, L, SSD_GROUPS, SSD_STATE), dt, q, k, v)

    zl, xl, bl, cl, dtl, ql, kl, vl = project(h_lat)
    zc, xc, bc, cc, dtc, qc, kc, vc = project(h_ctx)
    h0 = jnp.zeros((Bt, SSD_HEADS, SSD_HEAD_DIM, SSD_STATE), jnp.float32)
    y_lat = d_skip[:, None] * xl
    y_ctx = d_skip[:, None] * xc
    for d in range(2):
        f = rev if d else ident
        yc, hc = ssd_scan(f(xc), f(dtc[:, :, d]), A[d], f(bc), f(cc), h0)
        yl, _ = ssd_scan(f(xl), f(dtl[:, :, d]), A[d], f(bl), f(cl), hc)
        y_lat = y_lat + f(yl)
        if with_ctx:
            y_ctx = y_ctx + f(yc)

    def ssd_out(y, z):
        y = y.reshape(Bt, y.shape[1], SSD_INNER).astype(z.dtype)
        return rmsnorm(y * jax.nn.silu(z), ssd_norm)

    ql = axial_rope(ql, row, col)
    kl = axial_rope(kl, row, col)
    out_lat = jnp.concatenate([ssd_out(y_lat, zl), window_attention(ql, kl, vl, kc, vc, sink)], axis=-1) @ w_out
    out_ctx = None
    if with_ctx:
        out_ctx = (jnp.concatenate([ssd_out(y_ctx, zc), context_attention(qc, kc, vc, sink)], axis=-1) @ w_out).astype(h_ctx.dtype)
    return out_lat.astype(h_lat.dtype), out_ctx

def odd_mixer(h_lat, h_ctx, w_in, conv_w, conv_b, igate_b, fgate_b, head_norm, w_out, with_ctx):
    Bt = h_lat.shape[0]

    def project(h):
        L = h.shape[1]
        qkv, o, ig, fg = jnp.split(h @ w_in, cuts(ODD_SIZES), axis=-1)
        qkv = jax.nn.silu(dwconv_centred(qkv, conv_w, conv_b))
        q, k, v = jnp.split(qkv, [ML_HEADS * ML_QK_DIM, 2 * ML_HEADS * ML_QK_DIM], axis=-1)
        q = q.reshape(Bt, L, ML_HEADS, ML_QK_DIM)
        k = k.reshape(Bt, L, ML_HEADS, ML_QK_DIM) * (ML_QK_DIM ** -0.5)
        v = v.reshape(Bt, L, ML_HEADS, ML_V_DIM)
        ig = ig.reshape(Bt, L, 2, ML_HEADS).astype(jnp.float32) + igate_b
        lf = jax.nn.log_sigmoid(fg.reshape(Bt, L, 2, ML_HEADS).astype(jnp.float32) + fgate_b)
        return q, k, v, o, ig, lf

    ql, kl, vl, ol, igl, lfl = project(h_lat)
    qc, kc, vc, oc, igc, lfc = project(h_ctx)
    zero = (jnp.zeros((Bt, ML_HEADS, ML_QK_DIM, ML_V_DIM), jnp.float32),
            jnp.zeros((Bt, ML_HEADS, ML_QK_DIM), jnp.float32),
            jnp.zeros((Bt, ML_HEADS), jnp.float32))
    h_l = 0.0
    h_c = 0.0
    for d in range(2):
        f = rev if d else ident
        yc, sc = mlstm_scan(f(qc), f(kc), f(vc), f(igc[:, :, d]), f(lfc[:, :, d]), zero)
        yl, _ = mlstm_scan(f(ql), f(kl), f(vl), f(igl[:, :, d]), f(lfl[:, :, d]), sc)
        h_l = h_l + f(yl)
        if with_ctx:
            h_c = h_c + f(yc)

    def out(hh, o):
        hh = rmsnorm(hh, head_norm.reshape(ML_HEADS, ML_V_DIM)).reshape(Bt, hh.shape[1], ML_INNER).astype(o.dtype)
        return (hh * jax.nn.sigmoid(o)) @ w_out

    out_lat = out(h_l, ol).astype(h_lat.dtype)
    out_ctx = out(h_c, oc).astype(h_ctx.dtype) if with_ctx else None
    return out_lat, out_ctx

def moe(h, router_w, router_b, w1, w3, w2):
    scores = jax.nn.sigmoid((h @ router_w).astype(jnp.float32))
    biased = scores + router_b.astype(jnp.float32)
    per = N_EXPERTS // N_GROUPS
    grp = biased.reshape(biased.shape[:-1] + (N_GROUPS, per))
    grp_score = lax.top_k(grp, 2)[0].sum(-1)
    _, gidx = lax.top_k(grp_score, TOPK_GROUP)
    gsel = jax.nn.one_hot(gidx, N_GROUPS, dtype=jnp.float32).sum(-2) > 0
    esel = jnp.repeat(gsel, per, axis=-1)
    _, eidx = lax.top_k(jnp.where(esel, biased, -jnp.inf), TOP_K)
    w = jnp.take_along_axis(scores, eidx, axis=-1)
    w = w / w.sum(-1, keepdims=True)
    gates = (jax.nn.one_hot(eidx, N_EXPERTS, dtype=jnp.float32) * w[..., None]).sum(-2)
    out = jnp.zeros(h.shape, jnp.float32)
    for e in range(N_EXPERTS):
        a = jax.nn.silu(h @ w1[e]) * (h @ w3[e])
        out = out + gates[..., e:e + 1] * (a @ w2[e])
    return out.astype(h.dtype)

def setup_inputs(seed: int = 0) -> dict:
    key = jax.random.key(seed)
    keys = jax.random.split(key, 48)
    ki = iter(range(48))
    D = D_MODEL

    def nrm(shape, s):
        return jax.random.normal(keys[next(ki)], shape, jnp.float32) * s

    def unif(shape, lo, hi):
        return jax.random.uniform(keys[next(ki)], shape, jnp.float32, minval=lo, maxval=hi)

    dt = jnp.exp(unif((N_EVEN, 2, SSD_HEADS), math.log(1e-3), math.log(1e-1)))
    return {
        'x': nrm((BATCH, SEQ, D), 1.0),
        'c': nrm((BATCH, D), 1.0),
        'ctx': nrm((BATCH, CTX_LEN, D), 1.0),
        'c_ctx': nrm((D,), 1.0),
        'router_w': nrm((D, N_EXPERTS), D ** -0.5),
        'router_b': nrm((N_EXPERTS,), 0.01),
        'norm_mix': 1.0 + nrm((DEPTH, D), 0.02),
        'norm_ffn': 1.0 + nrm((DEPTH, D), 0.02),
        'w_mod': nrm((DEPTH, D, 6 * D), 0.5 * D ** -0.5),
        'b_mod': nrm((DEPTH, 6 * D), 0.02),
        'ev_w_in': nrm((N_EVEN, D, EVEN_IN), D ** -0.5),
        'ev_conv_w': nrm((N_EVEN, CONV_W, SSD_CONV_DIM), CONV_W ** -0.5),
        'ev_conv_b': nrm((N_EVEN, SSD_CONV_DIM), 0.02),
        'ev_dt_bias': dt + jnp.log(-jnp.expm1(-dt)),
        'ev_a_log': jnp.log(unif((N_EVEN, 2, SSD_HEADS), 1.0, 16.0)),
        'ev_d_skip': 1.0 + nrm((N_EVEN, SSD_HEADS), 0.1),
        'ev_ssd_norm': 1.0 + nrm((N_EVEN, SSD_INNER), 0.02),
        'ev_q_norm': 1.0 + nrm((N_EVEN, ATT_HEAD_DIM), 0.02),
        'ev_k_norm': 1.0 + nrm((N_EVEN, ATT_HEAD_DIM), 0.02),
        'ev_sink': nrm((N_EVEN, ATT_Q_HEADS), 1.0),
        'ev_w_out': nrm((N_EVEN, EVEN_MIX, D), EVEN_MIX ** -0.5),
        'od_w_in': nrm((N_ODD, D, ODD_IN), D ** -0.5),
        'od_conv_w': nrm((N_ODD, CONV_W, ML_QKV), CONV_W ** -0.5),
        'od_conv_b': nrm((N_ODD, ML_QKV), 0.02),
        'od_igate_b': nrm((N_ODD, 2, ML_HEADS), 0.1),
        'od_fgate_b': jnp.linspace(3.0, 6.0, ML_HEADS, dtype=jnp.float32)[None, None, :] + nrm((N_ODD, 2, ML_HEADS), 0.1),
        'od_head_norm': 1.0 + nrm((N_ODD, ML_INNER), 0.02),
        'od_w_out': nrm((N_ODD, ML_INNER, D), ML_INNER ** -0.5),
        'moe_w1': nrm((DEPTH, N_EXPERTS, D, D_EXPERT), D ** -0.5),
        'moe_w3': nrm((DEPTH, N_EXPERTS, D, D_EXPERT), D ** -0.5),
        'moe_w2': nrm((DEPTH, N_EXPERTS, D_EXPERT, D), D_EXPERT ** -0.5),
    }

def reference(x, c, ctx, c_ctx, router_w, router_b, norm_mix, norm_ffn, w_mod, b_mod,
              ev_w_in, ev_conv_w, ev_conv_b, ev_dt_bias, ev_a_log, ev_d_skip, ev_ssd_norm,
              ev_q_norm, ev_k_norm, ev_sink, ev_w_out,
              od_w_in, od_conv_w, od_conv_b, od_igate_b, od_fgate_b, od_head_norm, od_w_out,
              moe_w1, moe_w3, moe_w2):
    S = x.shape[1]
    ROWS = S // GRID_W
    row = jnp.repeat(jnp.arange(ROWS, dtype=jnp.int32), GRID_W)
    col = jnp.tile(jnp.arange(GRID_W, dtype=jnp.int32), ROWS)
    x_lat, x_ctx = x, ctx
    for l in range(DEPTH):
        with_ctx = l < DEPTH - 1
        sh_m, sc_m, g_m, sh_f, sc_f, g_f = adaln(c, w_mod[l], b_mod[l])
        csh_m, csc_m, cg_m, csh_f, csc_f, cg_f = adaln(c_ctx, w_mod[l], b_mod[l])
        h_lat = rmsnorm(x_lat, norm_mix[l]) * (1.0 + sc_m) + sh_m
        h_ctx = rmsnorm(x_ctx, norm_mix[l]) * (1.0 + csc_m) + csh_m
        i = l // 2
        if l % 2 == 0:
            m_lat, m_ctx = even_mixer(h_lat, h_ctx, row, col, ev_w_in[i], ev_conv_w[i], ev_conv_b[i], ev_dt_bias[i],
                                      ev_a_log[i], ev_d_skip[i], ev_ssd_norm[i], ev_q_norm[i], ev_k_norm[i],
                                      ev_sink[i], ev_w_out[i], with_ctx)
        else:
            m_lat, m_ctx = odd_mixer(h_lat, h_ctx, od_w_in[i], od_conv_w[i], od_conv_b[i], od_igate_b[i],
                                     od_fgate_b[i], od_head_norm[i], od_w_out[i], with_ctx)
        x_lat = x_lat + g_m * m_lat
        h_lat = rmsnorm(x_lat, norm_ffn[l]) * (1.0 + sc_f) + sh_f
        x_lat = x_lat + g_f * moe(h_lat, router_w, router_b, moe_w1[l], moe_w3[l], moe_w2[l])
        if with_ctx:
            x_ctx = x_ctx + cg_m * m_ctx
            h_ctx = rmsnorm(x_ctx, norm_ffn[l]) * (1.0 + csc_f) + csh_f
            x_ctx = x_ctx + cg_f * moe(h_ctx, router_w, router_b, moe_w1[l], moe_w3[l], moe_w2[l])
    return x_lat


_drawn_inputs = setup_inputs


def setup_inputs(seed=0):
    import zlib

    import numpy as np

    out = dict(_drawn_inputs(seed))
    spreads = {}
    factors = {'ev_conv_b': 3.179,
     'ev_ssd_norm': 26.266,
     'ev_q_norm': 32.45,
     'ev_k_norm': 17.068,
     'ev_sink': 8.0,
     'od_conv_b': 5.161,
     'od_igate_b': 8.0,
     'od_head_norm': 86.696,
     'router_b': 2.859,
     'norm_ffn': 3.608}
    for name, (base, spread) in spreads.items():
        noise = np.random.default_rng([zlib.crc32(name.encode()), seed]).standard_normal(out[name].shape)
        drawn = base * np.exp(spread * noise) if base else spread * noise
        out[name] = jnp.asarray(drawn.astype(out[name].dtype))
    for name, factor in factors.items():
        out[name] = (out[name] * factor).astype(out[name].dtype)
    return out
```

```python
import concourse.bass as bass
from concourse import mybir
from concourse.alu_op_type import AluOpType as ALU
import numpy as np

F32 = mybir.dt.float32
BF16 = mybir.dt.bfloat16
U32 = mybir.dt.uint32
ACT = mybir.ActivationFunctionType
AX = mybir.AxisListType

P = 128
D = 1024
KD = D // P
NT = 4
TOK = NT * P
STREAM = 256
H = 8
DIR1 = 32
ROWS = DIR1 + H
EPS = 1e-6
NEG = -1e30
SSD_IN = 512
XBC = 768
EV_DT, EV_Q, EV_K = 1280, 1296, 1808
QKV = 768
OD_CONV = 2048
OD_GATES = 3072
DV = 128
VA = DV + 1
E = 16
FE = 512
KF = FE // P
RMAX = TOK // P
NCOL = RMAX * E
NSLOT = 4
GROUP = 4
MODC = 12


def lat(t):
    return t >= 2


def tile_of(step, d):
    return step if d == 0 else (1, 0, 3, 2)[step]


def hybrid_program(nc, x, c, ctx, c_ctx, router_w, router_b, norm_mix, norm_ffn, w_mod, b_mod,
                   ev_w_in, ev_conv_w, ev_conv_b, ev_dt_bias, ev_a_log, ev_d_skip, ev_ssd_norm,
                   ev_q_norm, ev_k_norm, ev_sink, ev_w_out,
                   od_w_in, od_conv_w, od_conv_b, od_igate_b, od_fgate_b, od_head_norm, od_w_out,
                   moe_w1, moe_w3, moe_w2, const_f, const_b, out):
    sems = {}

    def S(name):
        if name not in sems:
            sems[name] = nc.alloc_semaphore(name)
        return sems[name]

    def counter():
        seen = {}

        def more(name, k=1):
            seen[name] = seen.get(name, 0) + k
            return S(name), seen[name]
        return more

    def sb(name, shape, dt=F32):
        return nc.alloc_sbuf_tensor(name, shape, dt)

    ring = sb("ring", [P, NSLOT, 4096])
    xres = sb("xres", [P, NT, D])
    cf = sb("cf", [P, const_f.shape[1]])
    cb = sb("cb", [P, const_b.shape[1]], BF16)
    colsa = sb("colsa", [P, 72])
    colsb = sb("colsb", [P, 64])
    spad = sb("spad", [P, KD, 32])
    bcol = sb("bcol", [P, 4, 2 * MODC])
    modrow = sb("modrow", [P, 512])
    mcol = sb("mcol", [P, 2, 48, 2])
    acol = sb("acol", [P, 2, 2, 2, KD])
    rw = sb("rw", [P, KD, E])
    rbias = sb("rbias", [P, E])
    rowpar = sb("rowpar", [ROWS, 8])
    brd = sb("brd", [P, 8 + 8])
    ssdn = sb("ssdn", [P, SSD_IN])
    qkw = sb("qkw", [P, 10, 64])
    hnorm = sb("hnorm", [P, D])
    stat = sb("stat", [P, 64])
    stat2 = sb("stat2", [P, 3, 64])
    zrow = sb("zrow", [P, NCOL], U32)
    idx = sb("idx", [P, NCOL], U32)
    idxg = sb("idxg", [P, GROUP], U32)
    flag = sb("flag", [1, 2], U32)
    rt = sb("rt", [P, 816])
    rw32 = sb("rw32", [P, KD, 32])
    tok32 = sb("tok32", [P, NT], U32)
    maskb = sb("maskb", [P, NT, E], BF16)
    gatew = sb("gatew", [P, NT, 2])
    rowy = sb("rowy", [P, NT, 2], U32)
    rowi = sb("rowi", [P, NT, 2], U32)

    ident = cf[:, 0:P]
    eiota = cf[:, 128:144]
    edesc = cf[:, 144:160]
    tokid = cf[:, 160:164]
    ones = cf[:, 164:164 + P]
    cosb = cf[:, 292:292 + 128].rearrange("p (t n) -> p t n", t=2)
    sinb = cf[:, 420:420 + 128].rearrange("p (t n) -> p t n", t=2)
    identb = cb[:, 0:P]
    onesb = cb[:, P:2 * P]
    upper = cb[:, 2 * P:3 * P]
    decmask = [cb[:, 384 + 512 * d:384 + 512 * (d + 1)] for d in range(2)]
    attmask = [cb[:, 1408 + 512 * i:1408 + 512 * (i + 1)] for i in range(2)]

    room = (nc.sbuf_bytes_remaining() if callable(nc.sbuf_bytes_remaining) else nc.sbuf_bytes_remaining) // 4
    AREA = room - 64
    arena = sb("arena", [P, AREA])

    def view(at, shape, dt=F32):
        n = int(np.prod(shape))
        assert at + n <= AREA, (at + n, AREA)
        v = arena[:, at:at + n]
        names = "abcd"[:len(shape)]
        if len(shape) == 1:
            return v
        return v.rearrange(f"p ({' '.join(names)}) -> p {' '.join(names)}", **dict(zip(names, shape)))

    hT = view(0, [KD, TOK])
    htok = view(4096, [NT, D])
    raw = view(4096, [6, 2, STREAM + 2])
    xbcT = view(8192, [6, TOK])
    zs = view(11264, [NT, SSD_IN])
    qkv = view(13312, [NT, QKV])
    xs = view(16384, [NT, SSD_IN])
    btok = view(18432, [NT, P])
    cbT = view(18944, [2, NT, P])
    sq = view(19968, [4, TOK])
    tq = view(22016, [4, TOK])
    cq = view(24064, [NT, 4, ROWS])
    catT = hT
    grow = view(18000, [2, D])
    ysum = view(4096, [NT, SSD_IN])
    xdt = view(6144, [512])
    xdd = view(6656, [512])
    wts = [view(19968 + 512 * i, [4, P]) for i in range(2)]
    sbd = [view(7168 + 512 * d, [512]) for d in range(2)]
    gtmp = view(4096 + 3200, [TOK])
    yoff = view(20992, [512])
    dg = view(21504, [4, ROWS])
    eb = view(21504 + 160, [4, ROWS])
    qT = view(4096, [4, TOK])
    kT2 = view(6144, [2, TOK])
    kdup = view(7168, [NT, 4, 64])
    ptb = [view(16384 + 2048 * i, [4, 2, 2, P]) for i in range(2)]
    pbuf = [view(20480 + 512 * i, [TOK]) for i in range(3)]
    att = view(23296, [4, NT * H])

    hdram = [nc.dram_tensor(f"hdram{l}", [n, D], F32, kind="Internal").ap() for l, n in enumerate((TOK, STREAM))]
    ydram = [nc.dram_tensor(f"ydram{l}", [n * E, D], F32, kind="Internal").ap() for l, n in enumerate((TOK, STREAM))]
    table = [nc.dram_tensor(f"table{l}", [NCOL * P, 1], U32, kind="Internal").ap() for l in range(2)]

    psum = nc.alloc_psum_tensor("psum", [P, 8, 512], F32)

    def bank(b, n=512):
        return psum[:, b, 0:n]

    def cols(w, a, b):
        return w[:, a:b].rearrange("(k p) n -> p k n", p=P), (b - a) * KD

    def mod_src(l, ch):
        return cols(w_mod[l], 512 * ch, 512 * ch + 512)

    ev = ev_w_in[0]
    od = od_w_in[0]
    MODS = [(l, ch) for l in range(2) for ch in range(MODC)]
    FIRST = 4
    before0 = [mod_src(*m) for m in MODS[:FIRST]]
    before0 += [cols(ev, 512, 1024), cols(ev, 1024, EV_Q), cols(ev, EV_K, 2064), cols(ev, EV_Q, EV_K), cols(ev, 0, 512)]
    before0 += [mod_src(*m) for m in MODS[FIRST:]]
    before0 += [cols(ev_w_out[0], 512 * i, 512 * i + 512) for i in range(2)]
    before1 = [cols(od, OD_GATES, OD_GATES + 32)] + [cols(od, 512 * i, 512 * i + 512) for i in range(6)]
    before1 += [cols(od_w_out[0], 512 * i, 512 * i + 512) for i in range(2)]
    MOE_BASE = [len(before0), len(before0) + 3 * E + len(before1)]

    def slot(i, n, k=KD):
        return ring[:, i % NSLOT, 0:k * n].rearrange("p (k n) -> p k n", k=k)

    def expert_src(l, kind, e):
        w = {"w1": moe_w1, "w3": moe_w3, "w2": moe_w2}[kind][l]
        we = w[e] if isinstance(e, int) else w[bass.ds(e, 1)].rearrange("a d n -> (a d) n")
        return we.rearrange("(k p) n -> p k n", p=P)

    def position(l, kind, e, looped=False):
        if kind == "w2":
            return MOE_BASE[l] + (3 * E - 1 if e == E - 1 else 3 * e + 4)
        if e == 0 and not looped:
            return MOE_BASE[l] + (kind == "w3")
        return MOE_BASE[l] + 3 * e - 1 + (kind == "w3")

    IN_EVEN = [("xbc", b, "act") for b in range(6)] + [("dt", 0, "dve")] \
        + [(kind, t, "act") for kind in ("kv", "q", "z") for t in range(NT)]


    pe_more, act_more, dve_more, pool_more, sp_more = (counter() for _ in range(5))
    pe, act, dve, pool, sp = nc.tensor, nc.scalar, nc.vector, nc.gpsimd, nc.sync

    def dve_step(ins):
        ins.then_inc(S("dve_step"), 1)
        dve.wait_ge(*dve_more("dve_step"))

    def act_step(ins):
        ins.then_inc(S("act_step"), 1)
        act.wait_ge(*act_more("act_step"))

    def pool_step(ins):
        ins.then_inc(S("pool_step"), 1)
        pool.wait_ge(*pool_more("pool_step"))

    def weights_here(i):
        pe.wait_ge(S(f"w_ready{i % NSLOT}"), 16 * (i // NSLOT + 1))

    r1, r2, r3, rc = (view(P * j, [P]) for j in range(4))
    brow = view(4 * P, [512])
    FIRST_PARAMS = [
        (cf[:, :], const_f),
        (rc[0:8, :], c.rearrange("a (b n) -> (a b) n", n=P)),
        (rc[8:16, :], c_ctx.rearrange("(b n) -> b n", n=P)),
    ]
    PARAMS = [
        (cb[:, :], const_b),
        (r3[0:18, :], ev_conv_w[0].rearrange("t (b n) -> (t b) n", n=P)),
        (r3[18:24, :], ev_conv_b[0].rearrange("(b n) -> b n", n=P)),
        (r2[0:48, :], od_conv_w[0].rearrange("t (b n) -> (t b) n", n=P)),
        (r2[48:64, :], od_conv_b[0].rearrange("(b n) -> b n", n=P)),
    ]
    PARAMS += [
        (r1[0:16, :], norm_mix.rearrange("l (b n) -> (l b) n", n=P)),
        (r1[16:32, :], norm_ffn.rearrange("l (b n) -> (l b) n", n=P)),
        (brow[0:2 * MODC, :], b_mod.rearrange("l (c n) -> (l c) n", n=512)),
        (rw[:, :, :], router_w.rearrange("(k p) e -> p k e", p=P)),
        (rbias[:, :], router_b.partition_broadcast(P)),
        (brd[:, 0:8], ev_d_skip[0].partition_broadcast(P)),
        (brd[:, 8:16], ev_sink[0].partition_broadcast(P)),
        (ssdn[:, :], ev_ssd_norm[0].partition_broadcast(P)),
        (qkw[:, 0, :], ev_q_norm[0].partition_broadcast(P)),
        (qkw[:, 8, :], ev_k_norm[0].partition_broadcast(P)),
        (hnorm[:, :], od_head_norm[0].partition_broadcast(P)),
        (xres[:, 0:2, :], ctx[0].rearrange("(t p) n -> p t n", p=P)),
        (xres[:, 2:4, :], x[0].rearrange("(t p) n -> p t n", p=P)),
    ]
    for d in range(2):
        for j, w in enumerate((ev_dt_bias, ev_a_log, od_igate_b, od_fgate_b)):
            PARAMS.append((rowpar[DIR1 * d:DIR1 * d + H, j:j + 1], w[0, d].unsqueeze(1)))
    PARAMS_IN = 16 * len(PARAMS)

    def act_setup():
        act.wait_ge(S("zeroed"), 1)
        for dst, src in PARAMS:
            act.dma_start(dst, src).then_inc(S("params"), 16)
        act.wait_ge(*act_more("cols_ready"))
        act.activation(stat2[:, 0, 0:16], colsa[:, 32:48], ACT.Exp, scale=-1.0).then_inc(S("c_exp"), 1)

    def act_setup_rest():
        act.wait_ge(S("params"), PARAMS_IN)
        act.activation(rowpar[:, 4:5], rowpar[:, 1:2], ACT.Exp).then_inc(S("c_exp"), 1)

    def pe_setup():
        pe.wait_ge(S("first_params"), 16 * len(FIRST_PARAMS))
        pe.transpose(psum[:, 0, 0:16], rc[0:16, :], ident[0:16, 0:16]).then_inc(S("cols_full"), 1)

    def pe_setup_rest():
        pe.wait_ge(S("params"), PARAMS_IN)
        pe.wait_ge(*pe_more("cols_ready"))
        pe.transpose(psum[:, 0, 0:32], r1[0:32, :], ident[0:32, 0:32])
        pe.transpose(psum[:, 0, 32:56], r3[0:24, :], ident[0:24, 0:24])
        pe.transpose(psum[:, 1, 0:64], r2[0:64, :], ident[0:64, 0:64])
        for b in range(4):
            mm = pe.transpose(psum[:, 2, 2 * MODC * b:2 * MODC * (b + 1)], brow[0:2 * MODC, P * b:P * b + P],
                              ident[0:2 * MODC, 0:2 * MODC])
        mm.then_inc(S("cols_full"), 1)

    def dve_setup():
        dve_step(dve.memset(spad[:], 0.0))
        dve.memset(rowpar[:], 0.0).then_inc(S("zeroed"), 1)
        dve.wait_ge(*dve_more("cols_full"))
        dve.tensor_copy(colsa[:, 32:48], psum[:, 0, 0:16]).then_inc(S("cols_ready"), 1)
        dve.wait_ge(*dve_more("cols_ready"))
        dve.wait_ge(*dve_more("c_exp"))
        dve_step(dve.tensor_scalar(stat2[:, 0, 0:16], stat2[:, 0, 0:16], 1.0, None, ALU.add))
        dve_step(dve.reciprocal(stat2[:, 1, 0:16], stat2[:, 0, 0:16]))
        dve.tensor_tensor(spad[:, :, 0:2].rearrange("p k s -> p s k"), stat2[:, 1, 0:16].rearrange("p (s k) -> p s k", s=2),
                          colsa[:, 32:48].rearrange("p (s k) -> p s k", s=2), ALU.mult).then_inc(S("spad_ready"), 1)

    def dve_setup_rest():
        dve.wait_ge(*dve_more("cols_full"))
        dve_step(dve.tensor_copy(bcol[:], psum[:, 2, 0:8 * MODC].rearrange("p (b n) -> p b n", b=4)))
        dve_step(dve.tensor_copy(colsb[:], psum[:, 1, 0:64]))
        dve_step(dve.tensor_copy(colsa[:, 48:72], psum[:, 0, 32:56]))
        dve.tensor_copy(colsa[:, 0:32], psum[:, 0, 0:32]).then_inc(S("cols_ready"), 1)
        dve.wait_ge(*dve_more("cols_ready"))
        dve.wait_ge(*dve_more("c_exp"))
        dve_step(dve.tensor_scalar(rowpar[:, 4:5], rowpar[:, 4:5], -1.0, None, ALU.mult))
        dve_step(dve.tensor_scalar(qkw[:, 1:8, :], qkw[:, 0:1, :].broadcast_to([P, 7, 64]), 1.0, None, ALU.mult))
        dve_step(dve.tensor_scalar(qkw[:, 9, :], qkw[:, 8, :], 1.0, None, ALU.mult))

    def mod_pos(m):
        return m if m < FIRST else m + 5

    def pe_mod_rows(m):
        weights_here(mod_pos(m))
        w = slot(mod_pos(m), 512)
        for k in range(KD):
            j = 32 * (k % 4)
            mm = pe.matmul(psum[j:j + 32, 7, :], spad[:, k, :], w[:, k, :], start=k < 4, stop=k >= 4)
        mm.then_inc(S("mod_full"), 1)

    def pe_mod_cols(m):
        pe.wait_ge(*pe_more("modrow_ready"))
        if m > 0:
            pe.wait_ge(*pe_more("mcol_done"))
        for b in range(4):
            mm = pe.transpose(psum[:, 6, P * b:P * b + P], modrow[:, P * b:P * b + P], ident)
        mm.then_inc(S("modcol_full"), 1)

    def pe_mod(m):
        pe_mod_rows(m)
        pe_mod_cols(m)

    def act_mod(m):
        act.wait_ge(*act_more("mod_full"))
        if m > 0:
            act.wait_ge(*act_more("modcol_full"))
        act.activation(modrow[:], bank(7), ACT.Copy).then_inc(S("modrow_ready"), 1)

    def dve_mod(m):
        l, ch = MODS[m]
        dve.wait_ge(*dve_more("modcol_full"))
        dve.tensor_reduce(mcol[:, l, 4 * ch:4 * ch + 4, :],
                          bank(6).rearrange("p (b g r) -> p b r g", b=4, g=4)[:, :, 0:2, :], AX.X, ALU.add
                          ).then_inc(S("mcol_done"), 1)

    def dve_mod_bias(l, a, b):
        dve.wait_ge(S("mcol_done"), MODC * l + b)
        v = mcol[:, l, 4 * a:4 * b, :].rearrange("p (n b) s -> p b n s", b=4)
        v2 = bcol[:, :, MODC * l + a:MODC * l + b]
        for s_ in range(2):
            dve.tensor_tensor(v[:, :, :, s_], v[:, :, :, s_], v2, ALU.add).then_inc(S("mod_done"), 1)
        dve.wait_ge(*dve_more("mod_done", 2))

    ACOL_AFTER = {(0, 0): 2, (0, 1): 4, (1, 0): 6, (1, 1): 8}

    def dve_acol(l, which):
        blk = 32 if which else 8
        for s in range(2):
            dve.scalar_tensor_tensor(acol[:, l, which, s, :], mcol[:, l, blk:blk + KD, s], 1.0,
                                     colsa[:, 16 * which + 8 * l:16 * which + 8 * l + KD], ALU.add, ALU.mult
                                     ).then_inc(S("acol_ready"), 1)

    def dve_rstd(n, width):
        v, y, t = (stat2[:, j, 0:n] for j in range(3))
        dve.tensor_scalar(v, stat[:, 0:n], 1.0 / width, EPS, ALU.mult, ALU.add).then_inc(S("var_ready"), 1)
        dve.wait_ge(*dve_more("rstd_guess"))
        dve_step(dve.reciprocal(y, y))
        dve_step(dve.tensor_tensor(t, y, y, ALU.mult))
        dve_step(dve.tensor_tensor(t, t, v, ALU.mult))
        dve_step(dve.tensor_scalar(t, t, -0.5, 1.5, ALU.mult, ALU.add))
        dve_step(dve.tensor_tensor(y, y, t, ALU.mult))

    def act_rstd(n):
        v, y = stat2[:, 0, 0:n], stat2[:, 1, 0:n]
        act.wait_ge(*act_more("var_ready"))
        act.activation(y, v, ACT.Sqrt).then_inc(S("rstd_guess"), 1)

    def act_norm(l, which, tiles, ready, value):
        for n, t in enumerate(tiles):
            act.wait_ge(S(ready), value if ready == "params" else value - len(tiles) + n + 1)
            act.activation(htok[:, t, :], xres[:, t, :], ACT.Square, accum_out=stat[:, n:n + 1]
                           ).then_inc(S("sum_ready"), 1)
        act_rstd(len(tiles))
        act.wait_ge(S("acol_ready"), ACOL_AFTER[l, which])
        for k in range(0, KD, 2):
            act_evac_ht(l, which, tiles, k)
        act_more("ht_full", 1)

    def ht_halves(l, which, tiles, k):
        shift = 24 * which + k
        n0 = 0
        for s, ts in ((1, [t for t in tiles if not lat(t)]), (0, [t for t in tiles if lat(t)])):
            if ts:
                n = P * len(ts)
                yield (hT[:, k, P * ts[0]:P * ts[0] + n], psum[:, k % 4, n0:n0 + n],
                       acol[:, l, which, s, k:k + 1], mcol[:, l, shift, s:s + 1])
                n0 += n

    def act_evac_ht(l, which, tiles, k):
        act.wait_ge(*act_more("ht_full", 1 if k == 0 else 2))
        for dst, src, a, b in ht_halves(l, which, tiles, k):
            last = act.activation(dst, src, ACT.Identity, bias=b, scale=a)
        last.then_inc(S("ht_act"), 1)

    def dve_norm(l, which, tiles):
        dve.wait_ge(*dve_more("sum_ready", len(tiles)))
        dve_rstd(len(tiles), D)
        for n, t in enumerate(tiles):
            dve.tensor_scalar(htok[:, t, :], xres[:, t, :], stat2[:, 1, n:n + 1], None, ALU.mult
                              ).then_inc(S("xn_ready"), 1)
        dve.wait_ge(S("acol_ready"), ACOL_AFTER[l, which])
        for k in range(1, KD, 2):
            dve.wait_ge(*dve_more("ht_full", 2))
            for dst, src, a, b in ht_halves(l, which, tiles, k):
                last = dve.tensor_scalar(dst, src, a, b, ALU.mult, ALU.add)
            last.then_inc(S("ht_dve"), 1)

    def pe_norm(tiles):
        pe.wait_ge(*pe_more("xn_ready", len(tiles)))
        for k in range(KD):
            if k >= 4:
                pe.wait_ge(*pe_more("ht_act" if k % 2 == 0 else "ht_dve"))
            for n, t in enumerate(tiles):
                mm = pe.transpose(psum[:, k % 4, P * n:P * n + P], htok[:, t, P * k:P * k + P], ident)
            mm.then_inc(S("ht_full"), 1)
        pe.wait_ge(*pe_more("ht_act", 2))
        pe.wait_ge(*pe_more("ht_dve", 2))

    EV0 = FIRST

    def pe_in_even():
        done, at = [], None
        for i, (kind, b, who) in enumerate(IN_EVEN):
            if i >= 6:
                pe.wait_ge(*pe_more(f"in_{done[i - 6]}"))
            done.append(who)
            bk = i % 6
            pos = EV0 + {"xbc": b // 4, "dt": 1, "kv": 2, "q": 3, "z": 4}[kind]
            if pos != at:
                weights_here(pos)
                at = pos
            if kind == "xbc":
                w = slot(pos, 512 if b < 4 else 272)
                for k in range(KD):
                    mm = pe.matmul(bank(bk), w[:, k, P * (b % 4):P * (b % 4) + P], hT[:, k, :], start=k == 0, stop=k == KD - 1)
            elif kind == "dt":
                w = slot(pos, 272)
                for k in range(KD):
                    pe.matmul(psum[0:H, bk, :], w[:, k, 256:264], hT[:, k, :], start=k == 0, stop=k == KD - 1)
                for s in range(2):
                    for k in range(KD):
                        mm = pe.matmul(psum[DIR1:ROWS, bk, STREAM * s:STREAM * s + STREAM], w[:, k, 264:272],
                                       hT[:, k, STREAM * s:STREAM * s + STREAM][:, ::-1], start=k == 0, stop=k == KD - 1)
            else:
                n = 256 if kind == "kv" else 512
                w = slot(pos, n)
                for k in range(KD):
                    mm = pe.matmul(bank(bk, n), hT[:, k, P * b:P * b + P], w[:, k, :], start=k == 0, stop=k == KD - 1)
            mm.then_inc(S("in_full"), 1)
        for who in done[-6:]:
            pe.wait_ge(*pe_more(f"in_{who}"))

    def act_in_even(*kinds):
        for i, (kind, b, who) in enumerate(IN_EVEN):
            if kind not in kinds:
                continue
            act.wait_ge(S("in_full"), i + 1)
            src = bank(i % 6)
            if kind == "xbc":
                ins = act.activation(raw[:, b, :, 1:STREAM + 1], src.rearrange("p (s n) -> p s n", s=2), ACT.Copy)
            elif kind == "kv":
                ins = act.activation(qkv[:, b, 512:QKV], src[:, 0:256], ACT.Copy)
            elif kind == "q":
                ins = act.activation(qkv[:, b, 0:512], src, ACT.Copy)
            else:
                ins = act.activation(zs[:, b, :], src, ACT.Silu)
            ins.then_inc(S("in_act"), 1)

    def act_conv():
        for b in range(6):
            act.wait_ge(*act_more("conv_ready"))
            act.activation(xbcT[:, b, :], xbcT[:, b, :], ACT.Silu).then_inc(S("conv_done"), 1)

    def dve_conv(dst, src, wcol, bcol):
        dst = dst.rearrange("p (s n) -> p s n", s=src.shape[1])
        dve_step(dve.tensor_scalar(dst, src[:, :, 0:STREAM], wcol(0), bcol, ALU.mult, ALU.add))
        dve_step(dve.scalar_tensor_tensor(dst, src[:, :, 1:STREAM + 1], wcol(1), dst, ALU.mult, ALU.add))
        dve.scalar_tensor_tensor(dst, src[:, :, 2:STREAM + 2], wcol(2), dst, ALU.mult, ALU.add
                                 ).then_inc(S("conv_ready"), 1)

    def dve_in_even():
        for side in (0, STREAM + 1):
            dve_step(dve.memset(raw[:, :, :, side:side + 1], 0.0))
        dve.memset(sq[0:ROWS, :, :], 0.0).then_inc(S("raw_cleared"), 1)
        for b in range(6):
            dve.wait_ge(*dve_more("in_act"))
            dve_conv(xbcT[:, b, :], raw[:, b, :, :], lambda j, b=b: colsa[:, 48 + 6 * j + b:49 + 6 * j + b],
                     colsa[:, 66 + b:67 + b])
        dve.wait_ge(S("in_full"), 7)
        dve.wait_ge(S("raw_cleared"), 1)
        dve_step(dve.tensor_scalar(sq[0:H, 0, :], psum[0:H, 6 % 6, :], rowpar[0:H, 0:1], None, ALU.add))
        dve.tensor_scalar(sq[DIR1:ROWS, 0, :], psum[DIR1:ROWS, 6 % 6, :], rowpar[DIR1:ROWS, 0:1], None, ALU.add
                          ).then_inc(S("in_dve"), 1)

    qn = view(16384, [10, 64])

    def dve_qk_norm():
        def qk_of(t):
            return qkv[:, t, 0:640].rearrange("p (h n) -> p h n", h=10)

        dve.wait_ge(S("in_act"), 14)
        for t in range(NT):
            dve_step(dve.tensor_tensor(qn, qk_of(t), qk_of(t), ALU.mult))
            dve_step(dve.tensor_reduce(stat[:, 10 * t:10 * t + 10], qn, AX.X, ALU.add))
        dve_rstd(10 * NT, 64)
        for t in range(NT):
            qk = qk_of(t)
            dve_step(dve.tensor_tensor(qk, qk, stat2[:, 1, 10 * t:10 * t + 10].unsqueeze(2).broadcast_to([P, 10, 64]), ALU.mult))
            dve_step(dve.tensor_tensor(qk, qk, qkw[:], ALU.mult))
            if lat(t):
                v = qk.rearrange("p h (a b n) -> p (h a) b n", a=2, b=2)
                sw = qn.rearrange("p h (a b n) -> p (h a) b n", a=2, b=2)
                for o in range(2):
                    dve_step(dve.tensor_copy(sw[:, :, o, :], v[:, :, 1 - o, :]))
                dve_step(dve.tensor_tensor(qn, qn, sinb[:, t - 2, :].unsqueeze(1).broadcast_to([P, 10, 64]), ALU.mult))
                dve_step(dve.tensor_tensor(qk, qk, cosb[:, t - 2, :].unsqueeze(1).broadcast_to([P, 10, 64]), ALU.mult))
                dve_step(dve.tensor_tensor(qk, qk, qn, ALU.add))
        dve.tensor_copy(stat[:, 0:1], stat2[:, 1, 0:1]).then_inc(S("qk_normed"), 1)

    def dve_log1p(x, e, w, d, t):
        dve_step(dve.tensor_scalar(e, x, -1.0, None, ALU.mult))
        dve.tensor_tensor(e, e, x, ALU.max).then_inc(S("row_dve"), 1)
        dve.wait_ge(*dve_more("row_act"))
        dve_step(dve.tensor_scalar(w, e, 1.0, None, ALU.add))
        dve_step(dve.tensor_scalar(d, w, -1.0, None, ALU.add))
        dve.tensor_scalar(t, d, 1e-30, None, ALU.max).then_inc(S("row_dve"), 1)
        dve.wait_ge(*dve_more("row_act"))
        dve_step(dve.reciprocal(t, t))
        dve_step(dve.tensor_tensor(w, w, t, ALU.mult))
        dve_step(dve.tensor_tensor(w, w, e, ALU.mult))
        dve_step(dve.scalar_tensor_tensor(d, d, 0.0, e, ALU.is_equal, ALU.mult))
        dve_step(dve.tensor_tensor(w, w, d, ALU.add))

    def act_log1p(e, w):
        act.wait_ge(*act_more("row_dve"))
        act.activation(e, e, ACT.Exp, scale=-1.0).then_inc(S("row_act"), 1)
        act.wait_ge(*act_more("row_dve"))
        act.activation(w, w, ACT.Ln).then_inc(S("row_act"), 1)

    def rows(a, q):
        return a[0:ROWS, q, :]

    def dve_true_order(dst, src, nq):
        dve_step(dve.tensor_copy(dst[0:DIR1, 0:nq, :], src[0:DIR1, 0:nq, :]))
        for q in range(nq):
            last = dve.tensor_copy(dst[DIR1:ROWS, q, :].rearrange("p (s n) -> p s n", s=2),
                                   src[DIR1:ROWS, q, :].rearrange("p (s n) -> p s n", s=2)[:, :, ::-1])
            dve_step(last) if q < nq - 1 else last.then_inc(S("tq_ready"), 1)
        dve.wait_ge(*dve_more("tq_ready"))

    TOT = stat[0:ROWS, 8:12]
    ETOT = stat[0:ROWS, 12:16]

    def dve_ssd_rows():
        x0, e, w, d_ = (rows(sq, q) for q in range(4))
        dve.wait_ge(S("in_dve"), 1)
        dve_log1p(x0, e, w, d_, gtmp[0:ROWS, :])
        dve_step(dve.scalar_tensor_tensor(w, x0, 0.0, w, ALU.max, ALU.add))
        dve_step(dve.tensor_scalar(e, w, rowpar[:, 4:5], None, ALU.mult))
        for st in range(4):
            dve_step(dve.tensor_tensor_scan(x0[:, P * st:P * st + P], ones[0:ROWS, :], e[:, P * st:P * st + P],
                                            0.0, ALU.mult, ALU.add))
        dve.tensor_copy(TOT, x0.rearrange("p (s n) -> p s n", s=4)[:, :, P - 1]).then_inc(S("row_dve"), 1)
        dve.wait_ge(*dve_more("row_act"))
        dve_step(dve.tensor_tensor(d_, d_, w, ALU.mult))
        dve_true_order(tq, sq, 4)
        dve.tensor_tensor(dg[0:ROWS, :, :], ETOT.unsqueeze(2).broadcast_to([ROWS, 4, ROWS]),
                          ident[0:ROWS, 0:ROWS].unsqueeze(1).broadcast_to([ROWS, 4, ROWS]), ALU.mult
                          ).then_inc(S("dg_ready"), 1)

    def act_ssd_rows():
        x0, e, w, d_ = (rows(sq, q) for q in range(4))
        act_log1p(e, w)
        act.wait_ge(*act_more("row_dve"))
        act.activation(e, x0, ACT.Exp)
        for st in range(4):
            act.activation(d_[:, P * st:P * st + P], x0[:, P * st:P * st + P], ACT.Exp, scale=-1.0, bias=TOT[:, st:st + 1])
        act.activation(ETOT, TOT, ACT.Exp).then_inc(S("row_act"), 1)

    def pe_ssd_prepare():
        pe.wait_ge(*pe_more("conv_done", 6))
        for t in range(NT):
            for b in range(4):
                mm = pe.transpose(psum[:, t, P * b:P * b + P], xbcT[:, b, P * t:P * t + P], ident)
            mm.then_inc(S("pre_full"), 1)
        for t in range(NT):
            mm = pe.transpose(psum[:, 4, P * t:P * t + P], xbcT[:, 4, P * t:P * t + P], ident)
        mm.then_inc(S("pre_full"), 1)
        for g in range(2):
            if g:
                pe.wait_ge(*pe_more("xs_ready", 1))
            for t in range(NT):
                mm = pe.matmul(psum[:, 0 if g else 5, P * t:P * t + P], xbcT[64 * g:64 * g + 64, 4, P * t:P * t + P],
                               xbcT[64 * g:64 * g + 64, 5, P * t:P * t + P], start=True, stop=True)
            mm.then_inc(S("pre_full"), 1)
        pe.wait_ge(*pe_more("xs_ready", 3))
        pe.wait_ge(*pe_more("tq_ready"))
        for t in range(NT):
            for q in range(4):
                mm = pe.transpose(psum[:, 1 + t // 2, 160 * (t % 2) + ROWS * q:160 * (t % 2) + ROWS * (q + 1)],
                                  tq[0:ROWS, q, P * t:P * t + P], ident[0:ROWS, 0:ROWS])
            if t % 2:
                mm.then_inc(S("pre_full"), 1)
        pe.wait_ge(*pe_more("dg_ready"))
        pe.matmul(bank(3, 4 * ROWS), ones[0:ROWS, :], dg[0:ROWS, :, :].rearrange("p s r -> p (s r)"), start=True, stop=True
                  ).then_inc(S("pre_full"), 1)

    def act_ssd_prepare():
        act.wait_ge(S("qk_normed"), 1)
        for t in range(NT):
            act.wait_ge(*act_more("pre_full"))
            act.activation(xs[:, t, :], bank(t), ACT.Copy).then_inc(S("xs_ready"), 1)
        act.wait_ge(*act_more("pre_full", 6))
        act.activation(eb.rearrange("p s r -> p (s r)"), bank(3, 4 * ROWS), ACT.Copy).then_inc(S("xs_ready"), 1)

    def dve_ssd_prepare():
        dve.wait_ge(*dve_more("pre_full", 5))
        dve_step(dve.tensor_copy(btok.rearrange("p t n -> p (t n)"), bank(4)))
        dve.wait_ge(*dve_more("pre_full", 1))
        dve_step(dve.tensor_copy(cbT[:, 0].rearrange("p t n -> p (t n)"), bank(5)))
        dve.wait_ge(*dve_more("pre_full", 1))
        dve_step(dve.tensor_copy(cbT[:, 1].rearrange("p t n -> p (t n)"), bank(0)))
        for j in range(2):
            dve.wait_ge(*dve_more("pre_full"))
            dve_step(dve.tensor_copy(cq[:, 2 * j:2 * j + 2].rearrange("p t q r -> p (t q r)"), bank(1 + j, 320)))
        for d in range(2):
            dve_step(dve.memset(sbd[d], 0.0))
        dve.wait_ge(*dve_more("pre_full", 1))
        dve.wait_ge(S("xs_ready"), 5)
        dve.tensor_tensor(ysum.rearrange("p t (h n) -> p t h n", h=H), xs.rearrange("p t (h n) -> p t h n", h=H),
                          brd[:, 0:8].unsqueeze(1).unsqueeze(3).broadcast_to([P, NT, H, 64]), ALU.mult
                          ).then_inc(S("ssd_prepared"), 1)

    SSD_ITER = [(st, d) for st in range(4) for d in range(2)]

    def colq(t, q, d):
        return cq[:, t, q, DIR1 * d:DIR1 * d + H].unsqueeze(2).broadcast_to([P, H, 64])

    def heads(v):
        return v.rearrange("p (h n) -> p h n", h=H)

    SSD_MODS = [2, 1] * 4
    SSD_MOD0 = [FIRST + sum(SSD_MODS[:i]) for i in range(8)]
    OUT_MOD = FIRST + sum(SSD_MODS)
    ATT_MOD = {4 * j + 3: OUT_MOD + 1 + j for j in range(2 * MODC - OUT_MOD - 1)}

    def pe_ssd():
        pe.wait_ge(S("ssd_prepared"), 1)
        for i, (st, d) in enumerate(SSD_ITER):
            t = tile_of(st, d)
            for g in range(2):
                if i:
                    pe.wait_ge(*pe_more("arg_ready"))
                pe.matmul(bank(g), identb, decmask[d], start=True, stop=False)
                for h in range(4):
                    r = DIR1 * d + 4 * g + h
                    mm = pe.matmul(psum[:, g, P * h:P * h + P], ident[0:ROWS, r:r + 1].broadcast_to([ROWS, P]),
                                   tq[0:ROWS, 0, P * t:P * t + P], start=False, stop=h == 3)
                mm.then_inc(S("dec_full"), 1)
            pe_mod_rows(SSD_MOD0[i])
            if st > 0:
                pe.wait_ge(S("state_done"), i - 1)
                if st > 1 or d > 0:
                    pe.wait_ge(S("yoff_done"), i - 2)
                pe.matmul(bank(3), xbcT[:, 5, P * t:P * t + P], sbd[d], start=True, stop=True).then_inc(S("yoff_full"), 1)
            pe.wait_ge(*pe_more("xdt_ready"))
            if st < 3:
                if i:
                    pe.wait_ge(S("state_done"), i)
                pe.matmul(bank(4), btok[:, t, :], xdd, start=True, stop=True).then_inc(S("state_full"), 1)
            pe_mod_cols(SSD_MOD0[i])
            if SSD_MODS[i] > 1:
                pe_mod_rows(SSD_MOD0[i] + 1)
            if i:
                pe.wait_ge(*pe_more("ydiag_done"))
            for g in range(2):
                pe.wait_ge(*pe_more("wts_ready"))
                for h in range(4):
                    hh = 4 * g + h
                    mm = pe.matmul(psum[:, 2, 64 * hh:64 * hh + 64], wts[g][:, h, :], xdt[:, 64 * hh:64 * hh + 64],
                                   start=True, stop=True)
            mm.then_inc(S("ydiag_full"), 1)
            if SSD_MODS[i] > 1:
                pe_mod_cols(SSD_MOD0[i] + 1)

    def pool_ssd():
        pool.wait_ge(S("ssd_prepared"), 1)
        for i, (st, d) in enumerate(SSD_ITER):
            t = tile_of(st, d)
            if i:
                pool.wait_ge(*pool_more("ydiag_full"))
            pool_step(pool.tensor_tensor(heads(xdd), heads(xs[:, t, :]), colq(t, 3, d), ALU.mult))
            pool.tensor_tensor(heads(xdt), heads(xs[:, t, :]), colq(t, 2, d), ALU.mult).then_inc(S("xdt_ready"), 1)

    def act_ssd():
        for i in range(8):
            for g in range(2):
                act.wait_ge(*act_more("arg_ready"))
                act.activation(wts[g], wts[g], ACT.Exp).then_inc(S("exp_ready"), 1)
            for j in range(SSD_MODS[i]):
                act_mod(SSD_MOD0[i] + j)

    def dve_ssd():
        dve.wait_ge(S("ssd_prepared"), 1)
        for i, (st, d) in enumerate(SSD_ITER):
            t = tile_of(st, d)
            for g in range(2):
                dve.wait_ge(*dve_more("dec_full"))
                if i and g == 0:
                    dve.wait_ge(S("ydiag_full"), i)
                dve.tensor_tensor(wts[g], bank(g).rearrange("p (h n) -> p h n", h=4),
                                  cq[:, t, 0, DIR1 * d + 4 * g:DIR1 * d + 4 * g + 4].unsqueeze(2).broadcast_to([P, 4, P]),
                                  ALU.subtract).then_inc(S("arg_ready"), 1)
            if st > 0:
                dve.wait_ge(*dve_more("yoff_full"))
                dve.tensor_tensor(heads(yoff), heads(bank(3)), colq(t, 1, d), ALU.mult).then_inc(S("yoff_done"), 1)
                dve.wait_ge(*dve_more("yoff_done"))
                dve_step(dve.tensor_tensor(ysum[:, t, :], ysum[:, t, :], yoff, ALU.add))
            if st < 3:
                dve.wait_ge(*dve_more("state_full"))
                for g in range(2):
                    a = slice(64 * g, 64 * g + 64)
                    v = sbd[d][a, 256 * g:256 * g + 256]
                    col = DIR1 * d + 4 * g
                    dve_step(dve.tensor_tensor(v.rearrange("p (h n) -> p h n", h=4), v.rearrange("p (h n) -> p h n", h=4),
                                               eb[a, st, col:col + 4].unsqueeze(2).broadcast_to([64, 4, 64]), ALU.mult))
                    last = dve.tensor_tensor(v, v, psum[a, 4, 256 * g:256 * g + 256], ALU.add)
                    dve_step(last) if g == 0 else last.then_inc(S("state_done"), 1)
            for g in range(2):
                dve.wait_ge(*dve_more("exp_ready"))
                dve.tensor_tensor(wts[g], wts[g], cbT[:, g, t, :].unsqueeze(1).broadcast_to([P, 4, P]), ALU.mult
                                  ).then_inc(S("wts_ready"), 1)
            dve_mod(SSD_MOD0[i])
            dve.wait_ge(*dve_more("ydiag_full"))
            dve.tensor_tensor(ysum[:, t, :], ysum[:, t, :], bank(2), ALU.add).then_inc(S("ydiag_done"), 1)
            if SSD_MODS[i] > 1:
                dve_mod(SSD_MOD0[i] + 1)
            dve.wait_ge(*dve_more("ydiag_done"))

    def dve_ssd_out():
        dve.wait_ge(S("in_act"), 18)
        for t in range(NT):
            dve.tensor_tensor(ysum[:, t, :], ysum[:, t, :], zs[:, t, :], ALU.mult).then_inc(S("yz_ready"), 1)
        dve_mod(OUT_MOD)
        dve.wait_ge(*dve_more("sum_ready", NT))
        dve_rstd(NT, SSD_IN)
        for t in range(NT):
            dve.scalar_tensor_tensor(ysum[:, t, :], ysum[:, t, :], stat2[:, 1, t:t + 1], ssdn[:], ALU.mult, ALU.mult
                                     ).then_inc(S("cat_ready"), 1)

    def act_ssd_out():
        for t in range(NT):
            act.wait_ge(*act_more("yz_ready"))
            act.activation(zs[:, t, :], ysum[:, t, :], ACT.Square, accum_out=stat[:, t:t + 1]).then_inc(S("sum_ready"), 1)
        act_mod(OUT_MOD)
        act_rstd(NT)
        for t in range(NT):
            act.wait_ge(*act_more("cat_full"))
            act.activation(catT[:, 0:4, P * t:P * t + P], bank(t).rearrange("p (b n) -> p b n", b=4), ACT.Copy
                           ).then_inc(S("cat_act"), 1)

    def pe_ssd_out():
        pe.wait_ge(*pe_more("arg_ready", 2))
        pe.wait_ge(*pe_more("ydiag_done"))
        pe.wait_ge(S("yoff_done"), 6)
        pe_mod(OUT_MOD)
        for t in range(NT):
            pe.wait_ge(*pe_more("cat_ready"))
            for b in range(4):
                mm = pe.transpose(psum[:, t, P * b:P * b + P], ysum[:, t, P * b:P * b + P], ident)
            mm.then_inc(S("cat_full"), 1)
        pe.wait_ge(*pe_more("cat_act", NT))

    NM, RSUM, ESINK, RDEN = (att[:, j, :] for j in range(4))
    ATT = [(t, h) for t in range(NT) for h in range(H)]

    def dve_att_prepare():
        dve.wait_ge(S("cat_full"), NT)
        for g in range(2):
            last = dve.tensor_copy(kdup[:, :, 2 * g:2 * g + 2, :],
                                   qkv[:, :, 512 + 64 * g:576 + 64 * g].unsqueeze(2).broadcast_to([P, NT, 2, 64]))
            dve_step(last) if g == 0 else last.then_inc(S("qk_ready"), 1)

    def act_att_prepare():
        for t in range(NT):
            act.wait_ge(*act_more("qk_full"))
            b = 2 * (t % 2)
            act.activation(qT[:, :, P * t:P * t + P], bank(b).rearrange("p (b n) -> p b n", b=4), ACT.Copy)
            act.activation(kT2[:, :, P * t:P * t + P], bank(b + 1, 256).rearrange("p (b n) -> p b n", b=2), ACT.Copy
                           ).then_inc(S("qkT_ready"), 1)

    def pe_att_prepare():
        pe.wait_ge(*pe_more("qk_ready"))
        for t in range(NT):
            if t >= 2:
                pe.wait_ge(*pe_more("qkT_ready"))
            b0 = 2 * (t % 2)
            for b in range(4):
                pe.transpose(psum[:, b0, P * b:P * b + P], qkv[:, t, P * b:P * b + P], ident)
            for b in range(2):
                mm = pe.transpose(psum[:, b0 + 1, P * b:P * b + P], kdup[:, t, 2 * b:2 * b + 2, :].rearrange("p a n -> p (a n)"), ident)
            mm.then_inc(S("qk_full"), 1)
        pe.wait_ge(*pe_more("qkT_ready", 2))

    def nkeys(t):
        return TOK if lat(t) else STREAM

    def pe_att():
        def transposes(i):
            t, h = ATT[i]
            pe.wait_ge(*pe_more("prob_ready"))
            if i >= 2:
                pe.wait_ge(*pe_more("probT_ready"))
            for k in range(nkeys(t) // P):
                mm = pe.transpose(psum[:, 3 + i % 2, P * k:P * k + P], pbuf[i % 3][:, P * k:P * k + P], ident)
            mm.then_inc(S("probT_full"), 1)

        def values(gi):
            t, g = gi // 2, gi % 2
            pe.wait_ge(S("probT_ready"), 4 * gi + 4)
            if gi:
                pe.wait_ge(*pe_more("o_done"))
            nk = nkeys(t) // P
            for par in range(2):
                for k in range(nk):
                    mm = pe.matmul(psum[64 * par:64 * par + 64, 5, 0:256], qkv[:, k, 640 + 64 * g:704 + 64 * g],
                                   ptb[gi % 2][:, k, par, :, :].rearrange("p j n -> p (j n)"), start=k == 0, stop=k == nk - 1)
            mm.then_inc(S("o_full"), 1)

        for i, (t, h) in enumerate(ATT):
            if i >= 3:
                pe.wait_ge(S("prob_ready"), i - 2)
            a, n = 64 * (h % 2), nkeys(t)
            if lat(t):
                pe.matmul(bank(i % 3), identb, attmask[t - 2], start=True, stop=False)
            pe.matmul(bank(i % 3, n), qT[a:a + 64, h // 2, P * t:P * t + P], kT2[a:a + 64, h // 4, 0:n],
                      start=not lat(t), stop=True).then_inc(S("score_full"), 1)
            if i >= 2:
                transposes(i - 2)
            if i >= 6 and (i - 6) % 4 == 0:
                values((i - 6) // 4)
            if i in ATT_MOD:
                pe_mod(ATT_MOD[i])
        for i in (len(ATT) - 2, len(ATT) - 1):
            transposes(i)
        values(len(ATT) // 4 - 1)
        pe.wait_ge(*pe_more("o_done"))
        pe.wait_ge(*pe_more("probT_ready", 2))

    def dve_att():
        def probs(i):
            t, h = ATT[i]
            dve.wait_ge(*dve_more("sum_ready"))
            dve_step(dve.tensor_tensor(RDEN[:, i:i + 1], RSUM[:, i:i + 1], ESINK[:, i:i + 1], ALU.add))
            dve_step(dve.reciprocal(RDEN[:, i:i + 1], RDEN[:, i:i + 1]))
            p = pbuf[i % 3][:, 0:nkeys(t)]
            dve.tensor_scalar(p, p, RDEN[:, i:i + 1], None, ALU.mult).then_inc(S("prob_ready"), 1)

        for i, (t, h) in enumerate(ATT):
            dve.wait_ge(*dve_more("score_full"))
            dve_step(dve.tensor_reduce(NM[:, i:i + 1], bank(i % 3, nkeys(t)), AX.X, ALU.max))
            dve_step(dve.tensor_scalar(NM[:, i:i + 1], NM[:, i:i + 1], 0.125, brd[:, 8 + h:9 + h], ALU.mult, ALU.max))
            dve.tensor_scalar(NM[:, i:i + 1], NM[:, i:i + 1], -1.0, None, ALU.mult).then_inc(S("max_ready"), 1)
            if i:
                probs(i - 1)
            if i in ATT_MOD:
                dve_mod(ATT_MOD[i])
        probs(len(ATT) - 1)

    def act_att():
        def evac(i):
            t, h = ATT[i]
            gi, par, j = i // 4, h % 2, (h % 4) // 2
            nk = nkeys(t) // P
            act.wait_ge(*act_more("probT_full"))
            if gi >= 2 and i % 4 == 0:
                act.wait_ge(S("o_full"), gi - 1)
            act.activation(ptb[gi % 2][:, 0:nk, par, j, :], bank(3 + i % 2, P * nk).rearrange("p (k n) -> p k n", k=nk), ACT.Copy
                           ).then_inc(S("probT_ready"), 1)

        def evac_o(gi):
            t, g = gi // 2, gi % 2
            act.wait_ge(*act_more("o_full"))
            act.activation(catT[:, 4 + 2 * g:6 + 2 * g, P * t:P * t + P], bank(5, 256).rearrange("p (j n) -> p j n", j=2), ACT.Copy
                           ).then_inc(S("o_done"), 1)

        for i, (t, h) in enumerate(ATT):
            act.wait_ge(*act_more("max_ready"))
            if i >= 3:
                act.wait_ge(S("probT_full"), i - 2)
            act_step(act.activation(pbuf[i % 3][:, 0:nkeys(t)], bank(i % 3, nkeys(t)), ACT.Exp, bias=NM[:, i:i + 1], scale=0.125,
                                    accum_out=RSUM[:, i:i + 1]))
            act.activation(ESINK[:, i:i + 1], brd[:, 8 + h:9 + h], ACT.Exp, bias=NM[:, i:i + 1]).then_inc(S("sum_ready"), 1)
            if i >= 2:
                evac(i - 2)
            if i >= 7 and (i - 7) % 4 == 0:
                evac_o((i - 7) // 4)
            if i in ATT_MOD:
                act_mod(ATT_MOD[i])
        for i in (len(ATT) - 2, len(ATT) - 1):
            evac(i)
        evac_o(len(ATT) // 4 - 1)

    def pe_grow(l, which, streams):
        blk = 16 + 24 * which
        pe.wait_ge(S("mod_done"), 6)
        for s in streams:
            for half in range(2):
                if s != streams[0]:
                    pe.wait_ge(*pe_more("grow_done"))
                for k in range(4):
                    mm = pe.matmul(psum[:, 6 + half, P * k:P * k + P],
                                   mcol[:, l, blk + 4 * half + k, s:s + 1].broadcast_to([P, P]), ident, start=True, stop=True)
                mm.then_inc(S("grow_full"), 1)
        for _ in range(2):
            pe.wait_ge(*pe_more("grow_done"))

    def act_grow(streams):
        for s in streams:
            for half in range(2):
                act.wait_ge(*act_more("grow_full"))
                act.activation(grow[:, s, 512 * half:512 * half + 512], bank(6 + half), ACT.Copy).then_inc(S("grow_done"), 1)

    def otmp(i):
        return view(16384 + 512 * (i % 3), [512])

    def pe_out(tiles, pos):
        n = 0
        for half in range(2):
            weights_here(pos + half)
            w = slot(pos + half, 512)
            for t in tiles:
                if n >= 6:
                    pe.wait_ge(*pe_more("out_done"))
                for k in range(KD):
                    mm = pe.matmul(bank(n % 6), catT[:, k, P * t:P * t + P], w[:, k, :], start=k == 0, stop=k == KD - 1)
                mm.then_inc(S("out_full"), 1)
                n += 1
        pe.wait_ge(*pe_more("out_done", min(n, 6)))

    def dve_out(tiles, l):
        n = 0
        dve.wait_ge(S("grow_done"), GROW_AFTER[l][0])
        for half in range(2):
            for t in tiles:
                dve.wait_ge(*dve_more("out_full"))
                if n >= 3:
                    dve.wait_ge(*dve_more("res_added"))
                dve.tensor_tensor(otmp(n), bank(n % 6), grow[:, 0 if lat(t) else 1, 512 * half:512 * half + 512], ALU.mult
                                  ).then_inc(S("out_done"), 1)
                n += 1
        dve.wait_ge(*dve_more("res_added", min(n, 3)))

    def pool_out(tiles):
        n = 0
        for half in range(2):
            for t in tiles:
                pool.wait_ge(*pool_more("out_done"))
                v = xres[:, t, 512 * half:512 * half + 512]
                pool.tensor_tensor(v, v, otmp(n), ALU.add).then_inc(S("res_added"), 1)
                n += 1
        pool.wait_ge(*pool_more("res_added", n))


    rawo = view(4096, [4, 2, STREAM + 2])
    accv = view(6160, [4, TOK])
    qTo = view(8208, [4, STREAM])
    kTo = view(9232, [4, TOK])
    ktok = view(11280, [NT, 512])
    vaug = view(13328, [NT, H, VA])
    og = view(17456, [2, D])
    sqo = view(19504, [5, TOK])
    tqo = view(22064, [5, TOK])
    tmpo = view(24624, [TOK])
    hacc = view(4096, [2, D])
    qk = view(6144, [2, H, P])
    state = [view(19504 + 516 * d, [4, VA]) for d in range(2)]
    wto = [view(20536 + 512 * i, [4, P]) for i in range(2)]
    qe = view(21560, [4, P])
    ktil = view(9232, [512])
    num = view(9744, [D])
    sq1 = view(10768, [512])
    coq = rt[:, 0:NT * 3 * ROWS].rearrange("p (t q r) -> p t q r", t=NT, q=3)
    spb = rt[:, 480:600].rearrange("p (s r) -> p s r", s=3)
    dgo = rt[:, 600:720].rearrange("p (s r) -> p s r", s=3)
    den = rt[:, 720:744].rearrange("p (j h) -> p j h", j=3)
    chain = rt[:, 744:784].rearrange("p (j s) -> p j s", j=10)
    BL, CML, MIN, MNEW, SPA, DEL, T1, T2 = (chain[0:ROWS, j, :] for j in range(8))

    OD0 = MOE_BASE[0] + 3 * E
    EVEN_FILLS = len(IN_EVEN)
    IN_ODD = [("q", b) for b in range(4)] + [("k", b) for b in range(4)] + [("v", b) for b in range(8)]

    def pe_in_odd():
        w = slot(OD0, 32)
        weights_here(OD0)
        for j, c0 in enumerate((0, 16)):
            for k in range(KD):
                pe.matmul(psum[0:H, j, :], w[:, k, c0:c0 + H], hT[:, k, :], start=k == 0, stop=k == KD - 1)
            for s in range(2):
                for k in range(KD):
                    mm = pe.matmul(psum[DIR1:ROWS, j, STREAM * s:STREAM * s + STREAM], w[:, k, c0 + H:c0 + 2 * H],
                                   hT[:, k, STREAM * s:STREAM * s + STREAM][:, ::-1], start=k == 0, stop=k == KD - 1)
            mm.then_inc(S("in_full"), 1)

        def transposes(j):
            kind, b = IN_ODD[j]
            pe.wait_ge(S("conv_done"), 6 + j + 1)
            bk = 4 + j % 2
            if j >= 6:
                pe.wait_ge(*pe_more("tok_done"))
            src = kTo[:, b, :] if kind == "k" else accv[:, j % 4, :]
            for t in range(NT):
                mm = pe.transpose(psum[:, bk, P * t:P * t + P], src[:, P * t:P * t + P], ident)
            mm.then_inc(S("tok_full"), 1)

        at = None
        for j, (kind, b) in enumerate(IN_ODD):
            bk = (j + 2) % 4
            if j in (2, 3):
                pe.wait_ge(*pe_more("gates_read"))
            elif j >= 4:
                pe.wait_ge(*pe_more("raw_ready"))
            pos = OD0 + 1 + j // 4
            if pos != at:
                weights_here(pos)
                at = pos
            w = slot(pos, 512)
            tok = slice(STREAM, TOK) if kind == "q" else slice(0, TOK)
            for k in range(KD):
                mm = pe.matmul(bank(bk, tok.stop - tok.start), w[:, k, P * (b % 4):P * (b % 4) + P], hT[:, k, tok],
                               start=k == 0, stop=k == KD - 1)
            mm.then_inc(S("in_full"), 1)
            if j >= 7:
                transposes(j - 3)
        for n in range(4):
            half, t = n // 2, 2 + n % 2
            pos = OD0 + 5 + half
            if n % 2 == 0:
                weights_here(pos)
            pe.wait_ge(*pe_more("raw_ready"))
            w = slot(pos, 512)
            for k in range(KD):
                mm = pe.matmul(bank((18 + n) % 4), hT[:, k, P * t:P * t + P], w[:, k, :], start=k == 0, stop=k == KD - 1)
            mm.then_inc(S("in_full"), 1)
            if n < 3:
                transposes(13 + n)
        pe.wait_ge(S("og_done"), 4)
        pe.wait_ge(*pe_more("tok_done", 2))

    def act_in_odd():
        act_log1p(rows(sqo, 2), rows(sqo, 3))
        act_od_rows()
        act.wait_ge(*act_more("raw_cleared"))
        act_more("in_full", EVEN_FILLS + 2)

        def silu(j):
            kind, b = IN_ODD[j]
            v = {"q": qTo[:, b, :] if kind == "q" else None, "k": kTo[:, b, :] if kind == "k" else None, "v": accv[:, j % 4, :]}[kind]
            act.wait_ge(*act_more("conv_ready"))
            act.activation(v, v, ACT.Silu).then_inc(S("conv_done"), 1)

        for j, (kind, b) in enumerate(IN_ODD):
            act.wait_ge(*act_more("in_full"))
            if j >= 4:
                act.wait_ge(S("conv_ready"), 6 + j - 3)
            bk = (j + 2) % 4
            if kind == "q":
                act.activation(rawo[:, j % 4, 1, 1:STREAM + 1], bank(bk, STREAM), ACT.Copy).then_inc(S("raw_ready"), 1)
            else:
                act.activation(rawo[:, j % 4, :, 1:STREAM + 1], bank(bk).rearrange("p (s n) -> p s n", s=2), ACT.Copy
                               ).then_inc(S("raw_ready"), 1)
            if j:
                silu(j - 1)
        silu(len(IN_ODD) - 1)
        for n in range(4):
            act.wait_ge(*act_more("in_full"))
            act.activation(og[:, n % 2, 512 * (n // 2):512 * (n // 2) + 512], bank((18 + n) % 4), ACT.Tanh, scale=0.5
                           ).then_inc(S("og_done"), 1)

    def dve_in_odd():
        dve_step(dve.memset(sqo[0:ROWS, :, :], 0.0))
        for side in (0, STREAM + 1):
            last = dve.memset(rawo[:, :, :, side:side + 1], 0.0)
            dve_step(last) if side == 0 else last.then_inc(S("raw_cleared"), 1)
        dve_step(dve.memset(vaug[:, :, :, DV:VA], 1.0))
        dve.wait_ge(S("in_full"), EVEN_FILLS + 2)
        for j, q, par in ((0, 0, 2), (1, 1, 3)):
            dve_step(dve.tensor_scalar(sqo[0:H, q, :], psum[0:H, j, :], rowpar[0:H, par:par + 1], None, ALU.add))
            dve.tensor_scalar(sqo[DIR1:ROWS, q, :], psum[DIR1:ROWS, j, :], rowpar[DIR1:ROWS, par:par + 1], None, ALU.add
                              ).then_inc(S("gates_read"), 1)
        dve.wait_ge(S("gates_read"), 2)
        dve_od_rows()

        def tok(j):
            kind, b = IN_ODD[j]
            dve.wait_ge(*dve_more("tok_full"))
            src = bank(4 + j % 2).rearrange("p (t n) -> p t n", t=NT)
            dst = ktok[:, :, P * b:P * b + P] if kind == "k" else vaug[:, :, b, 0:DV]
            dve.tensor_copy(dst, src).then_inc(S("tok_done"), 1)

        for j, (kind, b) in enumerate(IN_ODD):
            dve.wait_ge(*dve_more("raw_ready"))
            wc = lambda i, j=j: colsb[:, 16 * i + j:16 * i + j + 1]
            if kind == "q":
                dve_conv(qTo[:, b, :], rawo[:, j % 4, 1:2, :], wc, colsb[:, 48 + j:49 + j])
            elif kind == "k":
                dve_conv(kTo[:, b, :], rawo[:, j % 4, :, :], wc, colsb[:, 48 + j:49 + j])
            else:
                if j >= 8 + 4:
                    dve.wait_ge(S("tok_full"), j - 7)
                dve_conv(accv[:, j % 4, :], rawo[:, j % 4, :, :], wc, colsb[:, 48 + j:49 + j])
            if j >= 8:
                tok(j - 4)
        for j in range(12, 16):
            tok(j)

    def chunks(v):
        return v.rearrange("p (s n) -> p s n", s=4)

    def dve_od_rows():
        v, f, e3, w4, d5 = (rows(sqo, q) for q in range(5))
        t = tmpo[0:ROWS, :]
        dve_log1p(f, e3, w4, d5, t)
        dve_step(dve.scalar_tensor_tensor(f, f, 0.0, w4, ALU.min, ALU.subtract))
        b = e3
        for st in range(4):
            dve_step(dve.tensor_tensor_scan(b[:, P * st:P * st + P], ones[0:ROWS, :], f[:, P * st:P * st + P],
                                            0.0, ALU.mult, ALU.add))
        dve_step(dve.tensor_tensor(v, v, b, ALU.subtract))
        for st in range(4):
            dve_step(dve.tensor_tensor_scan(w4[:, P * st:P * st + P], ones[0:ROWS, :], v[:, P * st:P * st + P],
                                            NEG, ALU.mult, ALU.max))
        dve_step(dve.tensor_copy(BL, chunks(b)[:, :, P - 1]))
        dve_step(dve.tensor_tensor(CML, BL, chunks(w4)[:, :, P - 1], ALU.add))
        dve_step(dve.memset(MIN[:, 0:1], 0.0))
        for st in range(3):
            a = slice(st, st + 1)
            dve_step(dve.tensor_tensor(T1[:, a], BL[:, a], MIN[:, a], ALU.add))
            dve_step(dve.tensor_tensor(MIN[:, st + 1:st + 2], T1[:, a], CML[:, a], ALU.max))
        dve_step(dve.tensor_tensor(SPA[:, 0:3], T1[:, 0:3], MIN[:, 1:4], ALU.subtract))
        dve_step(dve.tensor_tensor(DEL[:, 0:3], BL[:, 0:3], MIN[:, 1:4], ALU.subtract))
        lt = slice(STREAM, TOK)
        dve_step(dve.tensor_tensor(w4[:, lt], w4[:, lt], b[:, lt], ALU.add))
        for st in (2, 3):
            dve_step(dve.tensor_scalar(d5[:, P * st:P * st + P], b[:, P * st:P * st + P], MIN[:, st:st + 1], None, ALU.add))
        dve_step(dve.tensor_tensor(w4[:, lt], w4[:, lt], d5[:, lt], ALU.max))
        dve_step(dve.tensor_tensor(b[:, lt], b[:, lt], w4[:, lt], ALU.subtract))
        dve_step(dve.tensor_tensor(d5[:, lt], d5[:, lt], w4[:, lt], ALU.subtract))
        dve_step(dve.memset(f[:, 3 * P:], 0.0))
        for q in (b, w4, d5):
            last = dve.memset(q[:, 0:STREAM], 0.0)
            dve_step(last) if q is not d5 else last.then_inc(S("row_dve"), 1)
        dve.wait_ge(*dve_more("row_act"))
        dve_true_order(tqo, sqo, 5)
        dve.tensor_tensor(dgo[0:ROWS, :, :], SPA[:, 0:3].unsqueeze(2).broadcast_to([ROWS, 3, ROWS]),
                          ident[0:ROWS, 0:ROWS].unsqueeze(1).broadcast_to([ROWS, 3, ROWS]), ALU.mult
                          ).then_inc(S("dg_ready"), 1)

    def act_od_rows():
        v, f, b, w4, d5 = (rows(sqo, q) for q in range(5))
        act.wait_ge(*act_more("row_dve"))
        for st in range(3):
            a = slice(P * st, P * st + P)
            act.activation(f[:, a], v[:, a], ACT.Exp, bias=DEL[:, st:st + 1])
        act.activation(w4, w4, ACT.Exp, scale=-1.0)
        act.activation(d5, d5, ACT.Exp)
        act.activation(SPA[:, 0:3], SPA[:, 0:3], ACT.Exp).then_inc(S("row_act"), 1)

    def pe_ml_prepare():
        pe.wait_ge(*pe_more("tq_ready"))
        for t in range(NT):
            for j, q in enumerate((0, 1, 3)):
                mm = pe.transpose(psum[:, t // 2, 120 * (t % 2) + ROWS * j:120 * (t % 2) + ROWS * (j + 1)],
                                  tqo[0:ROWS, q, P * t:P * t + P], ident[0:ROWS, 0:ROWS])
            if t % 2:
                mm.then_inc(S("pre_full"), 1)
        pe.wait_ge(*pe_more("dg_ready"))
        pe.matmul(bank(2, 3 * ROWS), ones[0:ROWS, :], dgo[0:ROWS, :, :].rearrange("p s r -> p (s r)"), start=True, stop=True
                  ).then_inc(S("pre_full"), 1)
        pe.wait_ge(S("conv_done"), 6 + 8)
        for n in range(4):
            t, odd = n // 2, n % 2
            for h in range(4):
                hh = 2 * h + odd
                a = 64 * odd
                mm = pe.matmul(psum[:, 3 + n, P * h:P * h + P], kTo[a:a + 64, hh // 2, STREAM + P * t:STREAM + P * t + P],
                               qTo[a:a + 64, hh // 2, P * t:P * t + P], start=True, stop=True)
            mm.then_inc(S("pre_full"), 1)

    def dve_ml_prepare():
        for j in range(2):
            dve.wait_ge(*dve_more("pre_full"))
            dve_step(dve.tensor_copy(coq[:, 2 * j:2 * j + 2].rearrange("p t q r -> p (t q r)"), bank(j, 240)))
        dve.wait_ge(*dve_more("pre_full"))
        dve_step(dve.tensor_copy(spb.rearrange("p s r -> p (s r)"), bank(2, 3 * ROWS)))
        for d in range(2):
            dve_step(dve.memset(state[d], 0.0))
        for n in range(4):
            dve.wait_ge(*dve_more("pre_full"))
            last = dve.tensor_scalar(qk[:, n // 2].rearrange("p (h o) n -> p o h n", o=2)[:, n % 2],
                                     bank(3 + n).rearrange("p (h n) -> p h n", h=4), 0.125, None, ALU.mult)
            dve_step(last) if n < 3 else last.then_inc(S("ml_prepared"), 1)
        dve.wait_ge(S("ml_prepared"), 1)

    def pe_ml():
        pe.wait_ge(S("ml_prepared"), 1)
        n_state = 0
        for i, (st, d) in enumerate(SSD_ITER):
            t = tile_of(st, d)
            if st >= 2:
                if st > 2 or d > 0:
                    pe.wait_ge(*pe_more("qe_ready"))
                for b in range(4):
                    for lo in range(2):
                        r = DIR1 * d + 2 * b + lo
                        mm = pe.matmul(psum[64 * lo:64 * lo + 64, 6, P * b:P * b + P],
                                       ident[0:ROWS, r:r + 1].broadcast_to([ROWS, 64]),
                                       tqo[0:ROWS, 4, P * t:P * t + P], start=True, stop=True)
                mm.then_inc(S("einter_full"), 1)
                for g in range(2):
                    if st > 2 or d > 0:
                        pe.wait_ge(*pe_more("oarg_ready"))
                    pe.matmul(bank(4 + g), identb, decmask[d], start=True, stop=False)
                    for h in range(4):
                        r = DIR1 * d + 4 * g + h
                        mm = pe.matmul(psum[:, 4 + g, P * h:P * h + P], ident[0:ROWS, r:r + 1].broadcast_to([ROWS, P]),
                                       tqo[0:ROWS, 2, P * t:P * t + P], start=False, stop=h == 3)
                    mm.then_inc(S("odec_full"), 1)
                pe.wait_ge(S("qe_ready"), 2 * (st - 2) + d + 1)
                if i:
                    pe.wait_ge(S("sstate_done"), n_state)
                if st > 2 or d > 0:
                    pe.wait_ge(S("num_done"), 2 * (st - 2) + d)
                for h in (0, 2, 4, 6, 1, 3, 5, 7):
                    if h in (0, 4):
                        pe.wait_ge(*pe_more("owts_ready"))
                    a = 64 * (h % 2)
                    b, j = 2 * (h % 2) + h // 6, h // 2 % 3
                    o = psum[:, b, VA * j:VA * j + VA]
                    pe.matmul(o, wto[h // 4][:, h % 4, :], vaug[:, t, h, :], start=True, stop=False)
                    mm = pe.matmul(o, qe[a:a + 64, h // 2, :], state[d][a:a + 64, h // 2, :], start=False, stop=True)
                mm.then_inc(S("num_full"), 1)
            if st < 3:
                pe.wait_ge(*pe_more("ktil_ready"))
                if i and st < 2:
                    pe.wait_ge(S("sstate_done"), n_state)
                elif st == 2:
                    pe.wait_ge(S("num_done"), d + 1)
                for b in range(4):
                    mm = pe.matmul(bank(b, 2 * VA), ktil[:, P * b:P * b + P],
                                   vaug[:, t, 2 * b:2 * b + 2, :].rearrange("p h n -> p (h n)"), start=True, stop=True)
                mm.then_inc(S("sprod_full"), 1)
                n_state += 1

    NUM_BANKS = [(0, slice(0, 5, 2)), (1, slice(6, 7, 2)), (2, slice(1, 6, 2)), (3, slice(7, 8, 2))]

    def dve_ml():
        for i, (st, d) in enumerate(SSD_ITER):
            t = tile_of(st, d)
            if st < 3:
                if i:
                    dve.wait_ge(S("sprod_full"), min(i, 6))
                dve.scalar_tensor_tensor(heads(ktil), heads(ktok[:, t, :]), 0.125,
                                         coq[:, t, 1, DIR1 * d:DIR1 * d + H].unsqueeze(2).broadcast_to([P, H, 64]),
                                         ALU.mult, ALU.mult).then_inc(S("ktil_ready"), 1)
            if st >= 2:
                dve.wait_ge(*dve_more("einter_full"))
                if st > 2 or d > 0:
                    dve.wait_ge(*dve_more("num_full"))
                dve.tensor_tensor(qe, qTo[:, :, P * (t - 2):P * (t - 1)], bank(6).rearrange("p (b n) -> p b n", b=4), ALU.mult
                                  ).then_inc(S("qe_ready"), 1)
                for g in range(2):
                    dve.wait_ge(*dve_more("odec_full"))
                    dve.tensor_tensor(wto[g], bank(4 + g).rearrange("p (h n) -> p h n", h=4),
                                      coq[:, t, 0, DIR1 * d + 4 * g:DIR1 * d + 4 * g + 4].unsqueeze(2).broadcast_to([P, 4, P]),
                                      ALU.add).then_inc(S("oarg_ready"), 1)
                for g in range(2):
                    dve.wait_ge(*dve_more("oexp_ready"))
                    dve.tensor_tensor(wto[g], wto[g], qk[:, t - 2, 4 * g:4 * g + 4, :], ALU.mult).then_inc(S("owts_ready"), 1)
                dve.wait_ge(S("num_full"), 2 * (st - 2) + d + 1)
                for b, hs in NUM_BANKS:
                    nh = len(range(*hs.indices(H)))
                    dve_step(dve.tensor_copy(den[:, 0, hs], bank(b, nh * VA).rearrange("p (h n) -> p h n", h=nh)[:, :, DV]))
                dve_step(dve.tensor_scalar(den[:, 1, :], den[:, 0, :], -1.0, None, ALU.mult))
                dve_step(dve.tensor_tensor(den[:, 0, :], den[:, 0, :], den[:, 1, :], ALU.max))
                dve_step(dve.tensor_tensor(den[:, 0, :], den[:, 0, :], coq[:, t, 2, DIR1 * d:DIR1 * d + H], ALU.max))
                dve_step(dve.reciprocal(den[:, 0, :], den[:, 0, :]))
                dst = hacc[:, t - 2, :] if d == first_dir(t) else num
                for b, hs in NUM_BANKS:
                    nh = len(range(*hs.indices(H)))
                    last = dve.tensor_tensor(dst.rearrange("p (h n) -> p h n", h=H)[:, hs],
                                             bank(b, nh * VA).rearrange("p (h n) -> p h n", h=nh)[:, :, 0:DV],
                                             den[:, 0, hs].unsqueeze(2).broadcast_to([P, nh, DV]), ALU.mult)
                    dve_step(last) if b < 3 else last.then_inc(S("num_done"), 1)
                dve.wait_ge(*dve_more("num_done"))
                if d != first_dir(t):
                    dve_step(dve.tensor_tensor(hacc[:, t - 2, :], hacc[:, t - 2, :], num, ALU.add))
            if st < 3:
                dve.wait_ge(S("sprod_full"), i + 1)
                for b in range(4):
                    for lo in range(2):
                        a = slice(64 * lo, 64 * lo + 64)
                        col = DIR1 * d + 2 * b + lo
                        v = state[d][a, b, :]
                        last = dve.scalar_tensor_tensor(v, v, spb[a, st, col:col + 1], psum[a, b, VA * lo:VA * lo + VA],
                                                        ALU.mult, ALU.add)
                        dve_step(last) if (b, lo) != (3, 1) else last.then_inc(S("sstate_done"), 1)
                dve.wait_ge(*dve_more("sstate_done"))

    def first_dir(t):
        return 0 if t == 2 else 1

    def act_ml():
        for i in range(4):
            for g in range(2):
                act.wait_ge(*act_more("oarg_ready"))
                act.activation(wto[g], wto[g], ACT.Exp).then_inc(S("oexp_ready"), 1)

    def dve_ml_out():
        for t in range(2):
            h2 = num
            dve_step(dve.tensor_tensor(h2, hacc[:, t, :], hacc[:, t, :], ALU.mult))
            dve_step(dve.tensor_reduce(stat[:, 0:H], h2.rearrange("p (h n) -> p h n", h=H), AX.X, ALU.add))
            dve_rstd(H, DV)
            v = hacc[:, t, :]
            dve_step(dve.tensor_tensor(heads(v), heads(v), stat2[:, 1, 0:H].unsqueeze(2).broadcast_to([P, H, DV]), ALU.mult))
            dve_step(dve.tensor_tensor(v, v, hnorm[:], ALU.mult))
            dve_step(dve.scalar_tensor_tensor(v, og[:, t, :], 1.0, v, ALU.add, ALU.mult))
            dve.tensor_scalar(v, v, 0.5, None, ALU.mult).then_inc(S("cat_ready"), 1)

    def pe_ml_out():
        pe.wait_ge(S("num_done"), 4)
        for t in range(2):
            pe.wait_ge(*pe_more("cat_ready"))
            for half in range(2):
                for b in range(4):
                    mm = pe.transpose(psum[:, 2 * t + half, P * b:P * b + P], hacc[:, t, 512 * half + P * b:512 * half + P * b + P], ident)
                mm.then_inc(S("cat_full"), 1)
        pe.wait_ge(*pe_more("cat_act", 4))

    def act_ml_out():
        for t in range(2):
            act_rstd(H)
            for half in range(2):
                act.wait_ge(*act_more("cat_full"))
                act.activation(catT[:, 4 * half:4 * half + 4, P * (t + 2):P * (t + 3)], bank(2 * t + half).rearrange("p (b n) -> p b n", b=4),
                               ACT.Copy).then_inc(S("cat_act"), 1)


    def rtv(at, shape):
        n = int(np.prod(shape))
        names = "abcd"[:len(shape)]
        return rt[:, at:at + n].rearrange(f"p ({' '.join(names)}) -> p {' '.join(names)}", **dict(zip(names, shape)))

    def pe_router(l, tiles):
        n = P * len(tiles)
        c0 = P * tiles[0]
        pe.wait_ge(S("rw_ready"), 1)
        for k in range(KD):
            j = 32 * (k % 4)
            mm = pe.matmul(psum[j:j + 32, 4, 0:n], rw32[:, k, :], hT[:, k, c0:c0 + n], start=k < 4, stop=k >= 4)
        mm.then_inc(S("score4_full"), 1)
        for i, t in enumerate(tiles):
            if i >= 2:
                pe.wait_ge(*pe_more("back_act"))
                pe.wait_ge(*pe_more("back_dve"))
            for half in range(2):
                for k in range(4):
                    mm = pe.transpose(psum[:, 2 * (i % 2) + half, P * k:P * k + P], hT[:, 4 * half + k, P * t:P * t + P], ident)
            mm.then_inc(S("back_full"), 1)
            if i == 0:
                pe.wait_ge(*pe_more("srow_ready"))
                for j in range(len(tiles)):
                    mm = pe.transpose(psum[:, 5, P * j:P * j + P], modrow[:, P * j:P * j + P], ident)
                mm.then_inc(S("scol_full"), 1)
        for _ in range(2):
            pe.wait_ge(*pe_more("back_act"))
            pe.wait_ge(*pe_more("back_dve"))
        pe.wait_ge(*pe_more("mask_ready"))
        mk = maskb[:, 0:len(tiles), :]
        for i in range(len(tiles)):
            for j in range(i):
                pe.matmul(psum[:, 6, E * i:E * i + E], onesb, mk[:, j, :], start=j == 0, stop=False)
            pe.matmul(psum[:, 6, E * i:E * i + E], upper, mk[:, i, :], start=i == 0, stop=True)
        for j in range(len(tiles)):
            mm = pe.matmul(psum[:, 6, E * NT:E * NT + E], onesb, mk[:, j, :], start=j == 0, stop=j == len(tiles) - 1)
        mm.then_inc(S("pos_full"), 1)

    def act_router(l, tiles):
        n = P * len(tiles)
        act.wait_ge(*act_more("score4_full"))
        act.wait_ge(S("modcol_full"), 2 * MODC)
        act.activation(modrow[:, 0:n], bank(4, n), ACT.Copy).then_inc(S("srow_ready"), 1)
        for i, t in enumerate(tiles):
            act.wait_ge(*act_more("back_full"))
            act.activation(htok[:, t, 0:512], bank(2 * (i % 2)), ACT.Copy).then_inc(S("back_act"), 1)
            act.wait_ge(*act_more("back_act"))
            act.wait_ge(*act_more("back_dve"))
            act.dma_start(hdram[l][P * i:P * i + P, :], htok[:, t, :]).then_inc(S(f"hstored{l}"), 16)
        act.wait_ge(*act_more("neg_ready"))
        v = rtv(0, [NT, E])[:, 0:len(tiles), :]
        act.activation(v, v, ACT.Exp, scale=-1.0).then_inc(S("sig_exp"), 1)

    def dve_router_setup():
        dve_step(dve.memset(rw32[:], 0.0))
        dve.wait_ge(S("params"), PARAMS_IN)
        dve_step(dve.tensor_copy(tok32[:], tokid))
        dve_step(dve.memset(zrow[:], 0))
        dve.tensor_copy(rw32[:, :, 0:E], rw[:]).then_inc(S("rw_ready"), 1)

    def dve_router(l, tiles):
        n = len(tiles)
        for i, t in enumerate(tiles):
            dve.wait_ge(*dve_more("back_full"))
            dve.tensor_copy(htok[:, t, 512:1024], bank(2 * (i % 2) + 1)).then_inc(S("back_dve"), 1)
        sc, bi, mb, oh1, oh2, t16, u16 = (rtv(64 * j, [NT, E])[:, 0:n] for j in range(7))
        mx, mn, c23 = (rtv(448 + 32 * j, [NT, 4, 2])[:, 0:n] for j in range(3))
        gs, eq, gsel = (rtv(544 + 16 * j, [NT, 4])[:, 0:n] for j in range(3))
        one, p1, e1, q1, r1_ = (rtv(600 + 8 * j, [NT, 2])[:, 0:n] for j in range(5))
        s1, s2, big = (rtv(640 + 8 * j, [NT, 1])[:, 0:n] for j in range(3))
        cnt = rtv(680, [E])
        pos = rtv(704, [NT, E])[:, 0:n]
        cmax = rtv(800, [1])

        def bc(v, *shape):
            return v.broadcast_to([P, *shape])

        dve.wait_ge(*dve_more("scol_full"))
        dve.tensor_reduce(sc, bank(5, P * n).rearrange("p (t g r) -> p t r g", t=n, g=4)[:, :, 0:E, :], AX.X, ALU.add
                          ).then_inc(S("neg_ready"), 1)
        dve.wait_ge(*dve_more("sig_exp"))
        dve_step(dve.tensor_scalar(sc, sc, 1.0, None, ALU.add))
        dve_step(dve.reciprocal(sc, sc))
        dve_step(dve.tensor_tensor(bi, sc, bc(rbias[:].unsqueeze(1), n, E), ALU.add))
        pr = bi.rearrange("p t (g a b) -> p t g a b", g=4, a=2)
        for i in range(n):
            dve_step(dve.tensor_tensor(mx[:, i], pr[:, i, :, :, 0], pr[:, i, :, :, 1], ALU.max))
            dve_step(dve.tensor_tensor(mn[:, i], pr[:, i, :, :, 0], pr[:, i, :, :, 1], ALU.min))
        dve_step(dve.tensor_tensor(c23, mx, mn, ALU.add))
        dve_step(dve.tensor_tensor(gs, mx[:, :, :, 0], mx[:, :, :, 1], ALU.add))
        dve_step(dve.tensor_tensor(gs, gs, c23[:, :, :, 0], ALU.max))
        dve_step(dve.tensor_tensor(gs, gs, c23[:, :, :, 1], ALU.max))

        def first_max(sel, v, tmp, desc, k):
            dve_step(dve.tensor_reduce(big, v, AX.X, ALU.max))
            dve_step(dve.tensor_tensor(tmp, v, bc(big, n, k), ALU.is_equal))
            dve_step(dve.tensor_tensor(tmp, tmp, bc(desc.unsqueeze(1), n, k), ALU.mult))
            dve_step(dve.tensor_reduce(big, tmp, AX.X, ALU.max))
            dve_step(dve.tensor_tensor(sel, tmp, bc(big, n, k), ALU.is_equal))

        first_max(gsel, gs, eq, edesc[:, 12:16], 4)
        dve_step(dve.tensor_scalar(eq, gsel, -NEG, NEG, ALU.mult, ALU.add))
        for i in range(n):
            g4 = lambda a: a[:, i].rearrange("p (g a) -> p g a", g=4)
            dve_step(dve.tensor_tensor(g4(mb), g4(bi), gsel[:, i].unsqueeze(2).broadcast_to([P, 4, 4]), ALU.mult))
            dve_step(dve.tensor_tensor(g4(mb), g4(mb), eq[:, i].unsqueeze(2).broadcast_to([P, 4, 4]), ALU.add))
        first_max(oh1, mb, t16, edesc, E)
        dve_step(dve.scalar_tensor_tensor(mb, oh1, 2.0 * NEG, mb, ALU.mult, ALU.add))
        first_max(oh2, mb, t16, edesc, E)
        dve.tensor_tensor(maskb[:, 0:n, :], oh1, oh2, ALU.add).then_inc(S("mask_ready"), 1)
        for j, oh in enumerate((oh1, oh2)):
            dve_step(dve.tensor_tensor(t16, sc, oh, ALU.mult))
            dve_step(dve.tensor_reduce(one[:, :, j:j + 1], t16, AX.X, ALU.add))
        dve_step(dve.tensor_tensor(s1, one[:, :, 0:1], one[:, :, 1:2], ALU.add))
        dve_step(dve.reciprocal(s1, s1))
        dve_step(dve.tensor_tensor(gatew[:, 0:n, :], one, bc(s1, n, 2), ALU.mult))
        dve.wait_ge(*dve_more("pos_full"))
        dve_step(dve.tensor_copy(rt[:, 704:704 + E * n], psum[:, 6, 0:E * n]))
        dve_step(dve.tensor_reduce(cmax, psum[:, 6, E * NT:E * NT + E], AX.X, ALU.max))
        for j, oh in enumerate((oh1, oh2)):
            dve_step(dve.tensor_tensor(t16, pos, oh, ALU.mult))
            dve_step(dve.tensor_reduce(p1[:, :, j:j + 1], t16, AX.X, ALU.add))
            dve_step(dve.tensor_tensor(t16, bc(eiota.unsqueeze(1), n, E), oh, ALU.mult))
            dve_step(dve.tensor_reduce(e1[:, :, j:j + 1], t16, AX.X, ALU.add))
        dve_step(dve.tensor_scalar(q1, p1, float(P), None, ALU.is_ge))
        for r in range(2, RMAX):
            dve_step(dve.scalar_tensor_tensor(q1, p1, float(P * r), q1, ALU.is_ge, ALU.add))
        dve_step(dve.scalar_tensor_tensor(p1, q1, -float(P), p1, ALU.mult, ALU.add))
        dve_step(dve.scalar_tensor_tensor(q1, q1, float(E), e1, ALU.mult, ALU.add))
        dve_step(dve.scalar_tensor_tensor(r1_, p1, float(NCOL), q1, ALU.mult, ALU.add))
        dve_step(dve.tensor_copy(rowi[:, 0:n, :], r1_))
        dve_step(dve.scalar_tensor_tensor(r1_, q1, float(P), p1, ALU.mult, ALU.add))
        dve_step(dve.tensor_copy(rowy[:, 0:n, :], r1_))
        dve.tensor_copy(flag[:, l:l + 1], cmax[0:1, :]).then_inc(S("rows_ready"), 1)

    def pool_dispatch(l, tiles):
        n = len(tiles)
        pool.wait_ge(S("rw_ready"), 1)
        pool.dma_start(table[l].rearrange("(p n) a -> p (n a)", p=P), zrow[:]).then_inc(S(f"table_zeroed{l}"), 16)
        pool.wait_ge(*pool_more("rows_ready"))
        pool.wait_ge(S(f"table_zeroed{l}"), 16)
        for i in range(n):
            for j in range(2):
                pool.indirect_dma_start(table[l], bass.IndirectOffsetOnAxis(ap=rowi[:, i, j:j + 1], axis=0),
                                        tok32[:, i:i + 1], None).then_inc(S(f"scattered{l}"), 16)
        pool.wait_ge(S(f"scattered{l}"), 32 * n)
        pool.dma_start(idx[:], table[l].rearrange("(p n) a -> p (n a)", p=P)).then_inc(S("idx_in"), 16)
        pool.wait_ge(S("idx_in"), 16 * (l + 1))
        pool.wait_ge(S(f"hstored{l}"), 16 * n)

    xg = [view(1024 * i, [D]) for i in range(2)]
    xT = [view(2048 + 1024 * i, [KD, P]) for i in range(2)]
    sil = [view(4096 + 512 * i, [FE]) for i in range(2)]
    ah = [view(5120 + 512 * i, [FE]) for i in range(2)]
    aT = [view(6144 + 512 * i, [KF, P]) for i in range(2)]
    yb = [view(7168 + 1024 * i, [D]) for i in range(2)]

    def expert_weights(l, kind, e, ds=0):
        pos = position(l, kind, e) if isinstance(e, int) else position(l, kind, e[0], looped=True)
        if isinstance(e, int):
            weights_here(pos)
        else:
            pe.wait_ge(S(f"w_ready{pos % NSLOT}"), 16 * (pos // NSLOT + 1) + e[1] * (16 * 3 * GROUP // NSLOT))
        return slot(pos, 512) if kind != "w2" else slot(pos, D, KF)

    def val(base, e, off=0):
        return base + e + off if isinstance(e, int) else base + e[0] + off + e[1] * GROUP

    def num_of(e):
        return e if isinstance(e, int) else e[0]

    XT = E + 1

    def half_count(base, e, off=0):
        n = 16 * (base + num_of(e) // 2 + off)
        return n if isinstance(e, int) else n + e[1] * (16 * GROUP // 2)

    def gather_count(l, e):
        return half_count((9 if num_of(e) % 2 == 0 else 8) * l, e, 1)

    def pe_xt(l, e):
        b = num_of(e) % 2
        pe.wait_ge(S(f"gathered{b}"), gather_count(l, e))
        if not (isinstance(e, int) and e == 0):
            pe.wait_ge(S("xt_act"), val(XT * l, e))
            pe.wait_ge(S("xt_dve"), val(XT * l, e))
        for k in range(KD):
            mm = pe.transpose(psum[:, 4 + k // 4, P * (k % 4):P * (k % 4) + P], xg[b][:, P * k:P * k + P], ident)
        mm.then_inc(S("xt_full"), 1)

    def pe_h(l, e):
        b = num_of(e) % 2
        for j, (kind, done, free) in enumerate((("w1", "h1_full", "sil_done"), ("w3", "h3_full", "a_done"))):
            w = expert_weights(l, kind, e)
            if j == 0:
                pe.wait_ge(S("xt_act"), val(XT * l, e, 1))
                pe.wait_ge(S("xt_dve"), val(XT * l, e, 1))
            if not (isinstance(e, int) and e == 0):
                pe.wait_ge(S(free), val(E * l, e))
            for k in range(KD):
                mm = pe.matmul(bank(j), xT[b][:, k, :], w[:, k, :], start=k == 0, stop=k == KD - 1)
            mm.then_inc(S(done), 1)

    def pe_at(l, e):
        b = num_of(e) % 2
        pe.wait_ge(S("a_done"), val(E * l, e, 1))
        if not (isinstance(e, int) and e == 0):
            pe.wait_ge(S("at_done"), val(E * l, e))
        for k in range(KF):
            mm = pe.transpose(psum[:, 6, P * k:P * k + P], ah[b][:, P * k:P * k + P], ident)
        mm.then_inc(S("at_full"), 1)

    def pe_y(l, e):
        b = num_of(e) % 2
        w = expert_weights(l, "w2", e)
        pe.wait_ge(S("at_done"), val(E * l, e, 1))
        if not (isinstance(e, int) and e == 0):
            pe.wait_ge(S("y_act"), val(E * l, e))
            pe.wait_ge(S("y_dve"), val(E * l, e))
        for half in range(2):
            for k in range(KF):
                mm = pe.matmul(bank(2 + half), aT[b][:, k, :], w[:, k, 512 * half:512 * half + 512], start=k == 0, stop=k == KF - 1)
        mm.then_inc(S("y_full"), 1)

    def prev(e):
        return e - 1 if isinstance(e, int) else (e[0] - 1, e[1])

    def nxt(e):
        return e + 1 if isinstance(e, int) else (e[0] + 1, e[1])

    def in_groups(eng, body):
        for e in range(GROUP):
            body(e)
        with eng.Fori(1, E // GROUP) as j:
            for e in range(GROUP):
                body((e, j))

    def pe_moe(l):
        pe_xt(l, 0)

        def body(e):
            pe_h(l, e)
            if e != 0:
                pe_y(l, prev(e))
            pe_xt(l, nxt(e))
            pe_at(l, e)
        in_groups(pe, body)
        pe_y(l, E - 1)

    def flat(v):
        return v.rearrange("p k n -> p (k n)")

    def act_moe(l):
        def xt(e):
            act.wait_ge(S("xt_full"), val(XT * l, e, 1))
            if not (isinstance(e, int) and e < 2):
                act.wait_ge(S("h3_full"), val(E * l, e, -1))
            act.activation(flat(xT[num_of(e) % 2][:, 0:4, :]), bank(4), ACT.Copy).then_inc(S("xt_act"), 1)

        def y(e):
            act.wait_ge(S("y_full"), val(E * l, e, 1))
            if not (isinstance(e, int) and e < 2):
                act.wait_ge(S(f"ystored{num_of(e) % 2}"), half_count(8 * l, e))
            act.activation(yb[num_of(e) % 2][:, 0:512], bank(2), ACT.Copy).then_inc(S("y_act"), 1)

        def body(e):
            act.wait_ge(S("h1_full"), val(E * l, e, 1))
            if not (isinstance(e, int) and e < 2):
                act.wait_ge(S("a_done"), val(E * l, e, -1))
            act.activation(sil[num_of(e) % 2], bank(0), ACT.Silu).then_inc(S("sil_done"), 1)
            if e != 0:
                y(prev(e))
            xt(nxt(e))
        xt(0)
        in_groups(act, body)
        y(E - 1)

    def dve_moe(l):
        def xt(e):
            dve.wait_ge(S("xt_full"), val(XT * l, e, 1))
            if not (isinstance(e, int) and e < 2):
                dve.wait_ge(S("h3_full"), val(E * l, e, -1))
            dve.tensor_copy(flat(xT[num_of(e) % 2][:, 4:8, :]), bank(5)).then_inc(S("xt_dve"), 1)

        def y(e):
            dve.wait_ge(S("y_full"), val(E * l, e, 1))
            if not (isinstance(e, int) and e < 2):
                dve.wait_ge(S(f"ystored{num_of(e) % 2}"), half_count(8 * l, e))
            dve.tensor_copy(yb[num_of(e) % 2][:, 512:1024], bank(3)).then_inc(S("y_dve"), 1)

        def body(e):
            b = num_of(e) % 2
            dve.wait_ge(S("sil_done"), val(E * l, e, 1))
            dve.wait_ge(S("h3_full"), val(E * l, e, 1))
            if not (isinstance(e, int) and e < 2):
                dve.wait_ge(S("at_full"), val(E * l, e, -1))
            dve.tensor_tensor(ah[b], sil[b], bank(1), ALU.mult).then_inc(S("a_done"), 1)
            if e != 0:
                y(prev(e))
            xt(nxt(e))
            dve.wait_ge(S("at_full"), val(E * l, e, 1))
            if not (isinstance(e, int) and e < 2):
                dve.wait_ge(S("y_full"), val(E * l, e, -1))
            dve.tensor_copy(flat(aT[b]), bank(6)).then_inc(S("at_done"), 1)
        xt(0)
        in_groups(dve, body)
        y(E - 1)

    def gather_x(l, b, col, sem, *free):
        free = [(name, n if isinstance(n, int) else pool.to_reg(n)) for name, n in free]
        pool.wait_ge(S("idx_in"), 16 * (l + 1))
        for name, n in free:
            pool.wait_ge(name, n)
        return pool.indirect_dma_start(xg[b], None, hdram[l], bass.IndirectOffsetOnAxis(ap=col, axis=0)).then_inc(S(sem), 16)

    def pool_moe(l):
        gather_x(l, 0, idx[:, 0:1], "gathered0")

        def y(e):
            pool.wait_ge(S("y_act"), val(E * l, e, 1))
            pool.wait_ge(S("y_dve"), val(E * l, e, 1))
            row = e * P if isinstance(e, int) else e[0] * P + e[1] * (GROUP * P)
            dst = ydram[l][row:row + P, :] if isinstance(e, int) else ydram[l][bass.ds(row, P), :]
            pool.dma_start(dst, yb[num_of(e) % 2]).then_inc(S(f"ystored{num_of(e) % 2}"), 16)

        def body(e):
            k = num_of(e)
            if k == 0:
                if not isinstance(e, int):
                    pool.wait_ge(S("gathered0"), gather_count(l, e))
                    pool.wait_ge(S("gathered1"), gather_count(l, (-1, e[1])))
                a = 1 if isinstance(e, int) else e[1] * GROUP + 1
                src = idx[:, 1:1 + GROUP] if isinstance(e, int) else idx[:, bass.ds(a, GROUP)]
                pool.tensor_copy(idxg[:], src).then_inc(S("idxg_ready"), 1)
            free = [(S("idxg_ready"), 4 * l + 1 if isinstance(e, int) else e[1] + (4 * l + 1))]
            if e != 0:
                free.append((S("xt_full"), val(XT * l, e)))
            b = (k + 1) % 2
            gather_x(l, b, idxg[:, k:k + 1], f"gathered{b}", *free)
            if e != 0:
                y(prev(e))
        in_groups(pool, body)
        y(E - 1)

    def sp_load(pos, src, wait=None, inc_only=False):
        dst = ring[:, pos % NSLOT, 0:src.shape[1] * src.shape[2]].rearrange("p (k n) -> p k n", k=src.shape[1])
        if wait is not None:
            sp.wait_ge(*wait)
        sp.dma_start(dst, src).then_inc(S(f"w_ready{pos % NSLOT}"), 16)

    used = [("mod_full", i + 1) for i in range(FIRST)]
    used += [("in_full", n) for n in (4, 7, 11, 15, 19)]
    used += [("mod_full", i + 1) for i in range(FIRST, 2 * MODC)]
    used += [("out_full", 4), ("out_full", 8)]

    def used_by_moe(l):
        at = {}
        for e in range(E):
            for kind, sem in (("w1", "h1_full"), ("w3", "h3_full"), ("w2", "y_full")):
                at[position(l, kind, e)] = (sem, E * l + e + 1)
        return [at[p] for p in sorted(at)]

    used += used_by_moe(0)
    used += [("in_full", EVEN_FILLS + n) for n in (2, 6, 10, 14, 18, 20, 22)]
    used += [("out_full", 10), ("out_full", 12)]
    used += used_by_moe(1)

    def free_wait(pos):
        if pos < NSLOT:
            return None
        name, n = used[pos - NSLOT]
        return S(name), n

    def sp_before(l):
        if l == 0:
            for dst, src in FIRST_PARAMS:
                sp.dma_start(dst, src).then_inc(S("first_params"), 16)
        srcs, base = (before0, 0) if l == 0 else (before1, OD0)
        for i, (src, _) in enumerate(srcs):
            sp_load(base + i, src, free_wait(base + i))

    def sp_moe(l):
        def load(kind, e):
            if isinstance(e, int):
                pos = position(l, kind, e)
                sp_load(pos, expert_src(l, kind, e), free_wait(pos))
            else:
                pos = position(l, kind, e[0], looped=True)
                name, off = {"w1": ("y_full", -2), "w3": ("h1_full", 0), "w2": ("h3_full", 1)}[kind]
                sp.wait_ge(S(name), val(E * l, e, off))
                sp_load(pos, expert_src(l, kind, e[1] * GROUP + e[0]), (S("rows_ready"), l + 1))

        def body(e):
            load("w1", e)
            load("w3", e)
            if e != 0:
                load("w2", prev(e))
        in_groups(sp, body)
        load("w2", E - 1)

    def extra_rounds(eng, l, tiles, body, ahead=None):
        eng.wait_ge(S("rows_ready"), l + 1)
        longest = eng.value_load(flag[0:1, l:l + 1], min_val=0, max_val=TOK)
        with eng.If(longest > P):
            if ahead is not None:
                ahead()
            with eng.Fori(1, len(tiles)) as r:
                with eng.Fori(0, E) as e:
                    body(r, e, (r - 1) * E + e)
        eng.end_ifs()

    def extra(l, name):
        return S(f"extra_{name}{l}")

    XPOS = [MOE_BASE[l] + 3 * E for l in range(2)]

    def sp_extra(l, tiles):
        def ahead():
            sp.wait_ge(S("y_full"), E * (l + 1))

        def body(r, e, n):
            sp.wait_ge(S("rows_ready"), l + 1)
            sp.wait_ge(extra(l, "turn"), n + 1)
            for i, kind in enumerate(("w1", "w3", "w2")):
                src = expert_src(l, kind, e)
                dst = ring[:, (XPOS[l] + i) % NSLOT, :].rearrange("p (k n) -> p k n", k=src.shape[1])
                sp.dma_start(dst, src).then_inc(extra(l, "w"), 16)
            sp.wait_ge(S("rows_ready"), l + 1)
            sp.wait_ge(extra(l, "y"), n + 1)
        extra_rounds(sp, l, tiles, body, ahead)

    def pool_extra(l, tiles):
        def ahead():
            for b in range(2):
                pool.wait_ge(S(f"ystored{b}"), 16 * 8 * (l + 1))
                pool.wait_ge(S(f"gathered{b}"), 16 * (9 - b) * (l + 1))

        def body(r, e, n):
            pool.tensor_copy(idxg[:, 0:1], idx[:, bass.ds(r * E + e, 1)]).then_inc(extra(l, "turn"), 1)
            gather_x(l, 0, idxg[:, 0:1], f"extra_gathered{l}", (extra(l, "turn"), n + 1))
            pool.wait_ge(extra(l, "yout"), n + 1)
            pool.dma_start(ydram[l][bass.ds((r * E + e) * P, P), :], yb[0]).then_inc(extra(l, "stored"), 16)
            pool.wait_ge(extra(l, "stored"), n * 16 + 16)
        extra_rounds(pool, l, tiles, body, ahead)

    def pe_extra(l, tiles):
        def body(r, e, n):
            pe.wait_ge(extra(l, "gathered"), n * 16 + 16)
            for k in range(KD):
                mm = pe.transpose(psum[:, 4 + k // 4, P * (k % 4):P * (k % 4) + P], xg[0][:, P * k:P * k + P], ident)
            mm.then_inc(extra(l, "xt"), 1)
            pe.wait_ge(extra(l, "w"), n * 48 + 48)
            pe.wait_ge(extra(l, "xtout"), n + 1)
            for j in range(2):
                w = slot(XPOS[l] + j, 512)
                for k in range(KD):
                    mm = pe.matmul(bank(j), xT[0][:, k, :], w[:, k, :], start=k == 0, stop=k == KD - 1)
            mm.then_inc(extra(l, "h"), 1)
            pe.wait_ge(extra(l, "a"), n + 1)
            for k in range(KF):
                mm = pe.transpose(psum[:, 6, P * k:P * k + P], ah[0][:, P * k:P * k + P], ident)
            mm.then_inc(extra(l, "at"), 1)
            pe.wait_ge(extra(l, "atout"), n + 1)
            w = slot(XPOS[l] + 2, D, KF)
            for half in range(2):
                for k in range(KF):
                    mm = pe.matmul(bank(2 + half), aT[0][:, k, :], w[:, k, 512 * half:512 * half + 512], start=k == 0, stop=k == KF - 1)
            mm.then_inc(extra(l, "y"), 1)
        extra_rounds(pe, l, tiles, body, lambda: pe_drained(l))

    def pe_drained(l):
        pe.wait_ge(S("y_act"), E * (l + 1))
        pe.wait_ge(S("y_dve"), E * (l + 1))
        pe.wait_ge(S("xt_act"), XT * (l + 1))
        pe.wait_ge(S("xt_dve"), XT * (l + 1))

    def act_extra(l, tiles):
        def body(r, e, n):
            act.wait_ge(extra(l, "xt"), n + 1)
            act.activation(flat(xT[0][:, 0:4, :]), bank(4), ACT.Copy)
            act.activation(flat(xT[0][:, 4:8, :]), bank(5), ACT.Copy).then_inc(extra(l, "xtout"), 1)
            act.wait_ge(extra(l, "h"), n + 1)
            act.activation(sil[0], bank(0), ACT.Silu).then_inc(extra(l, "sil"), 1)
        extra_rounds(act, l, tiles, body)

    def dve_extra(l, tiles):
        def body(r, e, n):
            dve.wait_ge(extra(l, "sil"), n + 1)
            dve.tensor_tensor(ah[0], sil[0], bank(1), ALU.mult).then_inc(extra(l, "a"), 1)
            dve.wait_ge(extra(l, "at"), n + 1)
            dve.tensor_copy(flat(aT[0]), bank(6)).then_inc(extra(l, "atout"), 1)
            dve.wait_ge(extra(l, "y"), n + 1)
            dve.tensor_copy(yb[0][:, 0:512], bank(2))
            dve.tensor_copy(yb[0][:, 512:1024], bank(3)).then_inc(extra(l, "yout"), 1)
        extra_rounds(dve, l, tiles, body)

    def ybuf(j, i):
        return view(9216 + 1024 * (2 * j + i % 2), [D])

    COMB = [0, NT]

    def pool_combine(l, tiles):
        for b in range(2):
            pool.wait_ge(S(f"ystored{b}"), 16 * 8 * (l + 1))
        longest = pool.value_load(flag[0:1, l:l + 1], min_val=0, max_val=TOK)
        with pool.If(longest > P):
            pool_gather_y(l, tiles, ydram[l])
        with pool.Else():
            pool_gather_y(l, tiles, ydram[l][0:E * P, :])
        pool.end_ifs()

    def pool_gather_y(l, tiles, src):
        for i in range(len(tiles)):
            if i >= 2:
                pool.wait_ge(S("comb_done"), COMB[l] + i - 1)
            for j in range(2):
                pool.indirect_dma_start(ybuf(j, i), None, src, bass.IndirectOffsetOnAxis(ap=rowy[:, i, j:j + 1], axis=0)
                                        ).then_inc(S(f"yback{j}{i % 2}"), 16)

    def act_combine(l, tiles):
        for i in range(len(tiles)):
            act.wait_ge(*act_more(f"yback0{i % 2}", 16))
            act.activation(ybuf(0, i), ybuf(0, i), ACT.Copy, scale=gatew[:, i, 0:1]).then_inc(S("y1_scaled"), 1)

    def dve_combine(l, tiles):
        dve.wait_ge(S("grow_done"), GROW_AFTER[l][1])
        for i, t in enumerate(tiles):
            dve.wait_ge(*dve_more(f"yback1{i % 2}", 16))
            dve.wait_ge(*dve_more("y1_scaled"))
            y = ybuf(0, i)
            dve_step(dve.scalar_tensor_tensor(y, ybuf(1, i), gatew[:, i, 1:2], y, ALU.mult, ALU.add))
            dve_step(dve.tensor_tensor(y, y, grow[:, 0 if lat(t) else 1, :], ALU.mult))
            dve.tensor_tensor(xres[:, t, :], xres[:, t, :], y, ALU.add).then_inc(S("comb_done"), 1)
            dve.wait_ge(*dve_more("comb_done"))

    GROW_AFTER = [(4, 8), (10, 12)]
    ALL, LAT = list(range(NT)), [2, 3]

    with nc.Block() as block:
        @block.sync
        def _(eng):
            sp_before(0)
            sp_moe(0)
            sp_extra(0, ALL)
            sp_before(1)
            sp_moe(1)
            sp_extra(1, LAT)
            for i, t in enumerate(LAT):
                sp.wait_ge(S("comb_done"), NT + i + 1)
                sp.dma_start(out[0, P * i:P * i + P, :], xres[:, t, :]).then_inc(S("stored"), 16)
            sp.wait_ge(S("stored"), 32)

        @block.gpsimd
        def _(eng):
            pool_ssd()
            pool_out(ALL)
            pool_dispatch(0, ALL)
            pool_moe(0)
            pool_extra(0, ALL)
            pool_combine(0, ALL)
            pool_out(LAT)
            pool_dispatch(1, LAT)
            pool_moe(1)
            pool_extra(1, LAT)
            pool_combine(1, LAT)

        @block.scalar
        def _(eng):
            act_setup()
            for m in range(FIRST):
                act_mod(m)
            act_setup_rest()
            act_norm(0, 0, ALL, "params", PARAMS_IN)
            act.wait_ge(*act_more("raw_cleared"))
            act_in_even("xbc")
            act_conv()
            act_ssd_rows()
            act_in_even("kv", "q")
            act_rstd(10 * NT)
            act_in_even("z")
            act_ssd_prepare()
            act_ssd()
            act_ssd_out()
            act_att_prepare()
            act_att()
            act_grow((0, 1))
            act_norm(0, 1, ALL, "res_added", 8)
            act_router(0, ALL)
            act_moe(0)
            act_extra(0, ALL)
            act.wait_ge(S("out_done"), 8)
            act_grow((0, 1))
            act_combine(0, ALL)
            act_norm(1, 0, ALL, "comb_done", NT)
            act_in_odd()
            act_ml()
            act_ml_out()
            act.wait_ge(S("comb_done"), NT)
            act_grow((0,))
            act_norm(1, 1, LAT, "res_added", 12)
            act_router(1, LAT)
            act_moe(1)
            act_extra(1, LAT)
            act.wait_ge(S("out_done"), 12)
            act_grow((0,))
            act_combine(1, LAT)

        @block.vector
        def _(eng):
            dve_setup()
            for m in range(FIRST):
                dve_mod(m)
            dve_setup_rest()
            dve_mod_bias(0, 0, FIRST)
            dve_acol(0, 0)
            dve_router_setup()
            dve_norm(0, 0, ALL)
            dve_in_even()
            dve_ssd_rows()
            dve_qk_norm()
            dve_ssd_prepare()
            dve_ssd()
            dve_ssd_out()
            dve_att_prepare()
            dve_att()
            dve_mod_bias(0, FIRST, MODC)
            dve_mod_bias(1, 0, MODC)
            for l, which in ((0, 1), (1, 0), (1, 1)):
                dve_acol(l, which)
            dve_out(ALL, 0)
            dve_norm(0, 1, ALL)
            dve_router(0, ALL)
            dve_moe(0)
            dve_extra(0, ALL)
            dve_combine(0, ALL)
            dve_norm(1, 0, ALL)
            dve_in_odd()
            dve_ml_prepare()
            dve_ml()
            dve_ml_out()
            dve_out(LAT, 1)
            dve_norm(1, 1, LAT)
            dve_router(1, LAT)
            dve_moe(1)
            dve_extra(1, LAT)
            dve_combine(1, LAT)

        @block.tensor
        def _(eng):
            pe_setup()
            pe.wait_ge(S("spad_ready"), 1)
            for m in range(FIRST):
                pe_mod(m)
            pe_setup_rest()
            pe_norm(ALL)
            pe_in_even()
            pe_ssd_prepare()
            pe_ssd()
            pe_ssd_out()
            pe_att_prepare()
            pe_att()
            pe_grow(0, 0, (0, 1))
            pe_out(ALL, 5 + 2 * MODC)
            pe_norm(ALL)
            pe_router(0, ALL)
            pe_moe(0)
            pe_extra(0, ALL)
            pe_grow(0, 1, (0, 1))
            pe_norm(ALL)
            pe_in_odd()
            pe_ml_prepare()
            pe_ml()
            pe_ml_out()
            pe_grow(1, 0, (0,))
            pe_out(LAT, OD0 + 7)
            pe_norm(LAT)
            pe_router(1, LAT)
            pe_moe(1)
            pe_extra(1, LAT)
            pe_grow(1, 1, (0,))
    return len(sems)


def constants():
    f = np.zeros((P, 548), np.float32)
    f[:, 0:P] = np.eye(P)
    f[:, 128:144] = np.arange(E)
    f[:, 144:160] = E - np.arange(E)
    f[:, 160:164] = np.arange(P)[:, None] + P * np.arange(NT)
    f[:, 164:292] = 1.0
    n = 16
    inv = 10000.0 ** (-np.arange(n, dtype=np.float32) / n)
    pos = np.arange(STREAM)
    ang = np.concatenate([(pos // 64)[:, None] * inv, (pos // 64)[:, None] * inv,
                          (pos % 64)[:, None] * inv, (pos % 64)[:, None] * inv], axis=1).astype(np.float32)
    cos, sin = np.cos(ang), np.sin(ang)
    sin[:, 0:16] *= -1
    sin[:, 32:48] *= -1
    f[:, 292:420] = cos.reshape(2, P, 64).transpose(1, 0, 2).reshape(P, 128)
    f[:, 420:548] = sin.reshape(2, P, 64).transpose(1, 0, 2).reshape(P, 128)
    b = np.zeros((P, 2432), np.float32)
    i = np.arange(P)
    b[:, 0:P] = np.eye(P)
    b[:, P:2 * P] = 1.0
    b[:, 2 * P:3 * P] = i[:, None] < i[None, :]
    b[:, 384:896] = np.tile(np.where(i[:, None] > i[None, :], NEG, 0.0), (1, 4))
    b[:, 896:1408] = np.tile(np.where(i[:, None] < i[None, :], NEG, 0.0), (1, 4))
    for t in range(2):
        key = np.arange(STREAM)[None, :]
        far = np.abs(key - (P * t + i[:, None])) > P
        b[:, 1408 + 512 * t + 256:1408 + 512 * (t + 1)] = np.where(far, NEG, 0.0)
    return f, b.astype(mybir.dt.np(BF16))


INPUTS = ["x", "c", "ctx", "c_ctx", "router_w", "router_b", "norm_mix", "norm_ffn", "w_mod", "b_mod",
          "ev_w_in", "ev_conv_w", "ev_conv_b", "ev_dt_bias", "ev_a_log", "ev_d_skip", "ev_ssd_norm",
          "ev_q_norm", "ev_k_norm", "ev_sink", "ev_w_out",
          "od_w_in", "od_conv_w", "od_conv_b", "od_igate_b", "od_fgate_b", "od_head_norm", "od_w_out",
          "moe_w1", "moe_w3", "moe_w2"]


def kernel(**inputs):
    import concourse.bacc as bacc
    from concourse.bass_utils import run_bass_kernel_spmd

    nc = bacc.Bacc("TRN2", target_bir_lowering=False, num_devices=1)
    arrays, args = {}, []
    const_f, const_b = constants()
    for name, a in [(n, inputs[n]) for n in INPUTS] + [("const_f", const_f), ("const_b", const_b)]:
        a = np.ascontiguousarray(a)
        arrays[f"in_{name}"] = a
        args.append(nc.dram_tensor(f"in_{name}", a.shape, mybir.dt.from_np(a.dtype), kind="ExternalInput").ap())
    args.append(nc.dram_tensor("out_x", (1, STREAM, D), F32, kind="ExternalOutput").ap())
    hybrid_program(nc, *args)
    result = run_bass_kernel_spmd(nc, [arrays], core_ids=[0])
    return result.results[0]["out_x"]
```

```python
import concourse.bass as bass
from concourse import mybir
from concourse.alu_op_type import AluOpType as ALU
import numpy as np

F32 = mybir.dt.float32
BF16 = mybir.dt.bfloat16
U32 = mybir.dt.uint32
ACT = mybir.ActivationFunctionType
AX = mybir.AxisListType

P = 128
D = 1024
KD = D // P
NT = 4
TOK = NT * P
STREAM = 256
H = 8
DIR1 = 32
ROWS = DIR1 + H
EPS = 1e-6
NEG = -1e30
SSD_IN = 512
XBC = 768
EV_DT, EV_Q, EV_K = 1280, 1296, 1808
QKV = 768
OD_CONV = 2048
OD_GATES = 3072
DV = 128
VA = DV + 1
E = 16
FE = 512
KF = FE // P
RMAX = TOK // P
NCOL = RMAX * E
NSLOT = 4
GROUP = 4
MODC = 12


def lat(t):
    return t >= 2


def tile_of(step, d):
    return step if d == 0 else (1, 0, 3, 2)[step]


def hybrid_program(nc, x, c, ctx, c_ctx, router_w, router_b, norm_mix, norm_ffn, w_mod, b_mod,
                   ev_w_in, ev_conv_w, ev_conv_b, ev_dt_bias, ev_a_log, ev_d_skip, ev_ssd_norm,
                   ev_q_norm, ev_k_norm, ev_sink, ev_w_out,
                   od_w_in, od_conv_w, od_conv_b, od_igate_b, od_fgate_b, od_head_norm, od_w_out,
                   moe_w1, moe_w3, moe_w2, const_f, const_b, out):
    sems = {}

    def S(name):
        if name not in sems:
            sems[name] = nc.alloc_semaphore(name)
        return sems[name]

    def counter():
        seen = {}

        def more(name, k=1):
            seen[name] = seen.get(name, 0) + k
            return S(name), seen[name]
        return more

    def sb(name, shape, dt=F32):
        return nc.alloc_sbuf_tensor(name, shape, dt)

    ring = sb("ring", [P, NSLOT, 4096])
    xres = sb("xres", [P, NT, D])
    cf = sb("cf", [P, const_f.shape[1]])
    cb = sb("cb", [P, const_b.shape[1]], BF16)
    colsa = sb("colsa", [P, 72])
    colsb = sb("colsb", [P, 64])
    spad = sb("spad", [P, KD, 32])
    bcol = sb("bcol", [P, 4, 2 * MODC])
    modrow = sb("modrow", [P, 512])
    mcol = sb("mcol", [P, 2, 48, 2])
    acol = sb("acol", [P, 2, 2, 2, KD])
    rw = sb("rw", [P, KD, E])
    rbias = sb("rbias", [P, E])
    rowpar = sb("rowpar", [ROWS, 8])
    brd = sb("brd", [P, 8 + 8])
    ssdn = sb("ssdn", [P, SSD_IN])
    qkw = sb("qkw", [P, 10, 64])
    hnorm = sb("hnorm", [P, D])
    stat = sb("stat", [P, 64])
    stat2 = sb("stat2", [P, 3, 64])
    zrow = sb("zrow", [P, NCOL], U32)
    idx = sb("idx", [P, NCOL], U32)
    idxg = sb("idxg", [P, GROUP], U32)
    flag = sb("flag", [1, 2], U32)
    cnts = sb("cnts", [1, 2 * (E + 1)], U32)
    rt = sb("rt", [P, 816])
    rw32 = sb("rw32", [P, KD, 32])
    tok32 = sb("tok32", [P, NT], U32)
    maskb = sb("maskb", [P, NT, E], BF16)
    gatew = sb("gatew", [P, NT, 2])
    rowy = sb("rowy", [P, NT, 2], U32)
    rowi = sb("rowi", [P, NT, 2], U32)

    ident = cf[:, 0:P]
    eiota = cf[:, 128:144]
    edesc = cf[:, 144:160]
    tokid = cf[:, 160:164]
    ones = cf[:, 164:164 + P]
    cosb = cf[:, 292:292 + 128].rearrange("p (t n) -> p t n", t=2)
    sinb = cf[:, 420:420 + 128].rearrange("p (t n) -> p t n", t=2)
    identb = cb[:, 0:P]
    onesb = cb[:, P:2 * P]
    upper = cb[:, 2 * P:3 * P]
    decmask = [cb[:, 384 + 512 * d:384 + 512 * (d + 1)] for d in range(2)]
    iotab = cb[:, 2432:2432 + P]
    tokparts = cb[:, 2560:2560 + 2 * NT].rearrange("p (t a) -> p t a", t=NT)
    attmask = [cb[:, 1408 + 512 * i:1408 + 512 * (i + 1)] for i in range(2)]

    room = (nc.sbuf_bytes_remaining() if callable(nc.sbuf_bytes_remaining) else nc.sbuf_bytes_remaining) // 4
    AREA = room - 64
    arena = sb("arena", [P, AREA])

    def view(at, shape, dt=F32):
        n = int(np.prod(shape))
        assert at + n <= AREA, (at + n, AREA)
        v = arena[:, at:at + n]
        names = "abcd"[:len(shape)]
        if len(shape) == 1:
            return v
        return v.rearrange(f"p ({' '.join(names)}) -> p {' '.join(names)}", **dict(zip(names, shape)))

    hT = view(0, [KD, TOK])
    htok = view(4096, [NT, D])
    raw = view(4096, [6, 2, STREAM + 2])
    xbcT = view(8192, [6, TOK])
    zs = view(11264, [NT, SSD_IN])
    qkv = view(13312, [NT, QKV])
    xs = view(16384, [NT, SSD_IN])
    btok = view(18432, [NT, P])
    cbT = view(18944, [2, NT, P])
    sq = view(19968, [4, TOK])
    tq = view(22016, [4, TOK])
    cq = view(24064, [NT, 4, ROWS])
    catT = hT
    grow = view(18000, [2, D])
    ysum = view(4096, [NT, SSD_IN])
    xdt = [view(6144, [512]), view(0, [512])]
    xdd = [view(6656, [512]), view(512, [512])]
    wts = [view(19968 + 512 * i, [4, P]) for i in range(2)]
    sbd = [view(7168 + 512 * d, [512]) for d in range(2)]
    gtmp = view(4096 + 3200, [TOK])
    yoff = view(20992, [512])
    dg = view(21504, [4, ROWS])
    eb = view(21504 + 160, [4, ROWS])
    qT = view(4096, [4, TOK])
    kT2 = view(6144, [2, TOK])
    kdup = view(7168, [NT, 4, 64])
    ptb = [view(16384 + 2048 * i, [4, 2, 2, P]) for i in range(2)]
    pbuf = [view(20480 + 512 * i, [TOK]) for i in range(3)]
    att = view(23296, [4, NT * H])

    zeros = view(25136, [256])
    slot1 = view(8192, [512]).bitcast(BF16).rearrange("p (j t s) -> p j t s", j=2, t=NT)
    tokat = view(8704, [128]).bitcast(BF16).rearrange("p (j t a e) -> p j t a e", j=2, t=NT, a=2)

    hdram = [nc.dram_tensor(f"hdram{l}", [n, D], F32, kind="Internal").ap() for l, n in enumerate((TOK, STREAM))]
    ydram = [nc.dram_tensor(f"ydram{l}", [n * E, D], F32, kind="Internal").ap() for l, n in enumerate((TOK, STREAM))]
    table = [nc.dram_tensor(f"table{l}", [NCOL * P, 1], U32, kind="Internal").ap() for l in range(2)]

    psum = nc.alloc_psum_tensor("psum", [P, 8, 512], F32)

    def bank(b, n=512):
        return psum[:, b, 0:n]

    def cols(w, a, b):
        return w[:, a:b].rearrange("(k p) n -> p k n", p=P), (b - a) * KD

    def mod_src(l, ch):
        return cols(w_mod[l], 512 * ch, 512 * ch + 512)

    ev = ev_w_in[0]
    od = od_w_in[0]
    MODS = [(l, ch) for l in range(2) for ch in range(MODC)]
    FIRST = 4
    before0 = [mod_src(*m) for m in MODS[:FIRST]]
    before0 += [cols(ev, 512, 1024), cols(ev, 1024, EV_Q), cols(ev, EV_K, 2064), cols(ev, EV_Q, EV_K), cols(ev, 0, 512)]
    before0 += [mod_src(*m) for m in MODS[FIRST:]]
    before0 += [cols(ev_w_out[0], 512 * i, 512 * i + 512) for i in range(2)]
    before1 = [cols(od, OD_GATES, OD_GATES + 32)] + [cols(od, 512 * i, 512 * i + 512) for i in range(6)]
    before1 += [cols(od_w_out[0], 512 * i, 512 * i + 512) for i in range(2)]
    MOE_BASE = [len(before0), len(before0) + 3 * E + len(before1)]

    def slot(i, n, k=KD):
        return ring[:, i % NSLOT, 0:k * n].rearrange("p (k n) -> p k n", k=k)

    def expert_src(l, kind, e):
        w = {"w1": moe_w1, "w3": moe_w3, "w2": moe_w2}[kind][l]
        we = w[e] if isinstance(e, int) else w[bass.ds(e, 1)].rearrange("a d n -> (a d) n")
        return we.rearrange("(k p) n -> p k n", p=P)

    def position(l, kind, e, looped=False):
        if kind == "w2":
            return MOE_BASE[l] + (3 * E - 1 if e == E - 1 else 3 * e + 4)
        if e == 0 and not looped:
            return MOE_BASE[l] + (kind == "w3")
        return MOE_BASE[l] + 3 * e - 1 + (kind == "w3")

    IN_EVEN = [("xbc", b, "act") for b in range(6)] + [("dt", 0, "dve")] \
        + [(kind, t, "act") for kind in ("kv", "q", "z") for t in range(NT)]


    pe_more, act_more, dve_more, pool_more, sp_more = (counter() for _ in range(5))
    pe, act, dve, pool, sp = nc.tensor, nc.scalar, nc.vector, nc.gpsimd, nc.sync

    def dve_step(ins):
        ins.then_inc(S("dve_step"), 1)
        dve.wait_ge(*dve_more("dve_step"))

    def act_step(ins):
        ins.then_inc(S("act_step"), 1)
        act.wait_ge(*act_more("act_step"))

    def pool_step(ins):
        ins.then_inc(S("pool_step"), 1)
        pool.wait_ge(*pool_more("pool_step"))

    def weights_here(i):
        pe.wait_ge(S(f"w_ready{i % NSLOT}"), 16 * (i // NSLOT + 1))

    r1, r2, r3, rc = (view(P * j, [P]) for j in range(4))
    brow = view(4 * P, [512])
    FIRST_PARAMS = [
        (cf[:, :], const_f),
        (rc[0:8, :], c.rearrange("a (b n) -> (a b) n", n=P)),
        (rc[8:16, :], c_ctx.rearrange("(b n) -> b n", n=P)),
    ]
    PARAMS = [
        (cb[:, :], const_b),
        (r3[0:18, :], ev_conv_w[0].rearrange("t (b n) -> (t b) n", n=P)),
        (r3[18:24, :], ev_conv_b[0].rearrange("(b n) -> b n", n=P)),
        (r2[0:48, :], od_conv_w[0].rearrange("t (b n) -> (t b) n", n=P)),
        (r2[48:64, :], od_conv_b[0].rearrange("(b n) -> b n", n=P)),
    ]
    PARAMS += [
        (r1[0:16, :], norm_mix.rearrange("l (b n) -> (l b) n", n=P)),
        (r1[16:32, :], norm_ffn.rearrange("l (b n) -> (l b) n", n=P)),
        (brow[0:2 * MODC, :], b_mod.rearrange("l (c n) -> (l c) n", n=512)),
        (rw[:, :, :], router_w.rearrange("(k p) e -> p k e", p=P)),
        (rbias[:, :], router_b.partition_broadcast(P)),
        (brd[:, 0:8], ev_d_skip[0].partition_broadcast(P)),
        (brd[:, 8:16], ev_sink[0].partition_broadcast(P)),
        (ssdn[:, :], ev_ssd_norm[0].partition_broadcast(P)),
        (qkw[:, 0, :], ev_q_norm[0].partition_broadcast(P)),
        (qkw[:, 8, :], ev_k_norm[0].partition_broadcast(P)),
        (hnorm[:, :], od_head_norm[0].partition_broadcast(P)),
    ]
    TOKENS = [(xres[:, 0:2, :], ctx[0].rearrange("(t p) n -> p t n", p=P)),
              (xres[:, 2:4, :], x[0].rearrange("(t p) n -> p t n", p=P))]
    for d in range(2):
        for j, w in enumerate((ev_dt_bias, ev_a_log, od_igate_b, od_fgate_b)):
            PARAMS.append((rowpar[DIR1 * d:DIR1 * d + H, j:j + 1], w[0, d].unsqueeze(1)))
    PARAMS_IN = 16 * len(PARAMS)

    def act_setup():
        act.wait_ge(*act_more("cols_ready"))
        act.activation(stat2[:, 0, 0:16], colsa[:, 32:48], ACT.Exp, scale=-1.0).then_inc(S("c_exp"), 1)

    def act_setup_rest():
        act.wait_ge(S("params"), PARAMS_IN)
        act.activation(rowpar[:, 4:5], rowpar[:, 1:2], ACT.Exp).then_inc(S("c_exp"), 1)

    def pe_setup():
        pe.wait_ge(S("first_params"), 16 * len(FIRST_PARAMS))
        pe.transpose(psum[:, 0, 0:16], rc[0:16, :], ident[0:16, 0:16]).then_inc(S("cols_full"), 1)

    def pe_setup_rest():
        pe.wait_ge(S("params"), PARAMS_IN)
        pe.transpose(psum[:, 4, 0:32], r1[0:32, :], ident[0:32, 0:32])
        pe.transpose(psum[:, 4, 32:56], r3[0:24, :], ident[0:24, 0:24])
        pe.transpose(psum[:, 5, 0:64], r2[0:64, :], ident[0:64, 0:64])
        for b in range(4):
            mm = pe.transpose(psum[:, 5, P + 2 * MODC * b:P + 2 * MODC * (b + 1)], brow[0:2 * MODC, P * b:P * b + P],
                              ident[0:2 * MODC, 0:2 * MODC])
        mm.then_inc(S("cols_full"), 1)

    def dve_setup():
        dve_step(dve.memset(spad[:], 0.0))
        dve.memset(rowpar[:], 0.0).then_inc(S("zeroed"), 1)
        dve.wait_ge(*dve_more("cols_full"))
        dve.tensor_copy(colsa[:, 32:48], psum[:, 0, 0:16]).then_inc(S("cols_ready"), 1)
        dve.wait_ge(*dve_more("cols_ready"))
        dve.wait_ge(*dve_more("c_exp"))
        dve_step(dve.tensor_scalar(stat2[:, 0, 0:16], stat2[:, 0, 0:16], 1.0, None, ALU.add))
        dve_step(dve.reciprocal(stat2[:, 1, 0:16], stat2[:, 0, 0:16]))
        dve.tensor_tensor(spad[:, :, 0:2].rearrange("p k s -> p s k"), stat2[:, 1, 0:16].rearrange("p (s k) -> p s k", s=2),
                          colsa[:, 32:48].rearrange("p (s k) -> p s k", s=2), ALU.mult).then_inc(S("spad_ready"), 1)

    def dve_setup_rest():
        dve.wait_ge(*dve_more("cols_full"))
        dve_step(dve.tensor_copy(bcol[:], psum[:, 5, P:P + 8 * MODC].rearrange("p (b n) -> p b n", b=4)))
        dve_step(dve.tensor_copy(colsb[:], psum[:, 5, 0:64]))
        dve_step(dve.tensor_copy(colsa[:, 48:72], psum[:, 4, 32:56]))
        dve.tensor_copy(colsa[:, 0:32], psum[:, 4, 0:32]).then_inc(S("cols_ready"), 1)
        dve.wait_ge(*dve_more("cols_ready"))
        dve.wait_ge(*dve_more("c_exp"))
        dve_step(dve.tensor_scalar(rowpar[:, 4:5], rowpar[:, 4:5], -1.0, None, ALU.mult))
        dve_step(dve.tensor_scalar(qkw[:, 1:8, :], qkw[:, 0:1, :].broadcast_to([P, 7, 64]), 1.0, None, ALU.mult))
        dve_step(dve.tensor_scalar(qkw[:, 9, :], qkw[:, 8, :], 1.0, None, ALU.mult))

    def mod_pos(m):
        return m if m < FIRST else m + 5

    def pe_mod_rows(m):
        weights_here(mod_pos(m))
        w = slot(mod_pos(m), 512)
        for k in range(KD):
            j = 32 * (k % 4)
            mm = pe.matmul(psum[j:j + 32, 7, :], spad[:, k, :], w[:, k, :], start=k < 4, stop=k >= 4)
        mm.then_inc(S("mod_full"), 1)

    def pe_mod_cols(m):
        pe.wait_ge(*pe_more("modrow_ready"))
        if m > 0:
            pe.wait_ge(*pe_more("mcol_done"))
        for b in range(4):
            mm = pe.transpose(psum[:, 6, P * b:P * b + P], modrow[:, P * b:P * b + P], ident)
        mm.then_inc(S("modcol_full"), 1)

    def pe_mod(m):
        pe_mod_rows(m)
        pe_mod_cols(m)

    def act_mod(m):
        act.wait_ge(*act_more("mod_full"))
        if m > 0:
            act.wait_ge(*act_more("modcol_full"))
        act.activation(modrow[:], bank(7), ACT.Copy).then_inc(S("modrow_ready"), 1)

    def dve_mod(m):
        l, ch = MODS[m]
        dve.wait_ge(*dve_more("modcol_full"))
        dve.tensor_reduce(mcol[:, l, 4 * ch:4 * ch + 4, :],
                          bank(6).rearrange("p (b g r) -> p b r g", b=4, g=4)[:, :, 0:2, :], AX.X, ALU.add
                          ).then_inc(S("mcol_done"), 1)

    def dve_mod_bias(l, a, b):
        dve.wait_ge(S("mcol_done"), MODC * l + b)
        v = mcol[:, l, 4 * a:4 * b, :].rearrange("p (n b) s -> p b n s", b=4)
        v2 = bcol[:, :, MODC * l + a:MODC * l + b]
        for s_ in range(2):
            dve.tensor_tensor(v[:, :, :, s_], v[:, :, :, s_], v2, ALU.add).then_inc(S("mod_done"), 1)
        dve.wait_ge(*dve_more("mod_done", 2))

    ACOL_AFTER = {(0, 0): 2, (0, 1): 4, (1, 0): 6, (1, 1): 8}

    def dve_acol(l, which):
        blk = 32 if which else 8
        for s in range(2):
            dve.scalar_tensor_tensor(acol[:, l, which, s, :], mcol[:, l, blk:blk + KD, s], 1.0,
                                     colsa[:, 16 * which + 8 * l:16 * which + 8 * l + KD], ALU.add, ALU.mult
                                     ).then_inc(S("acol_ready"), 1)

    def dve_rstd(n, width):
        v, y, t = (stat2[:, j, 0:n] for j in range(3))
        dve.tensor_scalar(v, stat[:, 0:n], 1.0 / width, EPS, ALU.mult, ALU.add).then_inc(S("var_ready"), 1)
        dve.wait_ge(*dve_more("rstd_guess"))
        dve_step(dve.reciprocal(y, y))
        dve_step(dve.tensor_tensor(t, y, y, ALU.mult))
        dve_step(dve.tensor_tensor(t, t, v, ALU.mult))
        dve_step(dve.tensor_scalar(t, t, -0.5, 1.5, ALU.mult, ALU.add))
        dve_step(dve.tensor_tensor(y, y, t, ALU.mult))

    def act_rstd(n):
        v, y = stat2[:, 0, 0:n], stat2[:, 1, 0:n]
        act.wait_ge(*act_more("var_ready"))
        act.activation(y, v, ACT.Sqrt).then_inc(S("rstd_guess"), 1)

    def act_norm(l, which, tiles, ready, value):
        act_norm_sums(tiles, ready, value)
        act_norm_rows(l, which, tiles)

    def act_norm_sums(tiles, ready, value):
        for n, t in enumerate(tiles):
            act.wait_ge(S(ready), value if ready == "tokens_in" else value - len(tiles) + n + 1)
            act.activation(htok[:, t, :], xres[:, t, :], ACT.Square, accum_out=stat[:, n:n + 1]
                           ).then_inc(S("sum_ready"), 1)
        act_rstd(len(tiles))

    def act_norm_rows(l, which, tiles):
        act.wait_ge(S("acol_ready"), ACOL_AFTER[l, which])
        for k in range(0, KD, 2):
            act_evac_ht(l, which, tiles, k)
        act_more("ht_full", 1)

    def ht_halves(l, which, tiles, k):
        shift = 24 * which + k
        n0 = 0
        for s, ts in ((1, [t for t in tiles if not lat(t)]), (0, [t for t in tiles if lat(t)])):
            if ts:
                n = P * len(ts)
                yield (hT[:, k, P * ts[0]:P * ts[0] + n], psum[:, k % 4, n0:n0 + n],
                       acol[:, l, which, s, k:k + 1], mcol[:, l, shift, s:s + 1])
                n0 += n

    def act_evac_ht(l, which, tiles, k):
        act.wait_ge(*act_more("ht_full", 1 if k == 0 else 2))
        for dst, src, a, b in ht_halves(l, which, tiles, k):
            last = act.activation(dst, src, ACT.Identity, bias=b, scale=a)
        last.then_inc(S("ht_act"), 1)

    def dve_norm(l, which, tiles):
        dve_norm_scale(tiles)
        dve_norm_rows(l, which, tiles)

    def dve_norm_scale(tiles):
        dve.wait_ge(*dve_more("sum_ready", len(tiles)))
        dve_rstd(len(tiles), D)
        for n, t in enumerate(tiles):
            dve.tensor_scalar(htok[:, t, :], xres[:, t, :], stat2[:, 1, n:n + 1], None, ALU.mult
                              ).then_inc(S("xn_ready"), 1)

    def dve_norm_rows(l, which, tiles):
        dve.wait_ge(S("acol_ready"), ACOL_AFTER[l, which])
        for k in range(1, KD, 2):
            dve.wait_ge(*dve_more("ht_full", 2))
            for dst, src, a, b in ht_halves(l, which, tiles, k):
                last = dve.tensor_scalar(dst, src, a, b, ALU.mult, ALU.add)
            last.then_inc(S("ht_dve"), 1)

    def pe_norm(tiles):
        pe.wait_ge(*pe_more("xn_ready", len(tiles)))
        for k in range(KD):
            if k >= 4:
                pe.wait_ge(*pe_more("ht_act" if k % 2 == 0 else "ht_dve"))
            for n, t in enumerate(tiles):
                mm = pe.transpose(psum[:, k % 4, P * n:P * n + P], htok[:, t, P * k:P * k + P], ident)
            mm.then_inc(S("ht_full"), 1)
        pe.wait_ge(*pe_more("ht_act", 2))
        pe.wait_ge(*pe_more("ht_dve", 2))

    EV0 = FIRST

    def pe_gates(bk, w, c0):
        for k in range(KD):
            pe.matmul(psum[0:H, bk, :], w[:, k, c0:c0 + H], hT[:, k, :], start=k == 0, stop=k == KD - 1)
            mm = pe.matmul(psum[DIR1:ROWS, bk, :].rearrange("p (s n) -> p s n", s=2), w[:, k, c0 + H:c0 + 2 * H],
                           hT[:, k, :].rearrange("p (s n) -> p s n", s=2)[:, :, ::-1], start=k == 0, stop=k == KD - 1)
        return mm

    def pe_in_even():
        done, at = [], None
        for i, (kind, b, who) in enumerate(IN_EVEN):
            if i >= 6:
                pe.wait_ge(*pe_more(f"in_{done[i - 6]}"))
            done.append(who)
            bk = i % 6
            pos = EV0 + {"xbc": b // 4, "dt": 1, "kv": 2, "q": 3, "z": 4}[kind]
            if pos != at:
                weights_here(pos)
                at = pos
            if kind == "xbc":
                w = slot(pos, 512 if b < 4 else 272)
                for k in range(KD):
                    mm = pe.matmul(bank(bk), w[:, k, P * (b % 4):P * (b % 4) + P], hT[:, k, :], start=k == 0, stop=k == KD - 1)
            elif kind == "dt":
                w = slot(pos, 272)
                mm = pe_gates(bk, w, 256)
            else:
                n = 256 if kind == "kv" else 512
                w = slot(pos, n)
                for k in range(KD):
                    mm = pe.matmul(bank(bk, n), hT[:, k, P * b:P * b + P], w[:, k, :], start=k == 0, stop=k == KD - 1)
            mm.then_inc(S("in_full"), 1)
        for who in done[-6:]:
            pe.wait_ge(*pe_more(f"in_{who}"))

    def act_in_even(*kinds):
        for i, (kind, b, who) in enumerate(IN_EVEN):
            if kind not in kinds:
                continue
            act.wait_ge(S("in_full"), i + 1)
            src = bank(i % 6)
            if kind == "xbc":
                ins = act.activation(raw[:, b, :, 1:STREAM + 1], src.rearrange("p (s n) -> p s n", s=2), ACT.Copy)
            elif kind == "kv":
                ins = act.activation(qkv[:, b, 512:QKV], src[:, 0:256], ACT.Copy)
            elif kind == "q":
                ins = act.activation(qkv[:, b, 0:512], src, ACT.Copy)
            else:
                ins = act.activation(zs[:, b, :], src, ACT.Silu)
            ins.then_inc(S("in_act"), 1)

    def act_conv():
        for b in range(6):
            act.wait_ge(*act_more("conv_ready"))
            act.activation(xbcT[:, b, :], xbcT[:, b, :], ACT.Silu).then_inc(S("conv_done"), 1)

    def dve_conv(dst, src, wcol, bcol):
        dst = dst.rearrange("p (s n) -> p s n", s=src.shape[1])
        dve_step(dve.tensor_scalar(dst, src[:, :, 0:STREAM], wcol(0), bcol, ALU.mult, ALU.add))
        dve_step(dve.scalar_tensor_tensor(dst, src[:, :, 1:STREAM + 1], wcol(1), dst, ALU.mult, ALU.add))
        dve.scalar_tensor_tensor(dst, src[:, :, 2:STREAM + 2], wcol(2), dst, ALU.mult, ALU.add
                                 ).then_inc(S("conv_ready"), 1)

    def dve_in_even():
        for side in (0, STREAM + 1):
            dve_step(dve.memset(raw[:, :, :, side:side + 1], 0.0))
        dve.memset(sq[0:ROWS, :, :], 0.0).then_inc(S("raw_cleared"), 1)
        for b in range(6):
            dve.wait_ge(*dve_more("in_act"))
            dve_conv(xbcT[:, b, :], raw[:, b, :, :], lambda j, b=b: colsa[:, 48 + 6 * j + b:49 + 6 * j + b],
                     colsa[:, 66 + b:67 + b])
        dve.wait_ge(S("in_full"), 7)
        dve.wait_ge(S("raw_cleared"), 1)
        dve_step(dve.tensor_scalar(sq[0:H, 0, :], psum[0:H, 0, :], rowpar[0:H, 0:1], None, ALU.add))
        dve.tensor_scalar(sq[DIR1:ROWS, 0, :], psum[DIR1:ROWS, 0, :], rowpar[DIR1:ROWS, 0:1], None, ALU.add
                          ).then_inc(S("in_dve"), 1)

    qn = view(16384, [10, 64])

    def dve_qk_norm():
        def qk_of(t):
            return qkv[:, t, 0:640].rearrange("p (h n) -> p h n", h=10)

        dve.wait_ge(S("in_act"), 14)
        for t in range(NT):
            dve_step(dve.tensor_tensor(qn, qk_of(t), qk_of(t), ALU.mult))
            dve_step(dve.tensor_reduce(stat[:, 10 * t:10 * t + 10], qn, AX.X, ALU.add))
        dve_rstd(10 * NT, 64)
        for t in range(NT):
            qk = qk_of(t)
            dve_step(dve.tensor_tensor(qk, qk, stat2[:, 1, 10 * t:10 * t + 10].unsqueeze(2).broadcast_to([P, 10, 64]), ALU.mult))
            dve_step(dve.tensor_tensor(qk, qk, qkw[:], ALU.mult))
            if lat(t):
                v = qk.rearrange("p h (a b n) -> p (h a) b n", a=2, b=2)
                sw = qn.rearrange("p h (a b n) -> p (h a) b n", a=2, b=2)
                for o in range(2):
                    dve_step(dve.tensor_copy(sw[:, :, o, :], v[:, :, 1 - o, :]))
                dve_step(dve.tensor_tensor(qn, qn, sinb[:, t - 2, :].unsqueeze(1).broadcast_to([P, 10, 64]), ALU.mult))
                dve_step(dve.tensor_tensor(qk, qk, cosb[:, t - 2, :].unsqueeze(1).broadcast_to([P, 10, 64]), ALU.mult))
                dve_step(dve.tensor_tensor(qk, qk, qn, ALU.add))
        dve.tensor_copy(stat[:, 0:1], stat2[:, 1, 0:1]).then_inc(S("qk_normed"), 1)

    def dve_log1p_abs(x, e):
        dve_step(dve.tensor_scalar(e, x, -1.0, None, ALU.mult))
        dve.tensor_tensor(e, e, x, ALU.max).then_inc(S("row_dve"), 1)

    def dve_log1p_sum(e, w, d, t):
        dve.wait_ge(*dve_more("row_act"))
        dve_step(dve.tensor_scalar(w, e, 1.0, None, ALU.add))
        dve_step(dve.tensor_scalar(d, w, -1.0, None, ALU.add))
        dve.tensor_scalar(t, d, 1e-30, None, ALU.max).then_inc(S("row_dve"), 1)

    def dve_log1p_end(e, w, d, t):
        dve.wait_ge(*dve_more("row_act"))
        dve_step(dve.reciprocal(t, t))
        dve_step(dve.tensor_tensor(w, w, t, ALU.mult))
        dve_step(dve.tensor_tensor(w, w, e, ALU.mult))
        dve_step(dve.scalar_tensor_tensor(d, d, 0.0, e, ALU.is_equal, ALU.mult))
        dve_step(dve.tensor_tensor(w, w, d, ALU.add))

    def act_log1p_exp(e):
        act.wait_ge(*act_more("row_dve"))
        act.activation(e, e, ACT.Exp, scale=-1.0).then_inc(S("row_act"), 1)

    def act_log1p_ln(w):
        act.wait_ge(*act_more("row_dve"))
        act.activation(w, w, ACT.Ln).then_inc(S("row_act"), 1)

    def rows(a, q):
        return a[0:ROWS, q, :]

    def dve_true_order(dst, src, nq):
        dve_step(dve.tensor_copy(dst[0:DIR1, 0:nq, :], src[0:DIR1, 0:nq, :]))
        for q in range(nq):
            last = dve.tensor_copy(dst[DIR1:ROWS, q, :].rearrange("p (s n) -> p s n", s=2),
                                   src[DIR1:ROWS, q, :].rearrange("p (s n) -> p s n", s=2)[:, :, ::-1])
            dve_step(last) if q < nq - 1 else last.then_inc(S("tq_ready"), 1)
        dve.wait_ge(*dve_more("tq_ready"))

    TOT = stat[0:ROWS, 8:12]
    ETOT = stat[0:ROWS, 12:16]

    def dve_ssd_rows():
        x0, e, w, d_ = (rows(sq, q) for q in range(4))
        dve.wait_ge(S("in_dve"), 1)
        dve_log1p_abs(x0, e)
        dve_log1p_sum(e, w, d_, gtmp[0:ROWS, :])
        dve_log1p_end(e, w, d_, gtmp[0:ROWS, :])
        dve_step(dve.scalar_tensor_tensor(w, x0, 0.0, w, ALU.max, ALU.add))
        dve_step(dve.tensor_scalar(e, w, rowpar[:, 4:5], None, ALU.mult))
        for st in range(4):
            dve_step(dve.tensor_tensor_scan(x0[:, P * st:P * st + P], ones[0:ROWS, :], e[:, P * st:P * st + P],
                                            0.0, ALU.mult, ALU.add))
        dve.tensor_copy(TOT, x0.rearrange("p (s n) -> p s n", s=4)[:, :, P - 1]).then_inc(S("row_dve"), 1)
        dve.wait_ge(*dve_more("row_act"))
        dve_step(dve.tensor_tensor(d_, d_, w, ALU.mult))
        dve_true_order(tq, sq, 4)
        dve.tensor_tensor(dg[0:ROWS, :, :], ETOT.unsqueeze(2).broadcast_to([ROWS, 4, ROWS]),
                          ident[0:ROWS, 0:ROWS].unsqueeze(1).broadcast_to([ROWS, 4, ROWS]), ALU.mult
                          ).then_inc(S("dg_ready"), 1)

    def act_ssd_rows():
        x0, e, w, d_ = (rows(sq, q) for q in range(4))
        act_log1p_exp(e)
        act_log1p_ln(w)
        act.wait_ge(*act_more("row_dve"))
        act.activation(e, x0, ACT.Exp)
        for st in range(4):
            act.activation(d_[:, P * st:P * st + P], x0[:, P * st:P * st + P], ACT.Exp, scale=-1.0, bias=TOT[:, st:st + 1])
        act.activation(ETOT, TOT, ACT.Exp).then_inc(S("row_act"), 1)

    def pe_ssd_prepare():
        pe.wait_ge(*pe_more("conv_done", 6))
        for t in range(NT):
            for b in range(4):
                mm = pe.transpose(psum[:, t, P * b:P * b + P], xbcT[:, b, P * t:P * t + P], ident)
            mm.then_inc(S("pre_full"), 1)
        for t in range(NT):
            mm = pe.transpose(psum[:, 4, P * t:P * t + P], xbcT[:, 4, P * t:P * t + P], ident)
        mm.then_inc(S("pre_full"), 1)
        for g in range(2):
            if g:
                pe.wait_ge(*pe_more("xs_ready", 1))
            for t in range(NT):
                mm = pe.matmul(psum[:, 0 if g else 5, P * t:P * t + P], xbcT[64 * g:64 * g + 64, 4, P * t:P * t + P],
                               xbcT[64 * g:64 * g + 64, 5, P * t:P * t + P], start=True, stop=True)
            mm.then_inc(S("pre_full"), 1)
        pe.wait_ge(*pe_more("xs_ready", 3))
        pe.wait_ge(*pe_more("tq_ready"))
        for t in range(NT):
            for q in range(4):
                mm = pe.transpose(psum[:, 1 + t // 2, 160 * (t % 2) + ROWS * q:160 * (t % 2) + ROWS * (q + 1)],
                                  tq[0:ROWS, q, P * t:P * t + P], ident[0:ROWS, 0:ROWS])
            if t % 2:
                mm.then_inc(S("pre_full"), 1)
        pe.wait_ge(*pe_more("dg_ready"))
        pe.matmul(bank(3, 4 * ROWS), ones[0:ROWS, :], dg[0:ROWS, :, :].rearrange("p s r -> p (s r)"), start=True, stop=True
                  ).then_inc(S("pre_full"), 1)

    def act_ssd_prepare():
        act.wait_ge(S("qk_normed"), 1)
        for t in range(NT):
            act.wait_ge(*act_more("pre_full"))
            act.activation(xs[:, t, :], bank(t), ACT.Copy).then_inc(S("xs_ready"), 1)
        act.wait_ge(*act_more("pre_full", 6))
        act.activation(eb.rearrange("p s r -> p (s r)"), bank(3, 4 * ROWS), ACT.Copy).then_inc(S("xs_ready"), 1)

    def dve_ssd_prepare():
        dve_step(dve.memset(sbd[0], 0.0))
        dve.wait_ge(*dve_more("pre_full", 5))
        dve_step(dve.tensor_copy(btok.rearrange("p t n -> p (t n)"), bank(4)))
        dve.wait_ge(*dve_more("pre_full", 1))
        dve_step(dve.tensor_copy(cbT[:, 0].rearrange("p t n -> p (t n)"), bank(5)))
        dve.wait_ge(*dve_more("pre_full", 1))
        dve_step(dve.tensor_copy(cbT[:, 1].rearrange("p t n -> p (t n)"), bank(0)))
        for j in range(2):
            dve.wait_ge(*dve_more("pre_full"))
            dve_step(dve.tensor_copy(cq[:, 2 * j:2 * j + 2].rearrange("p t q r -> p (t q r)"), bank(1 + j, 320)))
        dve.wait_ge(*dve_more("pre_full", 1))
        dve.wait_ge(S("xs_ready"), 5)
        dve.memset(sbd[1], 0.0).then_inc(S("ssd_prepared"), 1)
        dve.wait_ge(S("ssd_prepared"), 1)
        dve_step(dve.tensor_tensor(ysum.rearrange("p t (h n) -> p t h n", h=H), xs.rearrange("p t (h n) -> p t h n", h=H),
                          brd[:, 0:8].unsqueeze(1).unsqueeze(3).broadcast_to([P, NT, H, 64]), ALU.mult))

    SSD_ITER = [(st, d) for st in range(4) for d in range(2)]

    def colq(t, q, d):
        return cq[:, t, q, DIR1 * d:DIR1 * d + H].unsqueeze(2).broadcast_to([P, H, 64])

    def heads(v):
        return v.rearrange("p (h n) -> p h n", h=H)

    SSD_MODS = [1] * 8
    SSD_MOD0 = [FIRST + sum(SSD_MODS[:i]) for i in range(8)]
    OUT_MOD = FIRST + sum(SSD_MODS)
    ATT = [(t, h) for t in range(NT) for h in range(H)]
    ATT_LEFT = 2 * MODC - OUT_MOD - 1
    ATT_MOD = {(len(ATT) // ATT_LEFT) * (j + 1) - 1: OUT_MOD + 1 + j for j in range(ATT_LEFT)}

    def pe_ssd():
        pe.wait_ge(S("ssd_prepared"), 1)
        for i, (st, d) in enumerate(SSD_ITER):
            t = tile_of(st, d)
            if st > 0:
                pe.wait_ge(S("state_done"), i - 1)
                if st > 1 or d > 0:
                    pe.wait_ge(S("yoff_done"), i - 2)
                pe.matmul(bank(3), xbcT[:, 5, P * t:P * t + P], sbd[d], start=True, stop=True).then_inc(S("yoff_full"), 1)
            pe.wait_ge(*pe_more("xdt_ready"))
            if st < 3:
                if i:
                    pe.wait_ge(S("state_done"), i)
                pe.matmul(bank(4), btok[:, t, :], xdd[i % 2], start=True, stop=True).then_inc(S("state_full"), 1)
            for g in range(2):
                if i:
                    pe.wait_ge(*pe_more("arg_ready"))
                pe.matmul(bank(g), identb, decmask[d], start=True, stop=False)
                for h in range(4):
                    r = DIR1 * d + 4 * g + h
                    mm = pe.matmul(psum[:, g, P * h:P * h + P], ident[0:ROWS, r:r + 1].broadcast_to([ROWS, P]),
                                   tq[0:ROWS, 0, P * t:P * t + P], start=False, stop=h == 3)
                mm.then_inc(S("dec_full"), 1)
            pe_mod_rows(SSD_MOD0[i])
            pe_mod_cols(SSD_MOD0[i])
            if SSD_MODS[i] > 1:
                pe_mod_rows(SSD_MOD0[i] + 1)
            if i:
                pe.wait_ge(*pe_more("ydiag_done"))
            for g in range(2):
                pe.wait_ge(*pe_more("wts_ready"))
                for h in range(4):
                    hh = 4 * g + h
                    mm = pe.matmul(psum[:, 2, 64 * hh:64 * hh + 64], wts[g][:, h, :], xdt[i % 2][:, 64 * hh:64 * hh + 64],
                                   start=True, stop=True)
            mm.then_inc(S("ydiag_full"), 1)
            if SSD_MODS[i] > 1:
                pe_mod_cols(SSD_MOD0[i] + 1)

    def pool_ssd():
        pool.wait_ge(S("ssd_prepared"), 1)
        for i, (st, d) in enumerate(SSD_ITER):
            t = tile_of(st, d)
            if i >= 2:
                pool.wait_ge(*pool_more("ydiag_full"))
            pool_step(pool.tensor_tensor(heads(xdd[i % 2]), heads(xs[:, t, :]), colq(t, 3, d), ALU.mult))
            pool.tensor_tensor(heads(xdt[i % 2]), heads(xs[:, t, :]), colq(t, 2, d), ALU.mult).then_inc(S("xdt_ready"), 1)

    def act_ssd():
        for i in range(8):
            for g in range(2):
                act.wait_ge(*act_more("arg_ready"))
                act.activation(wts[g], wts[g], ACT.Exp).then_inc(S("exp_ready"), 1)
            for j in range(SSD_MODS[i]):
                act_mod(SSD_MOD0[i] + j)

    def dve_ssd():
        for i, (st, d) in enumerate(SSD_ITER):
            t = tile_of(st, d)
            if st > 0:
                dve.wait_ge(*dve_more("yoff_full"))
                dve.tensor_tensor(heads(yoff), heads(bank(3)), colq(t, 1, d), ALU.mult).then_inc(S("yoff_done"), 1)
                dve.wait_ge(*dve_more("yoff_done"))
                dve_step(dve.tensor_tensor(ysum[:, t, :], ysum[:, t, :], yoff, ALU.add))
            if st < 3:
                dve.wait_ge(*dve_more("state_full"))
                for g in range(2):
                    a = slice(64 * g, 64 * g + 64)
                    v = sbd[d][a, 256 * g:256 * g + 256]
                    col = DIR1 * d + 4 * g
                    dve_step(dve.tensor_tensor(v.rearrange("p (h n) -> p h n", h=4), v.rearrange("p (h n) -> p h n", h=4),
                                               eb[a, st, col:col + 4].unsqueeze(2).broadcast_to([64, 4, 64]), ALU.mult))
                    last = dve.tensor_tensor(v, v, psum[a, 4, 256 * g:256 * g + 256], ALU.add)
                    dve_step(last) if g == 0 else last.then_inc(S("state_done"), 1)
            for g in range(2):
                dve.wait_ge(*dve_more("dec_full"))
                if i and g == 0:
                    dve.wait_ge(S("ydiag_full"), i)
                dve.tensor_tensor(wts[g], bank(g).rearrange("p (h n) -> p h n", h=4),
                                  cq[:, t, 0, DIR1 * d + 4 * g:DIR1 * d + 4 * g + 4].unsqueeze(2).broadcast_to([P, 4, P]),
                                  ALU.subtract).then_inc(S("arg_ready"), 1)
            for g in range(2):
                dve.wait_ge(*dve_more("exp_ready"))
                dve.tensor_tensor(wts[g], wts[g], cbT[:, g, t, :].unsqueeze(1).broadcast_to([P, 4, P]), ALU.mult
                                  ).then_inc(S("wts_ready"), 1)
            dve_mod(SSD_MOD0[i])
            dve.wait_ge(*dve_more("ydiag_full"))
            dve.tensor_tensor(ysum[:, t, :], ysum[:, t, :], bank(2), ALU.add).then_inc(S("ydiag_done"), 1)
            if SSD_MODS[i] > 1:
                dve_mod(SSD_MOD0[i] + 1)
            dve.wait_ge(*dve_more("ydiag_done"))

    def dve_ssd_out():
        dve.wait_ge(S("in_act"), 18)
        for t in range(NT):
            dve.tensor_tensor(ysum[:, t, :], ysum[:, t, :], zs[:, t, :], ALU.mult).then_inc(S("yz_ready"), 1)
        dve_mod(OUT_MOD)
        dve.wait_ge(*dve_more("sum_ready", NT))
        dve_rstd(NT, SSD_IN)
        for t in range(NT):
            dve.scalar_tensor_tensor(ysum[:, t, :], ysum[:, t, :], stat2[:, 1, t:t + 1], ssdn[:], ALU.mult, ALU.mult
                                     ).then_inc(S("cat_ready"), 1)

    def act_ssd_out():
        for t in range(NT):
            act.wait_ge(*act_more("yz_ready"))
            act.activation(zs[:, t, :], ysum[:, t, :], ACT.Square, accum_out=stat[:, t:t + 1]).then_inc(S("sum_ready"), 1)
        act_mod(OUT_MOD)
        act_rstd(NT)
        for t in range(NT):
            act.wait_ge(*act_more("cat_full"))
            act.activation(catT[:, 0:4, P * t:P * t + P], bank(t).rearrange("p (b n) -> p b n", b=4), ACT.Copy
                           ).then_inc(S("cat_act"), 1)

    def pe_ssd_out():
        pe.wait_ge(*pe_more("arg_ready", 2))
        pe.wait_ge(*pe_more("ydiag_done"))
        pe.wait_ge(S("yoff_done"), 6)
        pe_mod(OUT_MOD)
        for t in range(NT):
            pe.wait_ge(*pe_more("cat_ready"))
            for b in range(4):
                mm = pe.transpose(psum[:, t, P * b:P * b + P], ysum[:, t, P * b:P * b + P], ident)
            mm.then_inc(S("cat_full"), 1)
        pe.wait_ge(*pe_more("cat_act", NT))

    NM, RSUM, ESINK, RDEN = (att[:, j, :] for j in range(4))

    def dve_att_prepare():
        dve.wait_ge(S("cat_full"), NT)
        for g in range(2):
            last = dve.tensor_copy(kdup[:, :, 2 * g:2 * g + 2, :],
                                   qkv[:, :, 512 + 64 * g:576 + 64 * g].unsqueeze(2).broadcast_to([P, NT, 2, 64]))
            dve_step(last) if g == 0 else last.then_inc(S("qk_ready"), 1)

    def act_att_prepare():
        for t in range(NT):
            act.wait_ge(*act_more("qk_full"))
            b = 2 * (t % 2)
            act.activation(qT[:, :, P * t:P * t + P], bank(b).rearrange("p (b n) -> p b n", b=4), ACT.Copy)
            act.activation(kT2[:, :, P * t:P * t + P], bank(b + 1, 256).rearrange("p (b n) -> p b n", b=2), ACT.Copy
                           ).then_inc(S("qkT_ready"), 1)

    def pe_att_prepare():
        pe.wait_ge(*pe_more("qk_ready"))
        for t in range(NT):
            if t >= 2:
                pe.wait_ge(*pe_more("qkT_ready"))
            b0 = 2 * (t % 2)
            for b in range(4):
                pe.transpose(psum[:, b0, P * b:P * b + P], qkv[:, t, P * b:P * b + P], ident)
            for b in range(2):
                mm = pe.transpose(psum[:, b0 + 1, P * b:P * b + P], kdup[:, t, 2 * b:2 * b + 2, :].rearrange("p a n -> p (a n)"), ident)
            mm.then_inc(S("qk_full"), 1)
        pe.wait_ge(*pe_more("qkT_ready", 2))

    def nkeys(t):
        return TOK if lat(t) else STREAM

    def pe_att():
        def transposes(i):
            t, h = ATT[i]
            pe.wait_ge(*pe_more("prob_ready"))
            if i >= 2:
                pe.wait_ge(*pe_more("probT_ready"))
            for k in range(nkeys(t) // P):
                mm = pe.transpose(psum[:, 3 + i % 2, P * k:P * k + P], pbuf[i % 3][:, P * k:P * k + P], ident)
            mm.then_inc(S("probT_full"), 1)

        def values(gi):
            t, g = gi // 2, gi % 2
            pe.wait_ge(S("probT_ready"), 4 * gi + 4)
            if gi:
                pe.wait_ge(*pe_more("o_done"))
            nk = nkeys(t) // P
            for par in range(2):
                for k in range(nk):
                    mm = pe.matmul(psum[64 * par:64 * par + 64, 5, 0:256], qkv[:, k, 640 + 64 * g:704 + 64 * g],
                                   ptb[gi % 2][:, k, par, :, :].rearrange("p j n -> p (j n)"), start=k == 0, stop=k == nk - 1)
            mm.then_inc(S("o_full"), 1)

        for i, (t, h) in enumerate(ATT):
            if i >= 3:
                pe.wait_ge(S("prob_ready"), i - 2)
            a, n = 64 * (h % 2), nkeys(t)
            if lat(t):
                pe.matmul(bank(i % 3), identb, attmask[t - 2], start=True, stop=False)
            pe.matmul(bank(i % 3, n), qT[a:a + 64, h // 2, P * t:P * t + P], kT2[a:a + 64, h // 4, 0:n],
                      start=not lat(t), stop=True).then_inc(S("score_full"), 1)
            if i >= 2:
                transposes(i - 2)
            if i >= 6 and (i - 6) % 4 == 0:
                values((i - 6) // 4)
            if i in ATT_MOD:
                pe_mod_rows(ATT_MOD[i])
            if i - 1 in ATT_MOD:
                pe_mod_cols(ATT_MOD[i - 1])
        for i in (len(ATT) - 2, len(ATT) - 1):
            transposes(i)
        values(len(ATT) // 4 - 1)
        pe.wait_ge(*pe_more("o_done"))
        pe.wait_ge(*pe_more("probT_ready", 2))

    def dve_att():
        def probs(i):
            t, h = ATT[i]
            dve.wait_ge(*dve_more("sum_ready"))
            dve_step(dve.tensor_tensor(RDEN[:, i:i + 1], RSUM[:, i:i + 1], ESINK[:, i:i + 1], ALU.add))
            dve_step(dve.reciprocal(RDEN[:, i:i + 1], RDEN[:, i:i + 1]))
            p = pbuf[i % 3][:, 0:nkeys(t)]
            dve.tensor_scalar(p, p, RDEN[:, i:i + 1], None, ALU.mult).then_inc(S("prob_ready"), 1)

        for i, (t, h) in enumerate(ATT):
            dve.wait_ge(*dve_more("score_full"))
            dve_step(dve.tensor_reduce(NM[:, i:i + 1], bank(i % 3, nkeys(t)), AX.X, ALU.max))
            dve_step(dve.tensor_scalar(NM[:, i:i + 1], NM[:, i:i + 1], 0.125, brd[:, 8 + h:9 + h], ALU.mult, ALU.max))
            dve.tensor_scalar(NM[:, i:i + 1], NM[:, i:i + 1], -1.0, None, ALU.mult).then_inc(S("max_ready"), 1)
            if i:
                probs(i - 1)
            if i - 1 in ATT_MOD:
                dve_mod(ATT_MOD[i - 1])
        probs(len(ATT) - 1)

    def act_att():
        def evac(i):
            t, h = ATT[i]
            gi, par, j = i // 4, h % 2, (h % 4) // 2
            nk = nkeys(t) // P
            act.wait_ge(*act_more("probT_full"))
            if gi >= 2 and i % 4 == 0:
                act.wait_ge(S("o_full"), gi - 1)
            act.activation(ptb[gi % 2][:, 0:nk, par, j, :], bank(3 + i % 2, P * nk).rearrange("p (k n) -> p k n", k=nk), ACT.Copy
                           ).then_inc(S("probT_ready"), 1)

        def evac_o(gi):
            t, g = gi // 2, gi % 2
            act.wait_ge(*act_more("o_full"))
            act.activation(catT[:, 4 + 2 * g:6 + 2 * g, P * t:P * t + P], bank(5, 256).rearrange("p (j n) -> p j n", j=2), ACT.Copy
                           ).then_inc(S("o_done"), 1)

        for i, (t, h) in enumerate(ATT):
            act.wait_ge(*act_more("max_ready"))
            if i >= 3:
                act.wait_ge(S("probT_full"), i - 2)
            act_step(act.activation(pbuf[i % 3][:, 0:nkeys(t)], bank(i % 3, nkeys(t)), ACT.Exp, bias=NM[:, i:i + 1], scale=0.125,
                                    accum_out=RSUM[:, i:i + 1]))
            act.activation(ESINK[:, i:i + 1], brd[:, 8 + h:9 + h], ACT.Exp, bias=NM[:, i:i + 1]).then_inc(S("sum_ready"), 1)
            if i >= 2:
                evac(i - 2)
            if i >= 7 and (i - 7) % 4 == 0:
                evac_o((i - 7) // 4)
            if i in ATT_MOD:
                act_mod(ATT_MOD[i])
        for i in (len(ATT) - 2, len(ATT) - 1):
            evac(i)
        evac_o(len(ATT) // 4 - 1)

    def pe_grow(l, which, streams):
        blk = 16 + 24 * which
        pe.wait_ge(S("mod_done"), 6)
        for s in streams:
            for half in range(2):
                if s != streams[0]:
                    pe.wait_ge(*pe_more("grow_done"))
                for k in range(4):
                    mm = pe.matmul(psum[:, 6 + half, P * k:P * k + P],
                                   mcol[:, l, blk + 4 * half + k, s:s + 1].broadcast_to([P, P]), ident, start=True, stop=True)
                mm.then_inc(S("grow_full"), 1)
        for _ in range(2):
            pe.wait_ge(*pe_more("grow_done"))

    def act_grow(streams):
        for s in streams:
            for half in range(2):
                act.wait_ge(*act_more("grow_full"))
                act.activation(grow[:, s, 512 * half:512 * half + 512], bank(6 + half), ACT.Copy).then_inc(S("grow_done"), 1)

    def otmp(i):
        return view(16384 + 512 * (i % 3), [512])

    def pe_out(tiles, pos):
        n = 0
        for half in range(2):
            weights_here(pos + half)
            w = slot(pos + half, 512)
            for t in tiles:
                if n >= 6:
                    pe.wait_ge(*pe_more("out_done"))
                for k in range(KD):
                    mm = pe.matmul(bank(n % 6), catT[:, k, P * t:P * t + P], w[:, k, :], start=k == 0, stop=k == KD - 1)
                mm.then_inc(S("out_full"), 1)
                n += 1
        pe.wait_ge(*pe_more("out_done", min(n, 6)))

    def dve_out(tiles, l):
        n = 0
        dve.wait_ge(S("grow_done"), GROW_AFTER[l][0])
        for half in range(2):
            for t in tiles:
                dve.wait_ge(*dve_more("out_full"))
                if n >= 3:
                    dve.wait_ge(*dve_more("res_added"))
                dve.tensor_tensor(otmp(n), bank(n % 6), grow[:, 0 if lat(t) else 1, 512 * half:512 * half + 512], ALU.mult
                                  ).then_inc(S("out_done"), 1)
                n += 1
        dve.wait_ge(*dve_more("res_added", min(n, 3)))

    def pool_out(tiles):
        n = 0
        for half in range(2):
            for t in tiles:
                pool.wait_ge(*pool_more("out_done"))
                v = xres[:, t, 512 * half:512 * half + 512]
                pool.tensor_tensor(v, v, otmp(n), ALU.add).then_inc(S("res_added"), 1)
                n += 1
        pool.wait_ge(*pool_more("res_added", n))


    rawo = view(4096, [4, 2, STREAM + 2])
    accv = view(6160, [4, TOK])
    qTo = view(8208, [4, STREAM])
    kTo = view(9232, [4, TOK])
    ktok = view(11280, [NT, 512])
    vaug = view(13328, [NT, H, VA])
    og = view(17456, [2, D])
    sqo = view(19504, [5, TOK])
    tqo = view(22064, [5, TOK])
    tmpo = view(24624, [TOK])
    hacc = view(4096, [2, D])
    qk = view(6144, [2, H, P])
    state = [view(19504 + 516 * d, [4, VA]) for d in range(2)]
    wto = [[view(20536 + 512 * g, [4, P]) for g in range(2)],
           [view(512 * g, [4, P]) for g in range(2)]]
    qe = [view(10768, [4, P]), view(1024, [4, P])]
    ktil = view(9232, [512])
    num = view(9744, [D])
    coq = rt[:, 0:NT * 3 * ROWS].rearrange("p (t q r) -> p t q r", t=NT, q=3)
    spb = rt[:, 480:600].rearrange("p (s r) -> p s r", s=3)
    dgo = rt[:, 600:720].rearrange("p (s r) -> p s r", s=3)
    den = rt[:, 720:744].rearrange("p (j h) -> p j h", j=3)
    chain = rt[:, 744:784].rearrange("p (j s) -> p j s", j=10)
    spb2 = rt[:, 784:808].rearrange("p (s r) -> p s r", s=3)
    BL, CML, MIN, MNEW, SPA, DEL, T1, T2 = (chain[0:ROWS, j, :] for j in range(8))

    OD0 = MOE_BASE[0] + 3 * E
    EVEN_FILLS = len(IN_EVEN)
    IN_ODD = [("q", b) for b in range(4)] + [("k", b) for b in range(4)] + [("v", b) for b in range(8)]

    def pe_in_odd():
        w = slot(OD0, 32)
        weights_here(OD0)
        for j, c0 in enumerate((0, 16)):
            pe_gates(j, w, c0).then_inc(S("in_full"), 1)

        def transposes(j):
            kind, b = IN_ODD[j]
            pe.wait_ge(S("conv_done"), 6 + j + 1)
            bk = 4 + j % 2
            if j >= 6:
                pe.wait_ge(*pe_more("tok_done"))
            src = kTo[:, b, :] if kind == "k" else accv[:, j % 4, :]
            for t in range(NT):
                mm = pe.transpose(psum[:, bk, P * t:P * t + P], src[:, P * t:P * t + P], ident)
            mm.then_inc(S("tok_full"), 1)

        at = None
        for j, (kind, b) in enumerate(IN_ODD):
            bk = (j + 2) % 4
            if j in (2, 3):
                pe.wait_ge(*pe_more("gates_read"))
            elif j >= 4:
                pe.wait_ge(*pe_more("raw_ready"))
            pos = OD0 + 1 + j // 4
            if pos != at:
                weights_here(pos)
                at = pos
            w = slot(pos, 512)
            tok = slice(STREAM, TOK) if kind == "q" else slice(0, TOK)
            for k in range(KD):
                mm = pe.matmul(bank(bk, tok.stop - tok.start), w[:, k, P * (b % 4):P * (b % 4) + P], hT[:, k, tok],
                               start=k == 0, stop=k == KD - 1)
            mm.then_inc(S("in_full"), 1)
            if j >= 7:
                transposes(j - 3)
        for n in range(4):
            half, t = n // 2, 2 + n % 2
            pos = OD0 + 5 + half
            if n % 2 == 0:
                weights_here(pos)
            pe.wait_ge(*pe_more("raw_ready"))
            w = slot(pos, 512)
            for k in range(KD):
                mm = pe.matmul(bank((18 + n) % 4), hT[:, k, P * t:P * t + P], w[:, k, :], start=k == 0, stop=k == KD - 1)
            mm.then_inc(S("in_full"), 1)
            if n < 3:
                transposes(13 + n)
        pe.wait_ge(S("og_done"), 4)
        pe.wait_ge(*pe_more("tok_done", 2))

    def act_in_odd():
        act_log1p_exp(rows(sqo, 2))
        act.wait_ge(*act_more("raw_cleared"))
        act_more("in_full", EVEN_FILLS + 2)

        def silu(j):
            kind, b = IN_ODD[j]
            v = accv[:, j % 4, :] if kind == "v" else (qTo if kind == "q" else kTo)[:, b, :]
            act.wait_ge(*act_more("conv_ready"))
            act.activation(v, v, ACT.Silu).then_inc(S("conv_done"), 1)

        for j, (kind, b) in enumerate(IN_ODD):
            if j == 1:
                act_log1p_ln(rows(sqo, 3))
            elif j == 3:
                act_od_rows()
            act.wait_ge(*act_more("in_full"))
            if j >= 4:
                act.wait_ge(S("conv_ready"), 6 + j - 3)
            bk = (j + 2) % 4
            if kind == "q":
                act.activation(rawo[:, j % 4, 1, 1:STREAM + 1], bank(bk, STREAM), ACT.Copy).then_inc(S("raw_ready"), 1)
            else:
                act.activation(rawo[:, j % 4, :, 1:STREAM + 1], bank(bk).rearrange("p (s n) -> p s n", s=2), ACT.Copy
                               ).then_inc(S("raw_ready"), 1)
            if j:
                silu(j - 1)
        silu(len(IN_ODD) - 1)
        for n in range(4):
            act.wait_ge(*act_more("in_full"))
            act.activation(og[:, n % 2, 512 * (n // 2):512 * (n // 2) + 512], bank((18 + n) % 4), ACT.Tanh, scale=0.5
                           ).then_inc(S("og_done"), 1)

    def dve_in_odd():
        dve_step(dve.memset(sqo[0:ROWS, :, :], 0.0))
        for side in (0, STREAM + 1):
            last = dve.memset(rawo[:, :, :, side:side + 1], 0.0)
            dve_step(last) if side == 0 else last.then_inc(S("raw_cleared"), 1)
        dve_step(dve.memset(vaug[:, :, :, DV:VA], 1.0))
        dve.wait_ge(S("in_full"), EVEN_FILLS + 2)
        for j, q, par in ((0, 0, 2), (1, 1, 3)):
            dve_step(dve.tensor_scalar(sqo[0:H, q, :], psum[0:H, j, :], rowpar[0:H, par:par + 1], None, ALU.add))
            dve.tensor_scalar(sqo[DIR1:ROWS, q, :], psum[DIR1:ROWS, j, :], rowpar[DIR1:ROWS, par:par + 1], None, ALU.add
                              ).then_inc(S("gates_read"), 1)
        dve.wait_ge(S("gates_read"), 2)
        dve_log1p_abs(rows(sqo, 1), rows(sqo, 2))

        def tok(j):
            kind, b = IN_ODD[j]
            dve.wait_ge(*dve_more("tok_full"))
            src = bank(4 + j % 2).rearrange("p (t n) -> p t n", t=NT)
            dst = ktok[:, :, P * b:P * b + P] if kind == "k" else vaug[:, :, b, 0:DV]
            dve.tensor_copy(dst, src).then_inc(S("tok_done"), 1)

        for j, (kind, b) in enumerate(IN_ODD):
            dve.wait_ge(*dve_more("raw_ready"))
            wc = lambda i, j=j: colsb[:, 16 * i + j:16 * i + j + 1]
            if kind == "q":
                dve_conv(qTo[:, b, :], rawo[:, j % 4, 1:2, :], wc, colsb[:, 48 + j:49 + j])
            elif kind == "k":
                dve_conv(kTo[:, b, :], rawo[:, j % 4, :, :], wc, colsb[:, 48 + j:49 + j])
            else:
                if j >= 8 + 4:
                    dve.wait_ge(S("tok_full"), j - 7)
                dve_conv(accv[:, j % 4, :], rawo[:, j % 4, :, :], wc, colsb[:, 48 + j:49 + j])
            if j >= 8:
                tok(j - 4)
            if j == 0:
                dve_log1p_sum(rows(sqo, 2), rows(sqo, 3), rows(sqo, 4), tmpo[0:ROWS, :])
            elif j == 1:
                dve_od_rows()
            elif j == 3:
                dve_od_rows_end()
        for j in range(12, 16):
            tok(j)

    def chunks(v):
        return v.rearrange("p (s n) -> p s n", s=4)

    def dve_od_rows():
        v, f, e3, w4, d5 = (rows(sqo, q) for q in range(5))
        dve_log1p_end(e3, w4, d5, tmpo[0:ROWS, :])
        dve_step(dve.scalar_tensor_tensor(f, f, 0.0, w4, ALU.min, ALU.subtract))
        b = e3
        for st in range(4):
            dve_step(dve.tensor_tensor_scan(b[:, P * st:P * st + P], ones[0:ROWS, :], f[:, P * st:P * st + P],
                                            0.0, ALU.mult, ALU.add))
        dve_step(dve.tensor_tensor(v, v, b, ALU.subtract))
        for st in range(4):
            dve_step(dve.tensor_tensor_scan(w4[:, P * st:P * st + P], ones[0:ROWS, :], v[:, P * st:P * st + P],
                                            NEG, ALU.mult, ALU.max))
        dve_step(dve.tensor_copy(BL, chunks(b)[:, :, P - 1]))
        dve_step(dve.tensor_tensor(CML, BL, chunks(w4)[:, :, P - 1], ALU.add))
        dve_step(dve.memset(MIN[:, 0:1], 0.0))
        for st in range(3):
            a = slice(st, st + 1)
            dve_step(dve.tensor_tensor(T1[:, a], BL[:, a], MIN[:, a], ALU.add))
            dve_step(dve.tensor_tensor(MIN[:, st + 1:st + 2], T1[:, a], CML[:, a], ALU.max))
        dve_step(dve.tensor_tensor(SPA[:, 0:3], T1[:, 0:3], MIN[:, 1:4], ALU.subtract))
        dve_step(dve.tensor_tensor(DEL[:, 0:3], BL[:, 0:3], MIN[:, 1:4], ALU.subtract))
        lt = slice(STREAM, TOK)
        dve_step(dve.tensor_tensor(w4[:, lt], w4[:, lt], b[:, lt], ALU.add))
        for st in (2, 3):
            dve_step(dve.tensor_scalar(d5[:, P * st:P * st + P], b[:, P * st:P * st + P], MIN[:, st:st + 1], None, ALU.add))
        dve_step(dve.tensor_tensor(w4[:, lt], w4[:, lt], d5[:, lt], ALU.max))
        dve_step(dve.tensor_tensor(b[:, lt], b[:, lt], w4[:, lt], ALU.subtract))
        dve_step(dve.tensor_tensor(d5[:, lt], d5[:, lt], w4[:, lt], ALU.subtract))
        dve_step(dve.memset(f[:, 3 * P:], 0.0))
        for q in (b, w4, d5):
            last = dve.memset(q[:, 0:STREAM], 0.0)
            dve_step(last) if q is not d5 else last.then_inc(S("row_dve"), 1)

    def dve_od_rows_end():
        dve.wait_ge(*dve_more("row_act"))
        dve_true_order(tqo, sqo, 5)
        dve.tensor_tensor(dgo[0:ROWS, :, :], SPA[:, 0:3].unsqueeze(2).broadcast_to([ROWS, 3, ROWS]),
                          ident[0:ROWS, 0:ROWS].unsqueeze(1).broadcast_to([ROWS, 3, ROWS]), ALU.mult
                          ).then_inc(S("dg_ready"), 1)

    def act_od_rows():
        v, f, b, w4, d5 = (rows(sqo, q) for q in range(5))
        act.wait_ge(*act_more("row_dve"))
        for st in range(3):
            a = slice(P * st, P * st + P)
            act.activation(f[:, a], v[:, a], ACT.Exp, bias=DEL[:, st:st + 1])
        act.activation(w4, w4, ACT.Exp, scale=-1.0)
        act.activation(d5, d5, ACT.Exp)
        act.activation(SPA[:, 0:3], SPA[:, 0:3], ACT.Exp).then_inc(S("row_act"), 1)

    def pe_ml_prepare():
        pe.wait_ge(*pe_more("tq_ready"))
        for t in range(NT):
            for j, q in enumerate((0, 1, 3)):
                mm = pe.transpose(psum[:, t // 2, 120 * (t % 2) + ROWS * j:120 * (t % 2) + ROWS * (j + 1)],
                                  tqo[0:ROWS, q, P * t:P * t + P], ident[0:ROWS, 0:ROWS])
            if t % 2:
                mm.then_inc(S("pre_full"), 1)
        pe.wait_ge(*pe_more("dg_ready"))
        pe.matmul(bank(2, 3 * ROWS), ones[0:ROWS, :], dgo[0:ROWS, :, :].rearrange("p s r -> p (s r)"), start=True, stop=True
                  ).then_inc(S("pre_full"), 1)
        pe.wait_ge(S("conv_done"), 6 + 8)
        for n in range(4):
            t, odd = n // 2, n % 2
            for h in range(4):
                hh = 2 * h + odd
                a = 64 * odd
                mm = pe.matmul(psum[:, 3 + n, P * h:P * h + P], kTo[a:a + 64, hh // 2, STREAM + P * t:STREAM + P * t + P],
                               qTo[a:a + 64, hh // 2, P * t:P * t + P], start=True, stop=True)
            mm.then_inc(S("pre_full"), 1)

    def dve_ml_prepare():
        for d in range(2):
            dve_step(dve.memset(state[d], 0.0))
        for j in range(2):
            dve.wait_ge(*dve_more("pre_full"))
            dve_step(dve.tensor_copy(coq[:, 2 * j:2 * j + 2].rearrange("p t q r -> p (t q r)"), bank(j, 240)))
        dve.wait_ge(*dve_more("pre_full"))
        dve_step(dve.tensor_copy(spb.rearrange("p s r -> p (s r)"), bank(2, 3 * ROWS)))
        for lo in range(2):
            a = slice(64 * lo, 64 * lo + 64)
            for d in range(2):
                dve_step(dve.tensor_copy(spb2[a, :, 4 * d:4 * d + 4], spb[a, :, DIR1 * d + lo:DIR1 * d + H:2]))
        for n in range(4):
            dve.wait_ge(*dve_more("pre_full"))
            last = dve.tensor_scalar(qk[:, n // 2].rearrange("p (h o) n -> p o h n", o=2)[:, n % 2],
                                     bank(3 + n).rearrange("p (h n) -> p h n", h=4), 0.125, None, ALU.mult)
            dve_step(last) if n < 3 else last.then_inc(S("ml_prepared"), 1)
        dve.wait_ge(S("ml_prepared"), 1)

    def sprod(i, b):
        return psum[:, 2 * (i % 2) + b // 2, VA * (b % 2):VA * (b % 2) + VA]

    def pe_ml():
        def decays(n):
            st, d = SSD_ITER[4 + n]
            t = tile_of(st, d)
            if n:
                pe.wait_ge(*pe_more("qe_ready"))
            for b in range(4):
                for lo in range(2):
                    r = DIR1 * d + 2 * b + lo
                    mm = pe.matmul(psum[64 * lo:64 * lo + 64, 6, P * b:P * b + P],
                                   ident[0:ROWS, r:r + 1].broadcast_to([ROWS, 64]),
                                   tqo[0:ROWS, 4, P * t:P * t + P], start=True, stop=True)
            mm.then_inc(S("einter_full"), 1)
            for g in range(2):
                if n:
                    pe.wait_ge(*pe_more("oarg_ready"))
                pe.matmul(bank(4 + g), identb, decmask[d], start=True, stop=False)
                for h in range(4):
                    r = DIR1 * d + 4 * g + h
                    mm = pe.matmul(psum[:, 4 + g, P * h:P * h + P], ident[0:ROWS, r:r + 1].broadcast_to([ROWS, P]),
                                   tqo[0:ROWS, 2, P * t:P * t + P], start=False, stop=h == 3)
                mm.then_inc(S("odec_full"), 1)

        pe.wait_ge(S("ml_prepared"), 1)
        decays(0)
        n_state = 0
        for i, (st, d) in enumerate(SSD_ITER):
            t = tile_of(st, d)
            if st >= 2:
                n = i - 4
                if n == 0:
                    decays(1)
                pe.wait_ge(S("qe_ready"), n + 1)
                pe.wait_ge(S("sstate_done"), n_state)
                if n:
                    pe.wait_ge(S("num_done"), n)
                for h in (0, 2, 4, 6, 1, 3, 5, 7):
                    if h in (0, 4):
                        pe.wait_ge(*pe_more("owts_ready"))
                    a = 64 * (h % 2)
                    b, j = 2 * (h % 2) + h // 6, h // 2 % 3
                    o = psum[:, b, VA * j:VA * j + VA]
                    pe.matmul(o, wto[n % 2][h // 4][:, h % 4, :], vaug[:, t, h, :], start=True, stop=False)
                    mm = pe.matmul(o, qe[n % 2][a:a + 64, h // 2, :], state[d][a:a + 64, h // 2, :], start=False, stop=True)
                mm.then_inc(S("num_full"), 1)
                if n < 2:
                    decays(n + 2)
            if st < 3:
                pe.wait_ge(*pe_more("ktil_ready"))
                if st == 2:
                    pe.wait_ge(S("num_done"), d + 1)
                elif i >= 2:
                    pe.wait_ge(S("sstate_done"), i - 1)
                for b in range(4):
                    for lo in range(2):
                        mm = pe.matmul(sprod(i, b)[64 * lo:64 * lo + 64], ktil[:, P * b + 64 * lo:P * b + 64 * lo + 64],
                                       vaug[:, t, 2 * b + lo, :], start=True, stop=True)
                mm.then_inc(S("sprod_full"), 1)
                n_state += 1

    NUM_BANKS = [(0, slice(0, 5, 2)), (1, slice(6, 7, 2)), (2, slice(1, 6, 2)), (3, slice(7, 8, 2))]

    def dve_ml():
        def keys(st, d):
            t = tile_of(st, d)
            dve.scalar_tensor_tensor(heads(ktil), heads(ktok[:, t, :]), 0.125,
                                     coq[:, t, 1, DIR1 * d:DIR1 * d + H].unsqueeze(2).broadcast_to([P, H, 64]),
                                     ALU.mult, ALU.mult).then_inc(S("ktil_ready"), 1)

        def weights(n):
            st, d = SSD_ITER[4 + n]
            t = tile_of(st, d)
            dve.wait_ge(*dve_more("einter_full"))
            dve.tensor_tensor(qe[n % 2], qTo[:, :, P * (t - 2):P * (t - 1)], bank(6).rearrange("p (b n) -> p b n", b=4), ALU.mult
                              ).then_inc(S("qe_ready"), 1)
            for g in range(2):
                dve.wait_ge(*dve_more("odec_full"))
                dve.tensor_tensor(wto[n % 2][g], bank(4 + g).rearrange("p (h n) -> p h n", h=4),
                                  coq[:, t, 0, DIR1 * d + 4 * g:DIR1 * d + 4 * g + 4].unsqueeze(2).broadcast_to([P, 4, P]),
                                  ALU.add).then_inc(S("oarg_ready"), 1)

        keys(0, 0)
        weights(0)
        for i, (st, d) in enumerate(SSD_ITER):
            t = tile_of(st, d)
            if st >= 2:
                n = i - 4
                for g in range(2):
                    dve.wait_ge(*dve_more("oexp_ready"))
                    dve.tensor_tensor(wto[n % 2][g], wto[n % 2][g], qk[:, t - 2, 4 * g:4 * g + 4, :], ALU.mult
                                      ).then_inc(S("owts_ready"), 1)
                if n < 3:
                    weights(n + 1)
                if n < 2:
                    dve_step(dve.scalar_tensor_tensor(og[:, n, :], og[:, n, :], 1.0, hnorm[:], ALU.add, ALU.mult))
                if n == 3:
                    dve_ml_out(OUT_ORDER[0])
                dve.wait_ge(S("num_full"), n + 1)
                for b, hs in NUM_BANKS:
                    nh = len(range(*hs.indices(H)))
                    dve_step(dve.tensor_copy(den[:, 0, hs], bank(b, nh * VA).rearrange("p (h n) -> p h n", h=nh)[:, :, DV]))
                dve_step(dve.tensor_scalar(den[:, 1, :], den[:, 0, :], -1.0, None, ALU.mult))
                dve_step(dve.tensor_tensor(den[:, 0, :], den[:, 0, :], den[:, 1, :], ALU.max))
                dve_step(dve.tensor_tensor(den[:, 0, :], den[:, 0, :], coq[:, t, 2, DIR1 * d:DIR1 * d + H], ALU.max))
                dve_step(dve.reciprocal(den[:, 0, :], den[:, 0, :]))
                dst = hacc[:, t - 2, :] if d == first_dir(t) else num
                for b, hs in NUM_BANKS:
                    nh = len(range(*hs.indices(H)))
                    last = dve.tensor_tensor(dst.rearrange("p (h n) -> p h n", h=H)[:, hs],
                                             bank(b, nh * VA).rearrange("p (h n) -> p h n", h=nh)[:, :, 0:DV],
                                             den[:, 0, hs].unsqueeze(2).broadcast_to([P, nh, DV]), ALU.mult)
                    dve_step(last) if b < 3 else last.then_inc(S("num_done"), 1)
                dve.wait_ge(*dve_more("num_done"))
                if d != first_dir(t):
                    dve_step(dve.tensor_tensor(hacc[:, t - 2, :], hacc[:, t - 2, :], num, ALU.add))
            if st < 3:
                dve.wait_ge(S("sprod_full"), i + 1)
                if i < 5:
                    keys(*SSD_ITER[i + 1])
                for b in range(4):
                    v = state[d][:, b, :]
                    last = dve.scalar_tensor_tensor(v, v, spb2[:, st, 4 * d + b:4 * d + b + 1], sprod(i, b), ALU.mult, ALU.add)
                    dve_step(last) if b != 3 else last.then_inc(S("sstate_done"), 1)
                dve.wait_ge(*dve_more("sstate_done"))

    def first_dir(t):
        return 0 if t == 2 else 1

    def act_ml():
        for i in range(4):
            for g in range(2):
                act.wait_ge(*act_more("oarg_ready"))
                act.activation(wto[i % 2][g], wto[i % 2][g], ACT.Exp).then_inc(S("oexp_ready"), 1)

    OUT_ORDER = [1, 0]

    def dve_ml_out(t):
        dve_step(dve.tensor_tensor(num, hacc[:, t, :], hacc[:, t, :], ALU.mult))
        dve_step(dve.tensor_reduce(stat[:, 0:H], num.rearrange("p (h n) -> p h n", h=H), AX.X, ALU.add))
        dve_rstd(H, DV)
        rstd = stat2[:, 1, 0:H]
        dve_step(dve.tensor_scalar(rstd, rstd, 0.5, None, ALU.mult))
        v = hacc[:, t, :]
        dve_step(dve.tensor_tensor(heads(v), heads(v), rstd.unsqueeze(2).broadcast_to([P, H, DV]), ALU.mult))
        dve.tensor_tensor(v, v, og[:, t, :], ALU.mult).then_inc(S("cat_ready"), 1)

    def pe_ml_out():
        pe.wait_ge(S("num_done"), 4)
        for t in OUT_ORDER:
            pe.wait_ge(*pe_more("cat_ready"))
            for half in range(2):
                for b in range(4):
                    mm = pe.transpose(psum[:, 2 * t + half, P * b:P * b + P], hacc[:, t, 512 * half + P * b:512 * half + P * b + P], ident)
                mm.then_inc(S("cat_full"), 1)
        pe.wait_ge(*pe_more("cat_act", 4))

    def act_ml_out():
        for t in OUT_ORDER:
            act_rstd(H)
            for half in range(2):
                act.wait_ge(*act_more("cat_full"))
                act.activation(catT[:, 4 * half:4 * half + 4, P * (t + 2):P * (t + 3)], bank(2 * t + half).rearrange("p (b n) -> p b n", b=4),
                               ACT.Copy).then_inc(S("cat_act"), 1)


    def rtv(at, shape):
        n = int(np.prod(shape))
        names = "abcd"[:len(shape)]
        return rt[:, at:at + n].rearrange(f"p ({' '.join(names)}) -> p {' '.join(names)}", **dict(zip(names, shape)))

    def pe_router(l, tiles):
        n = P * len(tiles)
        c0 = P * tiles[0]
        pe.wait_ge(S("zeroed"), 2)
        for k in range(KD):
            j = 32 * (k % 4)
            mm = pe.matmul(psum[j:j + 32, 4, 0:n], rw32[:, k, :], hT[:, k, c0:c0 + n], start=k < 4, stop=k >= 4)
        mm.then_inc(S("score4_full"), 1)
        pe.wait_ge(*pe_more("srow_ready"))
        for j in range(len(tiles)):
            mm = pe.transpose(psum[:, 5, P * j:P * j + P], modrow[:, P * j:P * j + P], ident)
        mm.then_inc(S("scol_full"), 1)
        for i, t in enumerate(tiles):
            if i >= 2:
                pe.wait_ge(*pe_more("back_act"))
            for half in range(2):
                for k in range(4):
                    mm = pe.transpose(psum[:, 2 * (i % 2) + half, P * k:P * k + P], hT[:, 4 * half + k, P * t:P * t + P], ident)
            mm.then_inc(S("back_full"), 1)
        pe.wait_ge(*pe_more("back_act", 2))
        pe.wait_ge(*pe_more("mask_ready"))
        mk = maskb[:, 0:len(tiles), :]
        for i in range(len(tiles)):
            for j in range(i):
                pe.matmul(psum[:, 6, E * i:E * i + E], onesb, mk[:, j, :], start=j == 0, stop=False)
            pe.matmul(psum[:, 6, E * i:E * i + E], upper, mk[:, i, :], start=i == 0, stop=True)
        for j in range(len(tiles)):
            mm = pe.matmul(psum[:, 6, E * NT:E * NT + E], onesb, mk[:, j, :], start=j == 0, stop=j == len(tiles) - 1)
        mm.then_inc(S("pos_full"), 1)
        pe.wait_ge(*pe_more("slot1_ready"))
        for j in range(2):
            for i in range(len(tiles)):
                mm = pe.matmul(psum[:, 7, 0:2 * E], slot1[:, j, i, :], tokat[:, j, i, :, :].rearrange("p a e -> p (a e)"),
                               start=j == 0 and i == 0, stop=j == 1 and i == len(tiles) - 1)
        mm.then_inc(S("table_full"), 1)

    def act_router(l, tiles):
        n = P * len(tiles)
        act.wait_ge(*act_more("score4_full"))
        act.wait_ge(S("modcol_full"), 2 * MODC)
        act.activation(modrow[:, 0:n], bank(4, n), ACT.Copy).then_inc(S("srow_ready"), 1)
        act.wait_ge(*act_more("neg_ready"))
        v = rtv(0, [NT, E])[:, 0:len(tiles), :]
        act.activation(v, v, ACT.Exp, scale=-1.0).then_inc(S("sig_exp"), 1)
        for i, t in enumerate(tiles):
            act.wait_ge(*act_more("back_full"))
            act.activation(htok[:, t, :].rearrange("p (b n) -> p b n", b=2), psum[:, 2 * (i % 2):2 * (i % 2) + 2, :], ACT.Copy
                           ).then_inc(S("back_act"), 1)
            act.wait_ge(*act_more("back_act"))
            act.dma_start(hdram[l][P * i:P * i + P, :], htok[:, t, :]).then_inc(S("hstored"), 16)

    def dve_router_setup():
        dve_step(dve.memset(rw32[:], 0.0))
        dve.wait_ge(S("params"), PARAMS_IN)
        dve_step(dve.tensor_copy(tok32[:], tokid))
        dve_step(dve.memset(zrow[:], 0))
        dve_step(dve.memset(cnts[:], 0))
        dve_step(dve.memset(zeros, 0.0))
        dve.tensor_copy(rw32[:, :, 0:E], rw[:]).then_inc(S("zeroed"), 1)

    def dve_router(l, tiles):
        n = len(tiles)
        sc, bi, mb, oh1, oh2, t16, u16 = (rtv(64 * j, [NT, E])[:, 0:n] for j in range(7))
        mx, mn, c23 = (rtv(448 + 32 * j, [NT, 4, 2])[:, 0:n] for j in range(3))
        gs, eq, gsel = (rtv(544 + 16 * j, [NT, 4])[:, 0:n] for j in range(3))
        one, p1, e1, q1, r1_ = (rtv(600 + 8 * j, [NT, 2])[:, 0:n] for j in range(5))
        s1, s2, big = (rtv(640 + 8 * j, [NT, 1])[:, 0:n] for j in range(3))
        cmax = rtv(800, [1])

        def bc(v, *shape):
            return v.broadcast_to([P, *shape])

        dve.wait_ge(*dve_more("scol_full"))
        dve.tensor_reduce(sc, bank(5, P * n).rearrange("p (t g r) -> p t r g", t=n, g=4)[:, :, 0:E, :], AX.X, ALU.add
                          ).then_inc(S("neg_ready"), 1)
        dve.wait_ge(*dve_more("sig_exp"))
        dve_step(dve.tensor_scalar(sc, sc, 1.0, None, ALU.add))
        dve_step(dve.reciprocal(sc, sc))
        dve_step(dve.tensor_tensor(bi, sc, bc(rbias[:].unsqueeze(1), n, E), ALU.add))
        pr = bi.rearrange("p t (g a b) -> p (t g) a b", g=4, a=2)
        groups = "p t g a -> p (t g) a"
        dve_step(dve.tensor_tensor(mx.rearrange(groups), pr[:, :, :, 0], pr[:, :, :, 1], ALU.max))
        dve_step(dve.tensor_tensor(mn.rearrange(groups), pr[:, :, :, 0], pr[:, :, :, 1], ALU.min))
        dve_step(dve.tensor_tensor(c23, mx, mn, ALU.add))
        dve_step(dve.tensor_tensor(gs, mx[:, :, :, 0], mx[:, :, :, 1], ALU.add))
        dve_step(dve.tensor_tensor(gs, gs, c23[:, :, :, 0], ALU.max))
        dve_step(dve.tensor_tensor(gs, gs, c23[:, :, :, 1], ALU.max))

        def first_max(sel, v, tmp, desc, k):
            dve_step(dve.tensor_reduce(big, v, AX.X, ALU.max))
            dve_step(dve.tensor_tensor(tmp, v, bc(big, n, k), ALU.is_equal))
            dve_step(dve.tensor_tensor(tmp, tmp, bc(desc.unsqueeze(1), n, k), ALU.mult))
            dve_step(dve.tensor_reduce(big, tmp, AX.X, ALU.max))
            dve_step(dve.tensor_tensor(sel, tmp, bc(big, n, k), ALU.is_equal))

        first_max(gsel, gs, eq, edesc[:, 12:16], 4)
        dve_step(dve.tensor_scalar(eq, gsel, -NEG, NEG, ALU.mult, ALU.add))
        mb4, bi4 = (a.rearrange("p t (g a) -> p (t g) a", g=4) for a in (mb, bi))
        gsel4, eq4 = (a.rearrange("p t g -> p (t g)").unsqueeze(2).broadcast_to([P, 4 * n, 4]) for a in (gsel, eq))
        dve_step(dve.tensor_tensor(mb4, bi4, gsel4, ALU.mult))
        dve_step(dve.tensor_tensor(mb4, mb4, eq4, ALU.add))
        first_max(oh1, mb, t16, edesc, E)
        dve_step(dve.scalar_tensor_tensor(mb, oh1, 2.0 * NEG, mb, ALU.mult, ALU.add))
        first_max(oh2, mb, t16, edesc, E)
        dve.tensor_tensor(maskb[:, 0:n, :], oh1, oh2, ALU.add).then_inc(S("mask_ready"), 1)
        for j, oh in enumerate((oh1, oh2)):
            dve_step(dve.tensor_tensor(t16, bc(eiota.unsqueeze(1), n, E), oh, ALU.mult))
            dve_step(dve.tensor_reduce(e1[:, :, j:j + 1], t16, AX.X, ALU.add))
            for a in range(2):
                dve_step(dve.tensor_tensor(tokat[:, j, 0:n, a, :], oh, bc(tokparts[:, 0:n, a:a + 1], n, E), ALU.mult))
        dve.wait_ge(*dve_more("pos_full"))
        pos = psum[:, 6, 0:E * n].rearrange("p (t e) -> p t e", t=n)
        for j, oh in enumerate((oh1, oh2)):
            dve_step(dve.tensor_tensor(t16, pos, oh, ALU.mult))
            dve_step(dve.tensor_reduce(p1[:, :, j:j + 1], t16, AX.X, ALU.add))
            dve.tensor_tensor(slot1[:, j, 0:n, :], bc(iotab.unsqueeze(1), n, P), bc(p1[:, :, j:j + 1], n, P), ALU.is_equal
                              ).then_inc(S("dve_step" if j == 0 else "slot1_ready"), 1)
            if j == 0:
                dve.wait_ge(*dve_more("dve_step"))
        dve_step(dve.tensor_copy(cnts[0:1, (E + 1) * l:(E + 1) * l + E], psum[0:1, 6, E * NT:E * NT + E]))
        dve_step(dve.tensor_reduce(cmax, psum[:, 6, E * NT:E * NT + E], AX.X, ALU.max))
        dve_step(dve.memset(idx[:, E:E + 1], 0))
        dve.wait_ge(*dve_more("table_full"))
        dve_step(dve.tensor_copy(rt[:, 704:704 + 2 * E], psum[:, 7, 0:2 * E]))
        dve.tensor_tensor(idx[:, 0:E], rt[:, 704:704 + E], rt[:, 704 + E:704 + 2 * E], ALU.add).then_inc(S("idx_in"), 1)
        dve_step(dve.tensor_scalar(q1, p1, float(P), None, ALU.is_ge))
        for r in range(2, RMAX):
            dve_step(dve.scalar_tensor_tensor(q1, p1, float(P * r), q1, ALU.is_ge, ALU.add))
        dve_step(dve.scalar_tensor_tensor(p1, q1, -float(P), p1, ALU.mult, ALU.add))
        dve_step(dve.scalar_tensor_tensor(q1, q1, float(E), e1, ALU.mult, ALU.add))
        dve_step(dve.scalar_tensor_tensor(r1_, p1, float(NCOL), q1, ALU.mult, ALU.add))
        dve_step(dve.tensor_copy(rowi[:, 0:n, :], r1_))
        dve_step(dve.scalar_tensor_tensor(r1_, q1, float(P), p1, ALU.mult, ALU.add))
        dve_step(dve.tensor_copy(rowy[:, 0:n, :], r1_))
        dve.tensor_copy(flag[:, l:l + 1], cmax[0:1, :]).then_inc(S("rows_ready"), 1)
        for j, oh in enumerate((oh1, oh2)):
            dve_step(dve.tensor_tensor(t16, sc, oh, ALU.mult))
            dve_step(dve.tensor_reduce(one[:, :, j:j + 1], t16, AX.X, ALU.add))
        dve_step(dve.tensor_tensor(s1, one[:, :, 0:1], one[:, :, 1:2], ALU.add))
        dve_step(dve.reciprocal(s1, s1))
        dve_step(dve.tensor_tensor(gatew[:, 0:n, :], one, bc(s1, n, 2), ALU.mult))

    ZEROING = 1 + E

    def pool_zero(l):
        pool.wait_ge(S("zeroed"), 2)
        pool.dma_start(table[l].rearrange("(p n) a -> p (n a)", p=P), zrow[:]).then_inc(S("dram_zeroed"), 16)
        for e in range(E):
            dst = ydram[l][P * e:P * (e + 1), :].rearrange("p (h n) -> p h n", h=4)
            pool.dma_start(dst, zeros.unsqueeze(1).broadcast_to([P, 4, 256])).then_inc(S("dram_zeroed"), 16)

    def pool_dispatch(l, tiles):
        n = len(tiles)
        pool.wait_ge(S("dram_zeroed"), 16 * ZEROING * (l + 1))
        pool.wait_ge(S("hstored"), 16 * (NT * l + n))

    def pool_table(l, tiles):
        n = len(tiles)
        for i in range(n):
            for j in range(2):
                pool.indirect_dma_start(table[l], bass.IndirectOffsetOnAxis(ap=rowi[:, i, j:j + 1], axis=0),
                                        tok32[:, i:i + 1], None).then_inc(S(f"scattered{l}"), 16)
        pool.wait_ge(S(f"scattered{l}"), 32 * n)
        pool.dma_start(idx[:], table[l].rearrange("(p n) a -> p (n a)", p=P)).then_inc(S(f"scattered{l}"), 16)
        pool.wait_ge(S(f"scattered{l}"), 32 * n + 16)

    xg = [view(1024 * i, [D]) for i in range(2)]
    xT = [view(2048 + 1024 * i, [KD, P]) for i in range(2)]
    sil = [view(4096 + 512 * i, [FE]) for i in range(2)]
    ah = [view(5120 + 512 * i, [FE]) for i in range(2)]
    aT = [view(6144 + 512 * i, [KF, P]) for i in range(2)]
    yb = [view(7168 + 1024 * i, [D]) for i in range(2)]

    def expert_weights(l, kind, e, ds=0):
        pos = position(l, kind, e) if isinstance(e, int) else position(l, kind, e[0], looped=True)
        if isinstance(e, int):
            weights_here(pos)
        else:
            pe.wait_ge(S(f"w_ready{pos % NSLOT}"), 16 * (pos // NSLOT + 1) + e[1] * (16 * 3 * GROUP // NSLOT))
        return slot(pos, 512) if kind != "w2" else slot(pos, D, KF)

    def val(base, e, off=0):
        return base + e + off if isinstance(e, int) else base + e[0] + off + e[1] * GROUP

    def num_of(e):
        return e if isinstance(e, int) else e[0]

    XT = E + 1

    def half_count(base, e, off=0):
        n = 16 * (base + num_of(e) // 2 + off)
        return n if isinstance(e, int) else n + e[1] * (16 * GROUP // 2)

    def stored_count(l, e):
        return 2 * half_count(8 * l, e)

    def gather_count(l, e):
        return half_count((9 if num_of(e) % 2 == 0 else 8) * l, e, 1)

    def pe_xt(l, e):
        b = num_of(e) % 2
        pe.wait_ge(S(f"gathered{b}"), gather_count(l, e))
        if not (isinstance(e, int) and e == 0):
            pe.wait_ge(S("xt_act"), val(XT * l, e))
            pe.wait_ge(S("xt_dve"), val(XT * l, e))
        for k in range(KD):
            mm = pe.transpose(psum[:, 4 + k // 4, P * (k % 4):P * (k % 4) + P], xg[b][:, P * k:P * k + P], ident)
        mm.then_inc(S("xt_full"), 1)

    HALF = P // 2

    def long_list(eng, l, e):
        i = (E + 1) * l + e if isinstance(e, int) else e[1] * GROUP + ((E + 1) * l + e[0])
        src = cnts[0:1, i:i + 1] if isinstance(e, int) else cnts[0:1, bass.ds(i, 1)]
        return eng.value_load(src, min_val=0, max_val=TOK) > HALF

    def either(eng, l, e, full, narrow):
        with eng.If(long_list(eng, l, e)):
            full(l, e)
        with eng.Else():
            narrow(l, e)
        eng.end_ifs()

    def pe_h(l, e, narrow=False):
        b = num_of(e) % 2
        for j, (kind, done, free) in enumerate((("w1", "h1_full", "sil_done"), ("w3", "h3_full", "a_done"))):
            w = expert_weights(l, kind, e)
            if j == 0:
                pe.wait_ge(S("xt_act"), val(XT * l, e, 1))
                pe.wait_ge(S("xt_dve"), val(XT * l, e, 1))
            if not (isinstance(e, int) and e == 0):
                pe.wait_ge(S(free), val(E * l, e))
            for k in range(KD):
                if narrow:
                    for g in range(2):
                        mm = pe.matmul(psum[64 * g:64 * g + 64, j, 0:256], xT[b][:, k, 0:64], w[:, k, 256 * g:256 * g + 256],
                                       start=k == 0, stop=k == KD - 1)
                else:
                    mm = pe.matmul(bank(j), xT[b][:, k, :], w[:, k, :], start=k == 0, stop=k == KD - 1)
            mm.then_inc(S(done), 1)

    def pe_at(l, e, narrow=False):
        b = num_of(e) % 2
        pe.wait_ge(S("a_done"), val(E * l, e, 1))
        if not (isinstance(e, int) and e == 0):
            pe.wait_ge(S("at_done"), val(E * l, e))
        for k in range(2 if narrow else KF):
            mm = pe.transpose(psum[:, 6, P * k:P * k + P], ah[b][:, P * k:P * k + P], ident)
        mm.then_inc(S("at_full"), 1)

    def pe_y(l, e, narrow=False):
        b = num_of(e) % 2
        w = expert_weights(l, "w2", e)
        pe.wait_ge(S("at_done"), val(E * l, e, 1))
        if not (isinstance(e, int) and e == 0):
            pe.wait_ge(S("y_act"), val(E * l, e))
            pe.wait_ge(S("y_dve"), val(E * l, e))
        if narrow:
            for k in range(KF):
                for half in range(2):
                    mm = pe.matmul(psum[64 * half:64 * half + 64, 2, :], aT[b][:, k % 2, 64 * (k // 2):64 * (k // 2) + 64],
                                   w[:, k, 512 * half:512 * half + 512], start=k == 0, stop=k == KF - 1)
        else:
            for half in range(2):
                for k in range(KF):
                    mm = pe.matmul(bank(2 + half), aT[b][:, k, :], w[:, k, 512 * half:512 * half + 512], start=k == 0, stop=k == KF - 1)
        mm.then_inc(S("y_full"), 1)

    def prev(e):
        return e - 1 if isinstance(e, int) else (e[0] - 1, e[1])

    def nxt(e):
        return e + 1 if isinstance(e, int) else (e[0] + 1, e[1])

    def in_groups(eng, body):
        for e in range(GROUP):
            body(e)
        with eng.Fori(1, E // GROUP) as j:
            for e in range(GROUP):
                body((e, j))

    def pe_moe(l):
        def both(stage, e):
            either(pe, l, e, stage, lambda l, e: stage(l, e, narrow=True))

        pe.wait_ge(S("rows_ready"), l + 1)
        pe_xt(l, 0)

        def body(e):
            both(pe_h, e)
            if e != 0:
                both(pe_y, prev(e))
            pe_xt(l, nxt(e))
            both(pe_at, e)
        in_groups(pe, body)
        both(pe_y, E - 1)

    def flat(v):
        return v.rearrange("p k n -> p (k n)")

    def act_moe(l):
        def xt(e):
            act.wait_ge(S("xt_full"), val(XT * l, e, 1))
            if not (isinstance(e, int) and e < 2):
                act.wait_ge(S("h3_full"), val(E * l, e, -1))
            act.activation(flat(xT[num_of(e) % 2][:, 0:4, :]), bank(4), ACT.Copy).then_inc(S("xt_act"), 1)

        def y(e):
            act.wait_ge(S("y_full"), val(E * l, e, 1))
            if not (isinstance(e, int) and e < 2):
                act.wait_ge(S(f"ystored{num_of(e) % 2}"), stored_count(l, e))
            act.activation(yb[num_of(e) % 2][:, 0:512], bank(2), ACT.Copy).then_inc(S("y_act"), 1)

        def body(e):
            act.wait_ge(S("h1_full"), val(E * l, e, 1))
            if not (isinstance(e, int) and e < 2):
                act.wait_ge(S("a_done"), val(E * l, e, -1))
            act.activation(sil[num_of(e) % 2], bank(0), ACT.Silu).then_inc(S("sil_done"), 1)
            if e != 0:
                y(prev(e))
            xt(nxt(e))
        xt(0)
        in_groups(act, body)
        y(E - 1)

    def dve_moe(l):
        def xt(e):
            dve.wait_ge(S("xt_full"), val(XT * l, e, 1))
            if not (isinstance(e, int) and e < 2):
                dve.wait_ge(S("h3_full"), val(E * l, e, -1))
            dve.tensor_copy(flat(xT[num_of(e) % 2][:, 4:8, :]), bank(5)).then_inc(S("xt_dve"), 1)

        def y(e):
            dve.wait_ge(S("y_full"), val(E * l, e, 1))
            if not (isinstance(e, int) and e < 2):
                dve.wait_ge(S(f"ystored{num_of(e) % 2}"), stored_count(l, e))
            dve.tensor_copy(yb[num_of(e) % 2][:, 512:1024], bank(3)).then_inc(S("y_dve"), 1)

        def body(e):
            b = num_of(e) % 2
            dve.wait_ge(S("sil_done"), val(E * l, e, 1))
            dve.wait_ge(S("h3_full"), val(E * l, e, 1))
            if not (isinstance(e, int) and e < 2):
                dve.wait_ge(S("at_full"), val(E * l, e, -1))
            dve.tensor_tensor(ah[b], sil[b], bank(1), ALU.mult).then_inc(S("a_done"), 1)
            if e != 0:
                y(prev(e))
            xt(nxt(e))
            dve.wait_ge(S("at_full"), val(E * l, e, 1))
            if not (isinstance(e, int) and e < 2):
                dve.wait_ge(S("y_full"), val(E * l, e, -1))
            dve.tensor_copy(flat(aT[b]), bank(6)).then_inc(S("at_done"), 1)
        xt(0)
        in_groups(dve, body)
        y(E - 1)

    def gather_x(l, b, col, sem, *free, n=P):
        free = [(name, v if isinstance(v, int) else pool.to_reg(v)) for name, v in free]
        pool.wait_ge(S("idx_in"), l + 1)
        for name, v in free:
            pool.wait_ge(name, v)
        pool.indirect_dma_start(xg[b][0:n, :], None, hdram[l], bass.IndirectOffsetOnAxis(ap=col[0:n, :], axis=0)
                                ).then_inc(S(sem), 16)

    def pool_moe(l):
        gather_x(l, 0, idx[:, 0:1], "gathered0")

        def y_store(l, e, n=P):
            pool.wait_ge(S("y_act"), val(E * l, e, 1))
            pool.wait_ge(S("y_dve"), val(E * l, e, 1))
            row = e * P if isinstance(e, int) else e[0] * P + e[1] * (GROUP * P)
            dst = ydram[l][row:row + n, :] if isinstance(e, int) else ydram[l][bass.ds(row, n), :]
            src = yb[num_of(e) % 2]
            if n == HALF:
                for h in range(2):
                    pool.dma_start(dst[:, 512 * h:512 * h + 512], src[64 * h:64 * h + 64, 0:512]
                                   ).then_inc(S(f"ystored{num_of(e) % 2}"), 16)
            else:
                for h in range(2):
                    pool.dma_start(dst[:, 512 * h:512 * h + 512], src[:, 512 * h:512 * h + 512]
                                   ).then_inc(S(f"ystored{num_of(e) % 2}"), 16)

        def y(e):
            either(pool, l, e, y_store, lambda l, e: y_store(l, e, HALF))

        def body(e):
            k = num_of(e)
            if k == 0:
                if not isinstance(e, int):
                    pool.wait_ge(S("gathered0"), gather_count(l, e))
                    pool.wait_ge(S("gathered1"), gather_count(l, (-1, e[1])))
                a = 1 if isinstance(e, int) else e[1] * GROUP + 1
                src = idx[:, 1:1 + GROUP] if isinstance(e, int) else idx[:, bass.ds(a, GROUP)]
                pool.tensor_copy(idxg[:], src).then_inc(S("idxg_ready"), 1)
            free = [(S("idxg_ready"), 4 * l + 1 if isinstance(e, int) else e[1] + (4 * l + 1))]
            if e != 0:
                free.append((S("xt_full"), val(XT * l, e)))
            b = (k + 1) % 2
            either(pool, l, nxt(e), lambda l, _: gather_x(l, b, idxg[:, k:k + 1], f"gathered{b}", *free),
                   lambda l, _: gather_x(l, b, idxg[:, k:k + 1], f"gathered{b}", *free, n=HALF))
            if e != 0:
                y(prev(e))
        in_groups(pool, body)
        y(E - 1)

    def sp_load(pos, src, wait=None):
        dst = ring[:, pos % NSLOT, 0:src.shape[1] * src.shape[2]].rearrange("p (k n) -> p k n", k=src.shape[1])
        if wait is not None:
            sp.wait_ge(*wait)
        sp.dma_start(dst, src).then_inc(S(f"w_ready{pos % NSLOT}"), 16)

    used = [("mod_full", i + 1) for i in range(FIRST)]
    used += [("in_full", n) for n in (4, 7, 11, 15, 19)]
    used += [("mod_full", i + 1) for i in range(FIRST, 2 * MODC)]
    used += [("out_full", 4), ("out_full", 8)]

    def used_by_moe(l):
        at = {}
        for e in range(E):
            for kind, sem in (("w1", "h1_full"), ("w3", "h3_full"), ("w2", "y_full")):
                at[position(l, kind, e)] = (sem, E * l + e + 1)
        return [at[p] for p in sorted(at)]

    used += used_by_moe(0)
    used += [("in_full", EVEN_FILLS + n) for n in (2, 6, 10, 14, 18, 20, 22)]
    used += [("out_full", 10), ("out_full", 12)]
    used += used_by_moe(1)

    def free_wait(pos):
        if pos < NSLOT:
            return None
        name, n = used[pos - NSLOT]
        return S(name), n

    def sp_before(l):
        if l == 0:
            for dst, src in FIRST_PARAMS:
                sp.dma_start(dst, src).then_inc(S("first_params"), 16)
        srcs, base = (before0, 0) if l == 0 else (before1, OD0)
        for i, (src, _) in enumerate(srcs):
            sp_load(base + i, src, free_wait(base + i))
            if l == 0 and i == 2:
                for dst, src in TOKENS:
                    sp.dma_start(dst, src).then_inc(S("tokens_in"), 16)
            if l == 0 and i == NSLOT - 1:
                sp.wait_ge(S("zeroed"), 1)
                for dst, src in PARAMS:
                    sp.dma_start(dst, src).then_inc(S("params"), 16)

    def sp_moe(l):
        def load(kind, e):
            if isinstance(e, int):
                pos = position(l, kind, e)
                sp_load(pos, expert_src(l, kind, e), free_wait(pos))
            else:
                pos = position(l, kind, e[0], looped=True)
                name, off = {"w1": ("y_full", -2), "w3": ("h1_full", 0), "w2": ("h3_full", 1)}[kind]
                sp.wait_ge(S(name), val(E * l, e, off))
                sp_load(pos, expert_src(l, kind, e[1] * GROUP + e[0]), (S("rows_ready"), l + 1))

        def body(e):
            load("w1", e)
            load("w3", e)
            if e != 0:
                load("w2", prev(e))
        in_groups(sp, body)
        load("w2", E - 1)

    def extra_rounds(eng, l, tiles, body, ahead=None):
        eng.wait_ge(S("rows_ready"), l + 1)
        longest = eng.value_load(flag[0:1, l:l + 1], min_val=0, max_val=TOK)
        with eng.If(longest > P):
            if ahead is not None:
                ahead()
            with eng.Fori(1, len(tiles)) as r:
                with eng.Fori(0, E) as e:
                    body(r, e, (r - 1) * E + e)
        eng.end_ifs()

    def extra(l, name):
        return S(f"extra_{name}{l}")

    XPOS = [MOE_BASE[l] + 3 * E for l in range(2)]

    def sp_extra(l, tiles):
        def ahead():
            sp.wait_ge(S("y_full"), E * (l + 1))

        def body(r, e, n):
            sp.wait_ge(S("rows_ready"), l + 1)
            sp.wait_ge(extra(l, "turn"), n + 1)
            for i, kind in enumerate(("w1", "w3", "w2")):
                src = expert_src(l, kind, e)
                dst = ring[:, (XPOS[l] + i) % NSLOT, :].rearrange("p (k n) -> p k n", k=src.shape[1])
                sp.dma_start(dst, src).then_inc(extra(l, "w"), 16)
            sp.wait_ge(S("rows_ready"), l + 1)
            sp.wait_ge(extra(l, "y"), n + 1)
        extra_rounds(sp, l, tiles, body, ahead)

    def pool_extra(l, tiles):
        def ahead():
            for b in range(2):
                pool.wait_ge(S(f"ystored{b}"), 2 * 16 * 8 * (l + 1))
                pool.wait_ge(S(f"gathered{b}"), 16 * (9 - b) * (l + 1))
            pool_table(l, tiles)

        def body(r, e, n):
            pool.tensor_copy(idxg[:, 0:1], idx[:, bass.ds(r * E + e, 1)]).then_inc(extra(l, "turn"), 1)
            gather_x(l, 0, idxg[:, 0:1], f"extra_gathered{l}", (extra(l, "turn"), n + 1))
            pool.wait_ge(extra(l, "yout"), n + 1)
            pool.dma_start(ydram[l][bass.ds((r * E + e) * P, P), :], yb[0]).then_inc(extra(l, "stored"), 16)
            pool.wait_ge(extra(l, "stored"), n * 16 + 16)
        extra_rounds(pool, l, tiles, body, ahead)

    def pe_extra(l, tiles):
        def body(r, e, n):
            pe.wait_ge(extra(l, "gathered"), n * 16 + 16)
            for k in range(KD):
                mm = pe.transpose(psum[:, 4 + k // 4, P * (k % 4):P * (k % 4) + P], xg[0][:, P * k:P * k + P], ident)
            mm.then_inc(extra(l, "xt"), 1)
            pe.wait_ge(extra(l, "w"), n * 48 + 48)
            pe.wait_ge(extra(l, "xtout"), n + 1)
            for j in range(2):
                w = slot(XPOS[l] + j, 512)
                for k in range(KD):
                    mm = pe.matmul(bank(j), xT[0][:, k, :], w[:, k, :], start=k == 0, stop=k == KD - 1)
            mm.then_inc(extra(l, "h"), 1)
            pe.wait_ge(extra(l, "a"), n + 1)
            for k in range(KF):
                mm = pe.transpose(psum[:, 6, P * k:P * k + P], ah[0][:, P * k:P * k + P], ident)
            mm.then_inc(extra(l, "at"), 1)
            pe.wait_ge(extra(l, "atout"), n + 1)
            w = slot(XPOS[l] + 2, D, KF)
            for half in range(2):
                for k in range(KF):
                    mm = pe.matmul(bank(2 + half), aT[0][:, k, :], w[:, k, 512 * half:512 * half + 512], start=k == 0, stop=k == KF - 1)
            mm.then_inc(extra(l, "y"), 1)
        extra_rounds(pe, l, tiles, body, lambda: pe_drained(l))

    def pe_drained(l):
        pe.wait_ge(S("y_act"), E * (l + 1))
        pe.wait_ge(S("y_dve"), E * (l + 1))
        pe.wait_ge(S("xt_act"), XT * (l + 1))
        pe.wait_ge(S("xt_dve"), XT * (l + 1))

    def act_extra(l, tiles):
        def body(r, e, n):
            act.wait_ge(extra(l, "xt"), n + 1)
            act.activation(flat(xT[0][:, 0:4, :]), bank(4), ACT.Copy)
            act.activation(flat(xT[0][:, 4:8, :]), bank(5), ACT.Copy).then_inc(extra(l, "xtout"), 1)
            act.wait_ge(extra(l, "h"), n + 1)
            act.activation(sil[0], bank(0), ACT.Silu).then_inc(extra(l, "sil"), 1)
        extra_rounds(act, l, tiles, body)

    def dve_extra(l, tiles):
        def body(r, e, n):
            dve.wait_ge(extra(l, "sil"), n + 1)
            dve.tensor_tensor(ah[0], sil[0], bank(1), ALU.mult).then_inc(extra(l, "a"), 1)
            dve.wait_ge(extra(l, "at"), n + 1)
            dve.tensor_copy(flat(aT[0]), bank(6)).then_inc(extra(l, "atout"), 1)
            dve.wait_ge(extra(l, "y"), n + 1)
            dve.tensor_copy(yb[0][:, 0:512], bank(2))
            dve.tensor_copy(yb[0][:, 512:1024], bank(3)).then_inc(extra(l, "yout"), 1)
        extra_rounds(dve, l, tiles, body)

    def ybuf(j, i):
        return view(9216 + 1024 * (2 * i + j), [D])

    COMB = [0, NT]

    def pool_combine(l, tiles):
        for b in range(2):
            pool.wait_ge(S(f"ystored{b}"), 2 * 16 * 8 * (l + 1))
        longest = pool.value_load(flag[0:1, l:l + 1], min_val=0, max_val=TOK)
        with pool.If(longest > P):
            pool_gather_y(l, tiles, ydram[l])
        with pool.Else():
            pool_gather_y(l, tiles, ydram[l][0:E * P, :])
        pool.end_ifs()

    def pool_gather_y(l, tiles, src):
        for i in range(len(tiles)):
            for j in range(2):
                pool.indirect_dma_start(ybuf(j, i), None, src, bass.IndirectOffsetOnAxis(ap=rowy[:, i, j:j + 1], axis=0)
                                        ).then_inc(S(f"yback{i}"), 16)

    def pool_combine_add(tiles):
        for i, t in enumerate(tiles[:-1]):
            pool.wait_ge(*pool_more("y_gated"))
            pool.tensor_tensor(xres[:, t, :], xres[:, t, :], ybuf(0, i), ALU.add).then_inc(S("comb_done"), 1)

    def act_combine(l, tiles):
        for i in range(len(tiles)):
            act.wait_ge(*act_more(f"yback{i}", 32))
            act.activation(ybuf(0, i), ybuf(0, i), ACT.Copy, scale=gatew[:, i, 0:1]).then_inc(S("y1_scaled"), 1)

    def dve_combine(l, tiles):
        dve.wait_ge(S("grow_done"), GROW_AFTER[l][1])
        for i, t in enumerate(tiles):
            dve.wait_ge(*dve_more(f"yback{i}", 32))
            dve.wait_ge(*dve_more("y1_scaled"))
            y = ybuf(0, i)
            dve_step(dve.scalar_tensor_tensor(y, ybuf(1, i), gatew[:, i, 1:2], y, ALU.mult, ALU.add))
            last = i == len(tiles) - 1
            g = grow[:, 0 if lat(t) else 1, :]
            if last:
                dve_step(dve.tensor_tensor(y, y, g, ALU.mult))
                dve.wait_ge(S("comb_done"), COMB[l] + i)
                dve.tensor_tensor(xres[:, t, :], xres[:, t, :], y, ALU.add).then_inc(S("comb_done"), 1)
                dve.wait_ge(S("comb_done"), COMB[l] + i + 1)
            else:
                dve.tensor_tensor(y, y, g, ALU.mult).then_inc(S("y_gated"), 1)

    GROW_AFTER = [(4, 8), (10, 12)]
    ALL, LAT = list(range(NT)), [2, 3]

    with nc.Block() as block:
        @block.sync
        def _(eng):
            sp_before(0)
            sp_moe(0)
            sp_extra(0, ALL)
            sp_before(1)
            sp_moe(1)
            sp_extra(1, LAT)
            for i, t in enumerate(LAT):
                sp.wait_ge(S("comb_done"), NT + i + 1)
                sp.dma_start(out[0, P * i:P * i + P, :], xres[:, t, :]).then_inc(S("stored"), 16)
            sp.wait_ge(S("stored"), 32)

        @block.gpsimd
        def _(eng):
            pool.wait_ge(S("in_full"), 4)
            pool_zero(0)
            pool_ssd()
            pool_out(ALL)
            pool_dispatch(0, ALL)
            pool_moe(0)
            pool_extra(0, ALL)
            pool_combine(0, ALL)
            pool_combine_add(ALL)
            pool_zero(1)
            pool_out(LAT)
            pool_dispatch(1, LAT)
            pool_moe(1)
            pool_extra(1, LAT)
            pool_combine(1, LAT)
            pool_combine_add(LAT)

        @block.scalar
        def _(eng):
            act_setup()
            act_mod(0)
            act_mod(1)
            act_norm_sums(ALL, "tokens_in", 16 * len(TOKENS))
            act_mod(2)
            act_mod(3)
            act_setup_rest()
            act_norm_rows(0, 0, ALL)
            act.wait_ge(*act_more("raw_cleared"))
            act_in_even("xbc")
            act_conv()
            act_ssd_rows()
            act_in_even("kv", "q")
            act_rstd(10 * NT)
            act_in_even("z")
            act_ssd_prepare()
            act_ssd()
            act_ssd_out()
            act_att_prepare()
            act_att()
            act_grow((0, 1))
            act_norm(0, 1, ALL, "res_added", 8)
            act_router(0, ALL)
            act_moe(0)
            act_extra(0, ALL)
            act.wait_ge(S("out_done"), 8)
            act_grow((0, 1))
            act_combine(0, ALL)
            act_norm(1, 0, ALL, "comb_done", NT)
            act_in_odd()
            act_ml()
            act_ml_out()
            act.wait_ge(S("comb_done"), NT)
            act_grow((0,))
            act_norm(1, 1, LAT, "res_added", 12)
            act_router(1, LAT)
            act_moe(1)
            act_extra(1, LAT)
            act.wait_ge(S("out_done"), 12)
            act_grow((0,))
            act_combine(1, LAT)

        @block.vector
        def _(eng):
            dve_setup()
            dve_mod(0)
            dve_mod(1)
            dve_norm_scale(ALL)
            dve_mod(2)
            dve_mod(3)
            dve_setup_rest()
            dve_mod_bias(0, 0, FIRST)
            dve_acol(0, 0)
            dve_norm_rows(0, 0, ALL)
            dve_router_setup()
            dve_in_even()
            dve_ssd_rows()
            dve_qk_norm()
            dve_ssd_prepare()
            dve_ssd()
            dve_ssd_out()
            dve_att_prepare()
            dve_att()
            dve_mod_bias(0, FIRST, MODC)
            dve_mod_bias(1, 0, MODC)
            for l, which in ((0, 1), (1, 0), (1, 1)):
                dve_acol(l, which)
            dve_out(ALL, 0)
            dve_norm(0, 1, ALL)
            dve_router(0, ALL)
            dve_moe(0)
            dve_extra(0, ALL)
            dve_combine(0, ALL)
            dve_norm(1, 0, ALL)
            dve_in_odd()
            dve_ml_prepare()
            dve_ml()
            dve_ml_out(OUT_ORDER[1])
            dve_out(LAT, 1)
            dve_norm(1, 1, LAT)
            dve_router(1, LAT)
            dve_moe(1)
            dve_extra(1, LAT)
            dve_combine(1, LAT)

        @block.tensor
        def _(eng):
            pe_setup()
            pe.wait_ge(S("spad_ready"), 1)
            for m in range(FIRST):
                pe_mod(m)
            pe_setup_rest()
            pe_norm(ALL)
            pe_in_even()
            pe_ssd_prepare()
            pe_ssd()
            pe_ssd_out()
            pe_att_prepare()
            pe_att()
            pe_grow(0, 0, (0, 1))
            pe_out(ALL, 5 + 2 * MODC)
            pe_norm(ALL)
            pe_router(0, ALL)
            pe_moe(0)
            pe_extra(0, ALL)
            pe_grow(0, 1, (0, 1))
            pe_norm(ALL)
            pe_in_odd()
            pe_ml_prepare()
            pe_ml()
            pe_ml_out()
            pe_grow(1, 0, (0,))
            pe_out(LAT, OD0 + 7)
            pe_norm(LAT)
            pe_router(1, LAT)
            pe_moe(1)
            pe_extra(1, LAT)
            pe_grow(1, 1, (0,))
    return len(sems)


def constants():
    f = np.zeros((P, 548), np.float32)
    f[:, 0:P] = np.eye(P)
    f[:, 128:144] = np.arange(E)
    f[:, 144:160] = E - np.arange(E)
    f[:, 160:164] = np.arange(P)[:, None] + P * np.arange(NT)
    f[:, 164:292] = 1.0
    n = 16
    inv = 10000.0 ** (-np.arange(n, dtype=np.float32) / n)
    pos = np.arange(STREAM)
    ang = np.concatenate([(pos // 64)[:, None] * inv, (pos // 64)[:, None] * inv,
                          (pos % 64)[:, None] * inv, (pos % 64)[:, None] * inv], axis=1).astype(np.float32)
    cos, sin = np.cos(ang), np.sin(ang)
    sin[:, 0:16] *= -1
    sin[:, 32:48] *= -1
    f[:, 292:420] = cos.reshape(2, P, 64).transpose(1, 0, 2).reshape(P, 128)
    f[:, 420:548] = sin.reshape(2, P, 64).transpose(1, 0, 2).reshape(P, 128)
    b = np.zeros((P, 2560 + 2 * NT), np.float32)
    b[:, 2432:2560] = np.arange(P)
    b[:, 2560::2] = P * np.arange(NT)
    b[:, 2561::2] = np.arange(P)[:, None]
    i = np.arange(P)
    b[:, 0:P] = np.eye(P)
    b[:, P:2 * P] = 1.0
    b[:, 2 * P:3 * P] = i[:, None] < i[None, :]
    b[:, 384:896] = np.tile(np.where(i[:, None] > i[None, :], NEG, 0.0), (1, 4))
    b[:, 896:1408] = np.tile(np.where(i[:, None] < i[None, :], NEG, 0.0), (1, 4))
    for t in range(2):
        key = np.arange(STREAM)[None, :]
        far = np.abs(key - (P * t + i[:, None])) > P
        b[:, 1408 + 512 * t + 256:1408 + 512 * (t + 1)] = np.where(far, NEG, 0.0)
    return f, b.astype(mybir.dt.np(BF16))


INPUTS = ["x", "c", "ctx", "c_ctx", "router_w", "router_b", "norm_mix", "norm_ffn", "w_mod", "b_mod",
          "ev_w_in", "ev_conv_w", "ev_conv_b", "ev_dt_bias", "ev_a_log", "ev_d_skip", "ev_ssd_norm",
          "ev_q_norm", "ev_k_norm", "ev_sink", "ev_w_out",
          "od_w_in", "od_conv_w", "od_conv_b", "od_igate_b", "od_fgate_b", "od_head_norm", "od_w_out",
          "moe_w1", "moe_w3", "moe_w2"]


def kernel(**inputs):
    import concourse.bacc as bacc
    from concourse.bass_utils import run_bass_kernel_spmd

    nc = bacc.Bacc("TRN2", target_bir_lowering=False, num_devices=1)
    arrays, args = {}, []
    const_f, const_b = constants()
    for name, a in [(n, inputs[n]) for n in INPUTS] + [("const_f", const_f), ("const_b", const_b)]:
        a = np.ascontiguousarray(a)
        arrays[f"in_{name}"] = a
        args.append(nc.dram_tensor(f"in_{name}", a.shape, mybir.dt.from_np(a.dtype), kind="ExternalInput").ap())
    args.append(nc.dram_tensor("out_x", (1, STREAM, D), F32, kind="ExternalOutput").ap())
    hybrid_program(nc, *args)
    result = run_bass_kernel_spmd(nc, [arrays], core_ids=[0])
    return result.results[0]["out_x"]
```
